# Optimizing a Trainium2 kernel written in Bass

```python
import math
import jax, jax.numpy as jnp
from jax import lax
import numpy as np

D_MODEL = 1024
BATCH = 1
SEQ = 256
DEPTH = 1

PLE_DIM = 256
D_FF = 2816
EPS = 1e-6
ATT_HEADS = 8
ATT_HEAD_DIM = 64
KV_LATENT = 128
IDX_HEADS = 8
IDX_HEAD_DIM = 64
TOPK_MAX = 256
Q_BLOCK = 128
ATT_SCALE = ATT_HEAD_DIM ** -0.5
IDX_W_SCALE = (IDX_HEADS ** -0.5) * (IDX_HEAD_DIM ** -0.5)
REL_BUCKETS = 32
REL_MAX_DIST = 128
HG_HEADS = 4
HG_KEY_DIM = 128
HG_VAL_DIM = 128
CHUNK = 64
ATT_WIDTH = ATT_HEADS * ATT_HEAD_DIM
IDX_Q_WIDTH = IDX_HEADS * IDX_HEAD_DIM
HG_KW = HG_HEADS * HG_KEY_DIM
HG_VW = HG_HEADS * HG_VAL_DIM
IN_SPLITS = (ATT_WIDTH, KV_LATENT, IDX_Q_WIDTH, IDX_HEAD_DIM, IDX_HEADS, HG_KW, HG_KW, HG_VW, HG_VW, D_MODEL, D_MODEL)
N_IN = sum(IN_SPLITS)


def rms_norm(x, g):
    xf = x.astype(jnp.float32)
    y = xf * lax.rsqrt(jnp.mean(xf * xf, axis=-1, keepdims=True) + EPS)
    return (y * g.astype(jnp.float32)).astype(x.dtype)

def swiglu(x, w_gate, w_up, w_down):
    return (jax.nn.silu(x @ w_gate) * (x @ w_up)) @ w_down

def split_cols(a):
    outs = []
    off = 0
    for w in IN_SPLITS:
        outs.append(a[..., off:off + w])
        off += w
    return outs

def rel_bucket(dist):
    max_exact = REL_BUCKETS // 2
    d_f = jnp.maximum(dist, 1).astype(jnp.float32)
    log_b = max_exact + (jnp.log(d_f / max_exact) / math.log(REL_MAX_DIST / max_exact)
                         * (REL_BUCKETS - max_exact)).astype(jnp.int32)
    return jnp.where(dist < max_exact, dist, jnp.minimum(log_b, REL_BUCKETS - 1))

def dsa_branch(q, c_kv, q_idx, k_idx, w_idx, w_uk, w_uv, rel_bias):
    B_, S_ = q.shape[0], q.shape[1]
    topk = min(TOPK_MAX, S_ // 4)
    nblk = S_ // Q_BLOCK
    q_lat = jnp.einsum('bshd,hcd->bshc', q, w_uk)
    key_pos = jnp.arange(S_, dtype=jnp.int32)

    def to_blocks(a):
        return jnp.moveaxis(a.reshape((B_, nblk, Q_BLOCK) + a.shape[2:]), 1, 0)

    def block(args):
        ql, qi, wi, t_pos = args
        dots = jnp.einsum('bqhd,bsd->bqhs', qi, k_idx)
        score = jnp.einsum('bqh,bqhs->bqs', wi, jax.nn.relu(dots)).astype(jnp.float32)
        causal = key_pos[None, :] <= t_pos[:, None]
        score = jnp.where(causal[None], score, -jnp.inf)
        _, idx = lax.top_k(score, topk)
        valid = idx <= t_pos[None, :, None]
        c_sel = jax.vmap(lambda c, i: c[i])(c_kv, idx)
        dist = jnp.maximum(t_pos[None, :, None] - idx, 0)
        bias = jnp.moveaxis(rel_bias[rel_bucket(dist)], -1, 2)
        logits = (jnp.einsum('bqhc,bqkc->bqhk', ql.astype(jnp.float32), c_sel.astype(jnp.float32)) * ATT_SCALE
                  + bias.astype(jnp.float32))
        logits = jnp.where(valid[:, :, None, :], logits, -jnp.inf)
        probs = jax.nn.softmax(logits, axis=-1).astype(c_kv.dtype)
        return jnp.einsum('bqhk,bqkc->bqhc', probs, c_sel)

    t_blocks = jnp.arange(S_, dtype=jnp.int32).reshape(nblk, Q_BLOCK)
    o_lat = lax.map(block, (to_blocks(q_lat), to_blocks(q_idx), to_blocks(w_idx), t_blocks))
    o_lat = jnp.moveaxis(o_lat, 0, 1).reshape(B_, S_, ATT_HEADS, KV_LATENT)
    o = jnp.einsum('bshc,hcd->bshd', o_lat, w_uv)
    return o.reshape(B_, S_, ATT_WIDTH)

def hgrn2_chunkwise(q, k, v, log_f):
    B_, S_, H_, DK_ = q.shape
    DV_ = v.shape[-1]
    n = S_ // CHUNK

    def chunks(a):
        return jnp.moveaxis(a.astype(jnp.float32).reshape(B_, n, CHUNK, H_, a.shape[-1]), 1, 0)

    tri = jnp.tril(jnp.ones((CHUNK, CHUNK), dtype=bool))

    def step(state, inp):
        qc, kc, vc, gc = inp
        G = jnp.cumsum(gc, axis=1)
        o_inter = jnp.einsum('bthk,bhkv->bthv', qc * jnp.exp(G), state)
        diff = G[:, :, None] - G[:, None, :]
        decay = jnp.exp(jnp.where(tri[None, :, :, None, None], diff, -jnp.inf))
        A = jnp.einsum('bthk,bshk,btshk->bhts', qc, kc, decay)
        o_intra = jnp.einsum('bhts,bshv->bthv', A, vc)
        G_last = G[:, -1]
        k_dec = kc * jnp.exp(G_last[:, None] - G)
        new_state = jnp.exp(G_last)[..., None] * state + jnp.einsum('bshk,bshv->bhkv', k_dec, vc)
        return new_state, o_inter + o_intra

    s0 = jnp.zeros((B_, H_, DK_, DV_), jnp.float32)
    _, o = lax.scan(step, s0, (chunks(q), chunks(k), chunks(v), chunks(log_f)))
    return jnp.moveaxis(o, 0, 1).reshape(B_, S_, H_, DV_)

def first_inputs(seed: int = 0) -> dict:
    key = jax.random.key(seed)
    ks = jax.random.split(key, 40)

    def nrm(k, shape, scale):
        return jax.random.normal(k, shape, jnp.float32) * scale

    def gain(k, shape):
        return 1.0 + 0.05 * jax.random.normal(k, shape, jnp.float32)

    L = DEPTH
    D = D_MODEL
    return {
        'x': nrm(ks[0], (BATCH, SEQ, D), 1.0),
        'p': nrm(ks[1], (DEPTH, BATCH, SEQ, PLE_DIM), 1.0),
        'rel_bias': nrm(ks[2], (REL_BUCKETS, ATT_HEADS), 0.1),
        'hgrn_lb': nrm(ks[3], (DEPTH + 1, HG_KW), 1.0),
        'ffn1_pre_g': gain(ks[4], (L, D)),
        'ffn1_post_g': gain(ks[5], (L, D)),
        'ffn1_w_gate': nrm(ks[6], (L, D, D_FF), D ** -0.5),
        'ffn1_w_up': nrm(ks[7], (L, D, D_FF), D ** -0.5),
        'ffn1_w_down': nrm(ks[8], (L, D_FF, D), D_FF ** -0.5),
        'mix_pre_g': gain(ks[9], (L, D)),
        'mix_post_g': gain(ks[10], (L, D)),
        'w_in': nrm(ks[11], (L, D, N_IN), D ** -0.5),
        'kv_norm_g': gain(ks[12], (L, KV_LATENT)),
        'kidx_norm_g': gain(ks[13], (L, IDX_HEAD_DIM)),
        'w_uk': nrm(ks[14], (L, ATT_HEADS, KV_LATENT, ATT_HEAD_DIM), KV_LATENT ** -0.5),
        'w_uv': nrm(ks[15], (L, ATT_HEADS, KV_LATENT, ATT_HEAD_DIM), KV_LATENT ** -0.5),
        'hgrn_norm_g': gain(ks[16], (L, HG_VAL_DIM)),
        'w_br_a': nrm(ks[17], (L, ATT_WIDTH, D), ATT_WIDTH ** -0.5),
        'w_br_b': nrm(ks[18], (L, HG_VW, D), HG_VW ** -0.5),
        'b_gate': nrm(ks[19], (L, 2 * D), 0.02),
        'w_out': nrm(ks[20], (L, D, D), D ** -0.5),
        'ffn2_pre_g': gain(ks[21], (L, D)),
        'ffn2_post_g': gain(ks[22], (L, D)),
        'ffn2_w_gate': nrm(ks[23], (L, D, D_FF), D ** -0.5),
        'ffn2_w_up': nrm(ks[24], (L, D, D_FF), D ** -0.5),
        'ffn2_w_down': nrm(ks[25], (L, D_FF, D), D_FF ** -0.5),
        'ple_pre_g': gain(ks[26], (L, D)),
        'ple_post_g': gain(ks[27], (L, D)),
        'w_ple_gate': nrm(ks[28], (L, D, D), D ** -0.5),
        'w_ple_proj': nrm(ks[29], (L, PLE_DIM, D), PLE_DIM ** -0.5),
    }

def first_block(x, p, rel_bias, hgrn_lb, ffn1_pre_g, ffn1_post_g, ffn1_w_gate, ffn1_w_up, ffn1_w_down,
              mix_pre_g, mix_post_g, w_in, kv_norm_g, kidx_norm_g, w_uk, w_uv, hgrn_norm_g,
              w_br_a, w_br_b, b_gate, w_out, ffn2_pre_g, ffn2_post_g, ffn2_w_gate, ffn2_w_up, ffn2_w_down,
              ple_pre_g, ple_post_g, w_ple_gate, w_ple_proj):
    B_, S_, D = x.shape
    lower_bounds = jnp.cumsum(jax.nn.softmax(hgrn_lb.astype(jnp.float32), axis=0), axis=0)
    h = x
    for i in range(DEPTH):
        h = h + 0.5 * rms_norm(swiglu(rms_norm(h, ffn1_pre_g[i]), ffn1_w_gate[i], ffn1_w_up[i], ffn1_w_down[i]),
                               ffn1_post_g[i])
        u = rms_norm(h, mix_pre_g[i])
        proj = u @ w_in[i]
        (q_a, c_kv, q_idx, k_idx, w_idx, q_h, f_h, i_h, g_h, gate_a, gate_b) = split_cols(proj)
        c_kv = rms_norm(c_kv, kv_norm_g[i])
        k_idx = rms_norm(k_idx, kidx_norm_g[i])
        y_a = dsa_branch(q_a.reshape(B_, S_, ATT_HEADS, ATT_HEAD_DIM), c_kv,
                         q_idx.reshape(B_, S_, IDX_HEADS, IDX_HEAD_DIM), k_idx, w_idx * IDX_W_SCALE,
                         w_uk[i], w_uv[i], rel_bias)
        lb = lower_bounds[i]
        f = (lb + (1.0 - lb) * jax.nn.sigmoid(f_h.astype(jnp.float32))).reshape(B_, S_, HG_HEADS, HG_KEY_DIM)
        o_h = hgrn2_chunkwise(jax.nn.silu(q_h).reshape(B_, S_, HG_HEADS, HG_KEY_DIM), 1.0 - f,
                              i_h.reshape(B_, S_, HG_HEADS, HG_VAL_DIM), jnp.log(f))
        o_h = rms_norm(o_h, hgrn_norm_g[i]) * jax.nn.silu(g_h.astype(jnp.float32).reshape(B_, S_, HG_HEADS, HG_VAL_DIM))
        y_b = o_h.reshape(B_, S_, HG_VW).astype(x.dtype)
        merged = (jax.nn.sigmoid(gate_a + b_gate[i, :D]) * (y_a @ w_br_a[i])
                  + jax.nn.sigmoid(gate_b + b_gate[i, D:]) * (y_b @ w_br_b[i]))
        h = h + rms_norm(merged @ w_out[i], mix_post_g[i])
        h = h + 0.5 * rms_norm(swiglu(rms_norm(h, ffn2_pre_g[i]), ffn2_w_gate[i], ffn2_w_up[i], ffn2_w_down[i]),
                               ffn2_post_g[i])
        ple_gate = jax.nn.sigmoid(rms_norm(h, ple_pre_g[i]) @ w_ple_gate[i])
        h = h + rms_norm(ple_gate * (p[i] @ w_ple_proj[i]), ple_post_g[i])
    return h


SSD_EXPAND = 2
SSD_INNER = SSD_EXPAND * D_MODEL
SSD_HEAD_DIM = 64
SSD_HEADS = SSD_INNER // SSD_HEAD_DIM
SSD_GROUPS = 4
SSD_HPG = SSD_HEADS // SSD_GROUPS
SSD_STATE = 128
SSD_CONV = 4
SSD_XBC = SSD_INNER + 2 * SSD_GROUPS * SSD_STATE
SCONV_DIM = D_MODEL
SCONV_K = 3
FFN_HIDDEN = ((8 * D_MODEL + 767) // 768) * 256
IN_SIZES = (SSD_INNER, SSD_XBC, SSD_HEADS, SCONV_DIM, SCONV_DIM, SCONV_DIM, D_MODEL, D_MODEL)
IN_DIM = sum(IN_SIZES)
IN_SPLITS_2 = tuple(int(v) for v in np.cumsum(IN_SIZES)[:-1])


def rmsnorm(x, w):
    x32 = x.astype(jnp.float32)
    y = x32 * lax.rsqrt(jnp.mean(x32 * x32, axis=-1, keepdims=True) + EPS)
    return (y * w.astype(jnp.float32)).astype(x.dtype)

def causal_depthwise_conv(x, w):
    k = w.shape[0]
    return lax.conv_general_dilated(
        x, w[:, None, :].astype(x.dtype), window_strides=(1,), padding=[(k - 1, 0)],
        dimension_numbers=('NWC', 'WIO', 'NWC'), feature_group_count=x.shape[-1])

def ssd_chunked_scan(x, dt, a, bm, cm):
    bsz, seqlen = x.shape[0], x.shape[1]
    nc = seqlen // CHUNK

    def to_chunks(t):
        return jnp.moveaxis(t.reshape((bsz, nc, CHUNK) + t.shape[2:]), 1, 0)

    causal = jnp.tril(jnp.ones((CHUNK, CHUNK), dtype=bool))[None, :, :, None, None]

    def step(state, inp):
        xc, dtc, bc, cc = inp
        acum = jnp.cumsum(dtc * a, axis=1)
        seg = acum[:, :, None] - acum[:, None, :]
        decay = jnp.exp(jnp.where(causal, seg, -jnp.inf))
        cb = jnp.einsum('blgn,bsgn->blsg', cc, bc)
        xdt = xc * dtc[..., None]
        scores = cb[..., None] * decay
        y_diag = jnp.einsum('blsgr,bsgrp->blgrp', scores, xdt)
        y_off = jnp.einsum('blgn,bgrpn->blgrp', cc, state) * jnp.exp(acum)[..., None]
        to_end = jnp.exp(acum[:, -1:] - acum)
        new_state = (state * jnp.exp(acum[:, -1])[..., None, None]
                     + jnp.einsum('bsgn,bsgr,bsgrp->bgrpn', bc, to_end, xdt))
        return new_state, y_diag + y_off

    state0 = jnp.zeros((bsz, SSD_GROUPS, SSD_HPG, SSD_HEAD_DIM, SSD_STATE), jnp.float32)
    _, ys = lax.scan(step, state0, (to_chunks(x), to_chunks(dt), to_chunks(bm), to_chunks(cm)))
    return jnp.moveaxis(ys, 0, 1).reshape(x.shape)

def hybrid_mixer(h, w_in, ssd_conv_w, ssd_conv_b, dt_bias, a_log, d_skip, ssd_norm_w,
                 w_ssd_proj, sconv_w, w_sconv_proj, w_o):
    bsz, seqlen, _ = h.shape
    u = h @ w_in
    z, xbc, dt_raw, s_b, s_c, s_x, g_a, g_b = jnp.split(u, IN_SPLITS_2, axis=-1)

    xbc = jax.nn.silu(causal_depthwise_conv(xbc, ssd_conv_w) + ssd_conv_b)
    xs, bm, cm = jnp.split(xbc, (SSD_INNER, SSD_INNER + SSD_GROUPS * SSD_STATE), axis=-1)
    xs32 = xs.astype(jnp.float32).reshape(bsz, seqlen, SSD_GROUPS, SSD_HPG, SSD_HEAD_DIM)
    dt = jax.nn.softplus(dt_raw.astype(jnp.float32) + dt_bias.astype(jnp.float32))
    dt = dt.reshape(bsz, seqlen, SSD_GROUPS, SSD_HPG)
    a = -jnp.exp(a_log.astype(jnp.float32)).reshape(SSD_GROUPS, SSD_HPG)
    bm32 = bm.astype(jnp.float32).reshape(bsz, seqlen, SSD_GROUPS, SSD_STATE)
    cm32 = cm.astype(jnp.float32).reshape(bsz, seqlen, SSD_GROUPS, SSD_STATE)
    y = ssd_chunked_scan(xs32, dt, a, bm32, cm32)
    y = y + d_skip.astype(jnp.float32).reshape(SSD_GROUPS, SSD_HPG)[..., None] * xs32
    y = y.reshape(bsz, seqlen, SSD_INNER) * jax.nn.silu(z.astype(jnp.float32))
    yg = y.reshape(bsz, seqlen, SSD_GROUPS, SSD_INNER // SSD_GROUPS)
    yg = yg * lax.rsqrt(jnp.mean(yg * yg, axis=-1, keepdims=True) + EPS)
    y = (yg.reshape(bsz, seqlen, SSD_INNER) * ssd_norm_w.astype(jnp.float32)).astype(h.dtype)
    branch_a = y @ w_ssd_proj

    v = causal_depthwise_conv(s_c * s_x, sconv_w)
    branch_b = (s_b * v) @ w_sconv_proj

    merged = jax.nn.sigmoid(g_a) * branch_a + jax.nn.sigmoid(g_b) * branch_b
    return merged @ w_o

def swiglu_2(h, w_gate, w_up, w_down):
    return (jax.nn.silu(h @ w_gate) * (h @ w_up)) @ w_down

def second_inputs(seed: int = 0) -> dict:
    key = jax.random.key(seed)
    ks = jax.random.split(key, 20)
    f32 = jnp.float32

    def nrm(k, shape, scale):
        return jax.random.normal(k, shape, f32) * scale

    x = jax.random.normal(ks[0], (BATCH, SEQ, D_MODEL), f32)
    dt_init = jnp.exp(jax.random.uniform(ks[5], (DEPTH, SSD_HEADS), f32, np.log(1e-3), np.log(1e-1)))
    dt_bias = dt_init + jnp.log(-jnp.expm1(-dt_init))
    return {
        'x': x,
        'norm_mix_w': 1.0 + nrm(ks[1], (DEPTH, D_MODEL), 0.05),
        'w_in': nrm(ks[2], (DEPTH, D_MODEL, IN_DIM), D_MODEL ** -0.5),
        'ssd_conv_w': nrm(ks[3], (DEPTH, SSD_CONV, SSD_XBC), SSD_CONV ** -0.5),
        'ssd_conv_b': nrm(ks[4], (DEPTH, SSD_XBC), 0.01),
        'dt_bias': dt_bias,
        'a_log': jnp.log(jax.random.uniform(ks[6], (DEPTH, SSD_HEADS), f32, 1.0, 16.0)),
        'd_skip': 1.0 + nrm(ks[7], (DEPTH, SSD_HEADS), 0.1),
        'ssd_norm_w': 1.0 + nrm(ks[8], (DEPTH, SSD_INNER), 0.05),
        'w_ssd_proj': nrm(ks[9], (DEPTH, SSD_INNER, D_MODEL), SSD_INNER ** -0.5),
        'sconv_w': nrm(ks[10], (DEPTH, SCONV_K, SCONV_DIM), SCONV_K ** -0.5),
        'w_sconv_proj': nrm(ks[11], (DEPTH, SCONV_DIM, D_MODEL), SCONV_DIM ** -0.5),
        'w_o': nrm(ks[12], (DEPTH, D_MODEL, D_MODEL), D_MODEL ** -0.5),
        'norm_ffn_w': 1.0 + nrm(ks[13], (DEPTH, D_MODEL), 0.05),
        'w_gate': nrm(ks[14], (DEPTH, D_MODEL, FFN_HIDDEN), D_MODEL ** -0.5),
        'w_up': nrm(ks[15], (DEPTH, D_MODEL, FFN_HIDDEN), D_MODEL ** -0.5),
        'w_down': nrm(ks[16], (DEPTH, FFN_HIDDEN, D_MODEL), FFN_HIDDEN ** -0.5),
        'final_norm_w': 1.0 + nrm(ks[17], (D_MODEL,), 0.05),
    }

def second_block(x, norm_mix_w, w_in, ssd_conv_w, ssd_conv_b, dt_bias, a_log, d_skip, ssd_norm_w,
              w_ssd_proj, sconv_w, w_sconv_proj, w_o, norm_ffn_w, w_gate, w_up, w_down,
              final_norm_w):
    h = x
    for i in range(DEPTH):
        h = h + hybrid_mixer(rmsnorm(h, norm_mix_w[i]), w_in[i], ssd_conv_w[i], ssd_conv_b[i],
                             dt_bias[i], a_log[i], d_skip[i], ssd_norm_w[i], w_ssd_proj[i],
                             sconv_w[i], w_sconv_proj[i], w_o[i])
        h = h + swiglu_2(rmsnorm(h, norm_ffn_w[i]), w_gate[i], w_up[i], w_down[i])
    return rmsnorm(h, final_norm_w)


def setup_inputs(seed=0):
    out = dict(first_inputs(seed))
    for name, value in second_inputs(seed + 1).items():
        if name != "x":
            out[name + "_2"] = value
    return out


def reference(
    x, p, rel_bias, hgrn_lb, ffn1_pre_g, ffn1_post_g, ffn1_w_gate, ffn1_w_up, ffn1_w_down,
    mix_pre_g, mix_post_g, w_in, kv_norm_g, kidx_norm_g, w_uk, w_uv, hgrn_norm_g, w_br_a,
    w_br_b, b_gate, w_out, ffn2_pre_g, ffn2_post_g, ffn2_w_gate, ffn2_w_up, ffn2_w_down,
    ple_pre_g, ple_post_g, w_ple_gate, w_ple_proj, norm_mix_w_2, w_in_2, ssd_conv_w_2,
    ssd_conv_b_2, dt_bias_2, a_log_2, d_skip_2, ssd_norm_w_2, w_ssd_proj_2, sconv_w_2,
    w_sconv_proj_2, w_o_2, norm_ffn_w_2, w_gate_2, w_up_2, w_down_2, final_norm_w_2,
):
    x = first_block(
        x, p, rel_bias, hgrn_lb, ffn1_pre_g, ffn1_post_g, ffn1_w_gate, ffn1_w_up, ffn1_w_down,
        mix_pre_g, mix_post_g, w_in, kv_norm_g, kidx_norm_g, w_uk, w_uv, hgrn_norm_g, w_br_a,
        w_br_b, b_gate, w_out, ffn2_pre_g, ffn2_post_g, ffn2_w_gate, ffn2_w_up, ffn2_w_down,
        ple_pre_g, ple_post_g, w_ple_gate, w_ple_proj,
    )
    return second_block(
        x, norm_mix_w_2, w_in_2, ssd_conv_w_2, ssd_conv_b_2, dt_bias_2, a_log_2, d_skip_2,
        ssd_norm_w_2, w_ssd_proj_2, sconv_w_2, w_sconv_proj_2, w_o_2, norm_ffn_w_2, w_gate_2,
        w_up_2, w_down_2, final_norm_w_2,
    )


_drawn_inputs = setup_inputs


def setup_inputs(seed=0):
    import zlib

    import numpy as np

    out = dict(_drawn_inputs(seed))
    spreads = {}
    factors = {'kv_norm_g': 3.156,
     'b_gate': 8.0,
     'ffn2_post_g': 3.496,
     'ple_pre_g': 4.611,
     'ssd_conv_b_2': 8.0,
     'd_skip_2': 3.402,
     'ssd_norm_w_2': 3.984,
     'norm_ffn_w_2': 2.725}
    for name, (base, spread) in spreads.items():
        noise = np.random.default_rng([zlib.crc32(name.encode()), seed]).standard_normal(out[name].shape)
        drawn = base * np.exp(spread * noise) if base else spread * noise
        out[name] = __import__('jax').numpy.asarray(drawn.astype(out[name].dtype))
    for name, factor in factors.items():
        out[name] = (out[name] * factor).astype(out[name].dtype)
    return out
```

```python
from contextlib import ExitStack
import math

import numpy as np

import concourse.bass as bass
from concourse import mybir

F32 = mybir.dt.float32
F32R = mybir.dt.float32r
U32 = mybir.dt.uint32
ALU = mybir.AluOpType
ACT = mybir.ActivationFunctionType
AX = mybir.AxisListType

P = 128
T = 256
NT = T // P
D = 1024
KD = D // P
D_FF = 2816
EPS = 1e-6
PLE_DIM = 256
HEADS, HEAD_DIM, LATENT = 8, 64, 128
PAIRS = HEADS // 2
TOPK = 64
ATT_SCALE = HEAD_DIM ** -0.5
IDX_W_SCALE = (HEADS ** -0.5) * (HEAD_DIM ** -0.5)
BUCKETS, MAX_DIST = 32, 128
HG = 4
HGD = 128
CHUNK = 64
SSD_HEADS, SSD_HD, GROUPS = 32, 64, 4
HPG = SSD_HEADS // GROUPS
XT = SSD_HEADS * SSD_HD // P
GT = XT // GROUPS
CONV_K, SCONV_K = 4, 3

UNIT = 2048
RING = 3
FCH = 256
NCH = D_FF // FCH
FFN_UNITS = 3 * NCH
KV_COLS = LATENT + HEAD_DIM + HEADS

PARTS = [
    ("ffn1", FFN_UNITS), ("kv", 1), ("q_idx", 2), ("q_a", 2), ("f_h", 2), ("q_h", 2), ("i_h", 2), ("g_h", 2),
    ("gate_b", 4), ("br_b", 2), ("gate_a", 4), ("br_a", 2), ("w_out", 4), ("ffn2", FFN_UNITS),
    ("ple_gate", 4), ("ple_proj", 1), ("s_c", 4), ("s_x", 4), ("s_b", 4), ("sconv_proj", 4), ("g_b", 4),
    ("xbc", 12), ("dt", 1), ("z", 8), ("g_a", 4), ("ssd_proj", 8), ("w_o", 4), ("ffn3", FFN_UNITS),
]
BASE = {}
N_UNITS = 0
for _name, _n in PARTS:
    BASE[_name] = N_UNITS
    N_UNITS += _n

SMALL = [
    ("g_ffn1", 8), ("g_mix", 8), ("g_ffn2", 8), ("g_ple", 8), ("g_mix2", 8), ("g_ffn3", 8),
    ("ssd_norm", XT), ("conv_w", 24 * CONV_K), ("conv_b", 24), ("sconv_w", KD * SCONV_K), ("d_skip", XT),
    ("hg_lb", 2 * HG), ("hg_norm", 1), ("dt_bias", SSD_HEADS), ("a_log", SSD_HEADS),
    ("kv_g", LATENT), ("ki_g", HEAD_DIM), ("w_uk", PAIRS * LATENT), ("w_uv", HEADS * HEAD_DIM),
    ("rel", HEADS),
]
LEVELS = [1, 2, 4, 8, 16, 32, 64]
NREL = 384
CONSTS = [("ident", P), ("tri", P), ("ones", P), ("causal", P), ("reset", T), ("flip", P), ("levels", (len(LEVELS) + 1) * P),
          ("onehot", NREL)]


def columns(table):
    at, out = 0, {}
    for name, n in table:
        out[name] = (at, at + n)
        at += n
    return out, at



def in_series():
    out = {}

    def add(name, n, members):
        for i, m in enumerate(members):
            out[f"{name}{m}"] = (f"{name}s", n * i)

    norms = ["_n0", "_n1", "_n2", "_n3", "_n4", "_n5", "_n6"]
    turned = ["_n0", "_n1", "_m1", "_n2", "_n3", "_n4", "_m2", "_n5"]
    add("nT", 4, turned)
    add("yhi", KD, turned)
    add("ylo", KD, turned)
    add("hn", NT, norms[:6])
    add("h", NT, norms[1:])
    roots = ["_n0", "_p0", "_n1", "_p1", "_n2", "_p2", "_n3", "_p3", "_n4", "_n5", "_n6"]
    add("ss", NT, roots)
    add("rstd", 1, roots)
    for f in (1, 2, 3):
        for name, n in (("tr_done", NCH), ("prod_ready", 2 * NCH), ("hT_ready", NCH), ("sil_ready", 2 * NCH),
                        ("hTh_ready", NCH)):
            out[f"{name}{f}"] = (name, n * (f - 1))
    return out


SERIES = in_series()
SMALL_AT, N_SMALL = columns(SMALL)
CONST_AT, N_CONST = columns(CONSTS)


def build(nc, stream, small, consts, bgate, posts, xin, pin, out):
    ctx = ExitStack()
    with ctx:
        sems = {}
        series = SERIES

        def S(name):
            name = series.get(name, (name, 0))[0]
            if name not in sems:
                sems[name] = ctx.enter_context(nc.semaphore(name))
            return sems[name]

        def W(name, n):
            return S(name), n + series.get(name, (name, 0))[1]

        def sb(name, shape, dt=F32):
            return ctx.enter_context(nc.sbuf_tensor(name, shape, dt))

        raw = [sb(f"raw{i}", [P, UNIT]) for i in range(RING)]
        whi = [sb(f"whi{i}", [P, UNIT], F32R) for i in range(RING)]
        wlo = [sb(f"wlo{i}", [P, UNIT], F32R) for i in range(RING)]
        h = sb("h", [P, NT, D])
        yTh = sb("yTh", [P, KD, T], F32R)
        yTl = sb("yTl", [P, KD, T], F32R)
        post = sb("post", [P, D])
        sm = sb("sm", [P, N_SMALL])
        cn = sb("cn", [P, N_CONST])
        bg = sb("bg", [4, 512])
        st = sb("st", [P, 64])
        half = sb("half", [P, 8])
        ps = ctx.enter_context(nc.psum_tensor("ps", [P, 8, 512], F32))

        def C(name):
            a, b = CONST_AT[name]
            return cn[:, a:b]

        def M(name):
            a, b = SMALL_AT[name]
            return sm[:, a:b]

        ident = C("ident")

        base = (nc.sbuf_base + 63) // 64 * 64
        room = nc.sbuf_usable_end - base - 64 if nc.sbuf_usable_end < nc.sbuf_top else nc.sbuf_top - base - 64
        top = {}

        def at(phase, name, shape, dt=F32, over=None):
            size = 4 * int(np.prod(shape[1:]))
            off = top.get(phase, 0) if over is None else over
            if over is None:
                top[phase] = off + size
                assert off + size <= room, (phase, name, off + size, room)
            t = nc.alloc_sbuf_tensor_at(f"{phase}_{name}", shape, dt, offset=base + off)
            return t

        def here(phase):
            return top.get(phase, 0)

        def scratch(phase):
            return at(phase, "hn", [P, NT, D])

        hn_f = scratch("f")
        sil = at("f", "sil", [P, NT, FCH])
        prod = at("f", "prod", [P, NT, FCH])
        hTh = at("f", "hTh", [P, 2, T], F32R)
        hTl = at("f", "hTl", [P, 2, T], F32R)
        pgate = at("f", "pgate", [P, NT, D])
        praw = at("f", "praw", [P, 2, T])
        pTh = at("f", "pTh", [P, 2, T], F32R)
        pTl = at("f", "pTl", [P, 2, T], F32R)

        hn_m = scratch("m")
        qiT = at("m", "qiT", [P, PAIRS, T])
        olat = nc.alloc_sbuf_tensor_at("m_olat", [P, HEADS, P], F32, offset=base + here("m") - 4096)
        qaT = at("m", "qaT", [P, PAIRS, T])
        kvT = at("m", "kvT", [P, 2, T])
        ckvn = at("m", "ckvn", [P, NT, P])
        kk2 = at("m", "kk2", [P, NT, P])
        wi = at("m", "wi", [P, NT, HEADS])
        vv = at("m", "vv", [P, NT, 512])
        sgh = at("m", "sgh", [P, NT, 512])
        ybh = at("m", "ybh", [P, 4, T], F32R)
        ybl = at("m", "ybl", [P, 4, T], F32R)
        yah = at("m", "yah", [P, 4, T], F32R)
        yal = at("m", "yal", [P, 4, T], F32R)
        gates = at("m", "gates", [P, NT, D])
        score = at("m", "score", [P, 3, P])
        rel8 = at("m", "rel8", [HEADS, NREL])
        top8 = at("m", "top8", [P, 8])
        r_at = here("m")
        at("m", "region", [P, 34 * 256])
        sg = at("m", "sg", [P, HG, T], over=r_at)
        kf = at("m", "kf", [P, HG, T], over=r_at + 4096)
        qh = at("m", "qh", [P, HG, T], over=r_at + 2 * 4096)
        G = at("m", "G", [P, HG, T], over=r_at + 3 * 4096)
        X = at("m", "X", [P, HG, T], over=r_at + 4 * 4096)
        E = [at("m", f"E{i}", [P, HG, T], over=r_at + (5 + i) * 4096) for i in range(2)]
        AT = at("m", "AT", [P, HG, NT, P], over=r_at + 7 * 4096)
        ATx = at("m", "ATx", [P, HG, P], over=r_at + 8 * 4096)
        on = hn_m
        bias = at("m", "bias", [P, HEADS, T], over=r_at)
        qlat = at("m", "qlat", [P, HEADS, T], over=r_at + 8192)
        lg = at("m", "lg", [P, HEADS, T], over=r_at + 2 * 8192)
        pT = at("m", "pT", [P, NT, HEADS, P], over=r_at + 3 * 8192)
        relu = [at("m", f"relu{i}", [P, 3, P], over=r_at + 8 * 4096 + 2048 * 0 + 0) for i in range(1)]
        relu = [hn_m[:, 0, 0:384].rearrange("p (a b) -> p a b", a=3), hn_m[:, 0, 512:896].rearrange("p (a b) -> p a b", a=3)]

        hn_s = scratch("s")
        merged = hn_s
        xs = at("s", "xs", [P, XT, T])
        bc = at("s", "bc", [P, 2 * GROUPS, T])
        sga = at("s", "sga", [P, NT, D])
        cbm = at("s", "cbm", [P, GROUPS, 3, P])
        dts = at("s", "dts", [P, 16, NT, SSD_HEADS])
        v_at = here("s")
        at("s", "region", [P, 36 * 256])
        xdt = at("s", "xdt", [P, NT, SSD_HEADS, SSD_HD], over=v_at)
        xw = at("s", "xw", [P, SSD_HEADS, SSD_HD], over=v_at + 16384)
        seg = at("s", "seg", [P, 4, 3, P], over=v_at + 24576)
        yhi = at("s", "yhi", [P, XT, T], F32R, over=v_at)
        ylo = at("s", "ylo", [P, XT, T], F32R, over=v_at + 16384)
        sq = at("s", "sq", [P, GT, T], over=v_at + 32768)
        cx = at("s", "cx", [P, KD, T], over=v_at)
        cv = at("s", "cv", [P, KD, T], over=v_at + 8192)
        svh = at("s", "svh", [P, KD, T], F32R, over=v_at + 16384)
        svl = at("s", "svl", [P, KD, T], F32R, over=v_at + 24576)
        cvt = at("s", "cvt", [P, 2, 2, T], over=v_at)
        zs = at("s", "zs", [P, 2, T], over=v_at + 32768)

        rscr = nc.dram_tensor("rel_scratch", (HEADS, NREL), F32).ap()

        block = ctx.enter_context(nc.Block())

        def f32(ap):
            return ap.bitcast(F32)

        @block.sync
        def _(sp):
            def unit(u, slot):
                sp.dma_start(raw[slot][:, :], stream[u, :, :]).then_inc(S(f"raw_loaded{slot}"), 16)

            sp.dma_start(h[:, :, :], xin.rearrange("(t p) d -> p t d", p=P)).then_inc(S("x_loaded"), 16)
            sp.dma_start(sm[:, :], small).then_inc(S("sm_loaded"), 16)
            for s in range(RING):
                unit(s, s)
            full = N_UNITS // RING
            with sp.Fori(1, full) as i:
                for s in range(RING):
                    sp.wait_ge(*W("lo_ready", i * RING + (s + 1 - RING)))
                    sp.dma_start(raw[s][:, :], stream[i * RING + s, :, :]).then_inc(S(f"raw_loaded{s}"), 16)
            for u in range(full * RING, N_UNITS):
                sp.wait_ge(*W("lo_ready", u + 1 - RING))
                unit(u, u % RING)
            for t in range(NT):
                sp.wait_ge(*W("final_ready", t + 1))
                sp.dma_start(out[t * P:(t + 1) * P, :], hn_f[:, t, :]).then_inc(S("out_written"), 16)
            sp.wait_ge(*W("out_written", 16 * NT))

        @block.gpsimd
        def _(pool):
            count = [0]

            def link(ins):
                count[0] += 1
                ins.then_inc(S("pool_chain"), 1)
                pool.wait_ge(*W("pool_chain", count[0]))

            pool.dma_start(cn[:, :], consts).then_inc(S("cn_loaded"), 16)
            pool.dma_start(bg[:, :], bgate).then_inc(S("bg_loaded"), 16)
            link(pool.memset(half[:, :], -0.5))

            def load_post(n, free):
                if free is not None:
                    pool.wait_ge(*W(free[0], free[1]))
                pool.dma_start(post[:, :], posts[n:n + 1, :].to_broadcast([P, D])).then_inc(S("post_loaded"), 16)

            def rstd(name, ready, a, b, width, scale=None):
                pool.wait_ge(*W(ready[0], ready[1]))
                link(pool.tensor_scalar(st[:, a:b], st[:, a:b], 1.0 / width, EPS, ALU.mult, ALU.add))
                if scale is None:
                    pool.tensor_tensor(st[:, a:b], st[:, a:b], half[:, 0:b - a], ALU.pow).then_inc(S(name), 1)
                else:
                    link(pool.tensor_tensor(st[:, a:b], st[:, a:b], half[:, 0:b - a], ALU.pow))
                    pool.tensor_scalar(st[:, a:b], st[:, a:b], scale, None, ALU.mult).then_inc(S(name), 1)

            load_post(0, None)
            rstd("rstd_n0", ("ss_n0", 2), 0, 2, D)
            rstd("rstd_p0", ("ss_p0", 2), 2, 4, D, 0.5)
            rstd("rstd_n1", ("ss_n1", 2), 0, 2, D)
            load_post(1, ("h_n1", 2))
            pool.wait_ge(*W("ss_kv", 4))
            link(pool.tensor_scalar(st[:, 8:10], st[:, 8:10], 1.0 / LATENT, EPS, ALU.mult, ALU.add))
            link(pool.tensor_scalar(st[:, 10:12], st[:, 10:12], 1.0 / HEAD_DIM, EPS, ALU.mult, ALU.add))
            pool.tensor_tensor(st[:, 8:12], st[:, 8:12], half[:, 0:4], ALU.pow).then_inc(S("rstd_kv"), 1)
            pool.wait_ge(*W("rel_ready", 1))
            pool.dma_start(rscr, rel8[:, :]).then_inc(S("rel_written"), 16)
            pool.wait_ge(*W("rel_written", 16))
            pool.wait_ge(*W("hg_o", 2))
            src = rscr[:, 0:T]
            src = bass.AP(tensor=src.tensor, offset=src.offset, ap=[[1, P], [NREL, HEADS], [1, T]])
            pool.dma_start(bias[:, :, :], src).then_inc(S("bias_loaded"), 16)
            for t in range(NT):
                rstd("rstd_hg", ("ss_hg", t + 1), 16 + 4 * t, 20 + 4 * t, HGD)
            rstd("rstd_p1", ("ss_p1", 2), 2, 4, D)
            rstd("rstd_n2", ("ss_n2", 2), 0, 2, D)
            load_post(2, ("h_n2", 2))
            pool.dma_start(praw[:, :, :], pin.rearrange("(k p) t -> p k t", p=P)).then_inc(S("p_loaded"), 16)
            rstd("rstd_p2", ("ss_p2", 2), 2, 4, D, 0.5)
            rstd("rstd_n3", ("ss_n3", 2), 0, 2, D)
            load_post(3, ("h_n3", 2))
            rstd("rstd_p3", ("ss_p3", 2), 2, 4, D)
            rstd("rstd_n4", ("ss_n4", 2), 0, 2, D)
            load_post(4, ("h_n4", 2))
            rstd("rstd_ssd", ("ss_ssd", 1), 24, 32, GT * P)
            rstd("rstd_n5", ("ss_n5", 2), 0, 2, D)
            rstd("rstd_n6", ("ss_n6", 2), 0, 2, D)

        @block.tensor
        def _(pe):
            drained = {}

            def take(banks, by):
                for b in banks:
                    for name, n in drained.get(b, []):
                        pe.wait_ge(*W(name, n))
                    drained[b] = by
                return banks

            def begin(u, reg=None):
                pe.wait_ge(*W("lo_ready", u + 1))

            def three(o, a, b, start, stop, swap=False):
                (ah, al), (bh, bl) = a, b
                pe.matmul(o, ah, bh, start=start, stop=False)
                pe.matmul(o, ah, bl, start=False, stop=False)
                return pe.matmul(o, al, bh, start=False, stop=stop)

            def w(slot, a, b):
                return whi[slot][:, a:b], wlo[slot][:, a:b]

            def acts(hl, k, t=None):
                hi, lo = hl
                if t is None:
                    return hi[:, k, :], lo[:, k, :]
                return hi[:, k, t * P:(t + 1) * P], lo[:, k, t * P:(t + 1) * P]

            yT = (yTh, yTl)

            def rows(u0, nk, hl, banks, bias_row=None):
                for n in range(nk):
                    begin(u0 + n)
                    s = (u0 + n) % RING
                    for t in range(NT):
                        o = ps[:, banks[t], :]
                        for k in range(4):
                            last = n == nk - 1 and k == 3
                            ins = three(o, acts(hl, 4 * n + k, t), w(s, k * 512, (k + 1) * 512),
                                        n == 0 and k == 0, last and bias_row is None)
                        if n == nk - 1 and bias_row is not None:
                            ins = pe.matmul(o, ident[0:4, bias_row:bias_row + 1].to_broadcast([4, P]),
                                            bg[:, :], start=False, stop=True)
                    ins.then_inc(S("unit_used"), 1)

            def features(u, bank):
                begin(u)
                s = u % RING
                for j in range(2):
                    for k in range(KD):
                        c = k * 256 + j * P
                        ins = three(ps[:, bank, j * T:(j + 1) * T], w(s, c, c + P), acts(yT, k), k == 0, k == KD - 1)
                ins.then_inc(S("unit_used"), 1)

            def turn(ready, src, done, by):
                for j in range(4):
                    take([j], [(by, 2 * (j + 1))])
                    if j == 0:
                        pe.wait_ge(*W(ready[0], ready[1]))
                    for f in range(2):
                        for t in range(NT):
                            c = (2 * j + f) * P
                            ins = pe.transpose(ps[:, j, (f * NT + t) * P:(f * NT + t + 1) * P],
                                               src[:, t, c:c + P], ident)
                    ins.then_inc(S(done), 1)

            def ffn(f):
                u0 = BASE[f"ffn{f}"]
                acc = take([4, 5, 6, 7], [({1: "h_n1", 2: "h_n3", 3: "h_n6"}[f], 2)])
                gu = take([0, 1], [])
                tr = take([2], [])[0]
                TRN = S(f"tr_done{f}")

                def up(s, half_, c):
                    for t in range(NT):
                        for k in range(4):
                            ins = three(ps[:, gu[t], :], acts(yT, 4 * half_ + k, t), w(s, k * 512, (k + 1) * 512),
                                        half_ == 0 and k == 0, half_ == 1 and k == 3)
                    ins.then_inc(S("unit_used"), 1)
                    return ins

                def turn_hidden():
                    for k in range(2):
                        for t in range(NT):
                            ins = pe.transpose(ps[:, tr, (k * NT + t) * P:(k * NT + t + 1) * P],
                                               prod[:, t, k * P:(k + 1) * P], ident)
                    ins.then_inc(TRN, 1)

                def down(s, first, last=False):
                    for k in range(2):
                        for t in range(NT):
                            for j in range(2):
                                c = k * D + j * 512
                                ins = three(ps[:, acc[2 * t + j], :], acts((hTh, hTl), k, t), w(s, c, c + 512),
                                            first and k == 0, last and k == 1)
                    ins.then_inc(S("unit_used"), 1)

                def step(c, s0, first):
                    u = 3 * c - 1 + u0
                    pe.wait_ge(*W("lo_ready", u + 1))
                    pe.wait_ge(*W(f"prod_ready{f}", 2 * c))
                    up(s0, 0, c)
                    turn_hidden()
                    pe.wait_ge(*W("lo_ready", u + 2))
                    up((s0 + 1) % RING, 1, c)
                    pe.wait_ge(*W("lo_ready", u + 3))
                    pe.wait_ge(*W(f"hT_ready{f}", c))
                    down((s0 + 2) % RING, first)

                begin(u0)
                pe.wait_ge(*W({1: "ylo_n0", 2: "ylo_n2", 3: "ylo_n5"}[f], KD))
                up(u0 % RING, 0, 0)
                begin(u0 + 1)
                up((u0 + 1) % RING, 1, 0)
                s0 = (u0 + 2) % RING
                step(1, s0, True)
                with pe.Fori(2, NCH) as c:
                    step(c, s0, False)
                pe.wait_ge(*W(f"prod_ready{f}", 2 * NCH))
                turn_hidden()
                pe.wait_ge(*W("lo_ready", u0 + FFN_UNITS))
                pe.wait_ge(*W(f"hT_ready{f}", NCH))
                down((u0 + FFN_UNITS - 1) % RING, False, True)
                drained[0] = drained[1] = [(f"prod_ready{f}", 2 * NCH)]
                drained[2] = [(f"hT_ready{f}", NCH)]

            pe.wait_ge(*W("cn_loaded", 16))
            pe.wait_ge(*W("sm_loaded", 16))

            take([3], [("rel_ready", 1)])
            pe.matmul(ps[0:HEADS, 3, 0:NREL], M("rel")[0:BUCKETS, :], C("onehot")[0:BUCKETS, :],
                      start=True, stop=True).then_inc(S("rel_done"), 1)

            turn(("hn_n0", 2), hn_f, "nT_n0", "ylo_n0")
            ffn(1)

            turn(("hn_n1", 2), hn_m, "nT_n1", "ylo_n1")
            pe.wait_ge(*W("ylo_n1", KD))
            u = BASE["kv"]
            begin(u)
            take([0, 1], [("kvn", 8)])
            for t in range(NT):
                for k in range(KD):
                    ins = three(ps[:, t, 0:KV_COLS], acts(yT, k, t), w(u % RING, k * 256, k * 256 + KV_COLS),
                                k == 0, k == KD - 1)
            ins.then_inc(S("unit_used"), 1)
            for part, name in (("q_idx", "qi"), ("q_a", "qa"), ("f_h", "fh"), ("q_h", "qh")):
                for n in range(2):
                    b = take([4 + n], [(f"{name}_out", n + 1)])[0]
                    features(BASE[part] + n, b)
            take([6], [("kvT_out", 1)])
            pe.wait_ge(*W("kvn", 8))
            for m, src in enumerate((ckvn, kk2)):
                for t in range(NT):
                    ins = pe.transpose(ps[:, 6, (m * NT + t) * P:(m * NT + t + 1) * P], src[:, t, :], ident)
            ins.then_inc(S("kvT_done"), 1)
            pe.wait_ge(*W("kvT_out", 1))
            pe.wait_ge(*W("qi_out", 2))
            for hd in range(HEADS):
                b = take([6 + hd % 2], [("relu_out", hd + 1)])[0]
                a = HEAD_DIM * (hd % 2)
                pe.matmul(ps[:, b, 0:P], qiT[a:a + 64, hd // 2, 0:P], kvT[a:a + 64, 1, 0:P], start=True, stop=True)
                pe.matmul(ps[:, b, P:3 * P], qiT[a:a + 64, hd // 2, P:T], kvT[a:a + 64, 1, :],
                          start=True, stop=True).then_inc(S("dots_done"), 1)
            take([0, 1], [("ih_out", 2)])
            rows(BASE["i_h"], 2, yT, [0, 1])
            take([2, 3], [("gh_out", 2)])
            rows(BASE["g_h"], 2, yT, [2, 3])
            pe.wait_ge(*W("qh_out", 2))
            pe.wait_ge(*W("kf_ready", 1))
            for n in range(len(LEVELS) + 1):
                bs = take([4, 5], [("level_out", n + 1)])
                if n:
                    pe.wait_ge(*W("E_ready", 2 * n))
                for hd in range(HG):
                    for t in range(NT):
                        e = E[n % 2]
                        a, q = (e, e) if n else (kf, qh)
                        m = hd * NT + t
                        ins = pe.matmul(ps[:, bs[m // 4], (m % 4) * P:(m % 4 + 1) * P],
                                        a[:, hd, t * P:(t + 1) * P], q[:, hd, t * P:(t + 1) * P],
                                        start=True, stop=True)
                ins.then_inc(S("level_done"), 1)
            b = take([4], [("cross_out", 1)])[0]
            n = len(LEVELS) + 1
            pe.wait_ge(*W("E_ready", 2 * n))
            for hd in range(HG):
                e = E[n % 2]
                ins = pe.matmul(ps[:, b, hd * P:(hd + 1) * P], e[:, hd, 0:P], e[:, hd, P:T], start=True, stop=True)
            ins.then_inc(S("cross_done"), 1)
            for j in range(2):
                bs = take([2 * j, 2 * j + 1], [("gate_out", 2 * (j + 1))])
                rows(BASE["gate_b"] + 2 * j, 2, yT, bs, 2 + j)
            pe.wait_ge(*W("level_out", len(LEVELS) + 1))
            pe.wait_ge(*W("cross_out", 1))
            pe.wait_ge(*W("ih_out", 2))
            for t in range(NT):
                b = take([6 + t], [("on_ready", 2 * (t + 1))])[0]
                for hd in range(HG):
                    c = slice(hd * P, (hd + 1) * P)
                    ins = pe.matmul(ps[:, b, c], AT[:, hd, t, :], vv[:, t, c], start=True, stop=(t == 0))
                    if t:
                        ins = pe.matmul(ps[:, b, c], ATx[:, hd, :], vv[:, 0, c], start=False, stop=True)
                ins.then_inc(S("hg_o"), 1)
            for t in range(NT):
                b = take([4 + t], [("yb_ready", t + 1)])[0]
                pe.wait_ge(*W("on_ready", 2 * (t + 1)))
                for hd in range(HG):
                    ins = pe.transpose(ps[:, b, hd * P:(hd + 1) * P], on[:, t, hd * P:(hd + 1) * P], ident)
                ins.then_inc(S("ybT_done"), 1)
            pe.wait_ge(*W("yb_ready", 2))
            for j in range(2):
                bs = take([2 * j, 2 * j + 1], [("mb_out", 2 * (j + 1))])
                rows(BASE["br_b"] + j, 1, (ybh, ybl), bs)
            pe.wait_ge(*W("qa_out", 2))
            for n in range(2):
                bs = take([4, 5], [("ql_out", 2 * (n + 1))])
                for m in range(2):
                    for r in range(2):
                        a, pair = HEAD_DIM * r, 2 * n + m
                        ins = pe.matmul(ps[:, bs[r], m * T:(m + 1) * T],
                                        M("w_uk")[a:a + 64, pair * LATENT:(pair + 1) * LATENT],
                                        qaT[a:a + 64, pair, :], start=True, stop=True)
                ins.then_inc(S("ql_done"), 1)
            for j in range(2):
                bs = take([2 * j, 2 * j + 1], [("gate_out", 4 + 2 * (j + 1))])
                rows(BASE["gate_a"] + 2 * j, 2, yT, bs, j)
            pe.wait_ge(*W("ql_out", 4))
            for qt in range(NT):
                nk = (qt + 1) * P
                for n in range(4):
                    b = take([4 + n % 2], [("lg_out", 4 * qt + n + 1)])[0]
                    for r in range(2):
                        o, hd = ps[:, b, r * T:r * T + nk], 2 * n + r
                        pe.matmul(o, qlat[:, hd, qt * P:(qt + 1) * P], kvT[:, 0, 0:nk], start=True, stop=False)
                        if hd == 0:
                            pe.wait_ge(*W("bias_loaded", 16))
                        ins = pe.matmul(o, C("flip"), bias[:, hd, T - nk:T], start=False, stop=True)
                    ins.then_inc(S("lg_done"), 1)
                pe.wait_ge(*W("probs_ready", qt + 1))
                for n in range(2 * (qt + 1)):
                    kt, g = n // 2, n % 2
                    m = 2 * qt + n
                    b = take([4 + n % 2], [("pT_out", m + 1)])[0]
                    for r in range(4):
                        ins = pe.transpose(ps[:, b, r * P:(r + 1) * P], lg[:, 4 * g + r, kt * P:(kt + 1) * P], ident)
                    ins.then_inc(S("pT_done"), 1)
                pe.wait_ge(*W("pT_out", 2 + 4 * qt))
                for g in range(2):
                    b = take([6 + g], [("ol_out", 2 * qt + g + 1)])[0]
                    for kt in range(qt + 1):
                        ins = pe.matmul(ps[:, b, :], ckvn[:, kt, :],
                                        pT[:, kt, 4 * g:4 * g + 4, :].rearrange("p a b -> p (a b)"),
                                        start=(kt == 0), stop=(kt == qt))
                    ins.then_inc(S("ol_done"), 1)
                b = take([4], [("ya_ready", qt + 1)])[0]
                pe.wait_ge(*W("ol_out", 2 * (qt + 1)))
                for hd in range(HEADS):
                    a = HEAD_DIM * (hd % 2)
                    ins = pe.matmul(ps[a:a + 64, b, (hd // 2) * P:(hd // 2 + 1) * P],
                                    M("w_uv")[:, hd * 64:(hd + 1) * 64], olat[:, hd, :], start=True, stop=True)
                ins.then_inc(S("oT_done"), 1)
            pe.wait_ge(*W("ya_ready", 2))
            for j in range(2):
                bs = take([2 * j, 2 * j + 1], [("ma_out", 4 * (j + 1))])
                rows(BASE["br_a"] + j, 1, (yah, yal), bs)
            turn(("ma_out", 8), hn_m, "nT_m1", "ylo_m1")
            pe.wait_ge(*W("ylo_m1", KD))

            def out_proj(part, nk, hl, by):
                take([4, 5, 6, 7], by)
                for j in range(2):
                    rows(BASE[part] + nk * j, nk, hl, [4 + j, 6 + j])

            out_proj("w_out", 2, yT, [("h_n2", 2)])

            turn(("hn_n2", 2), hn_f, "nT_n2", "ylo_n2")
            ffn(2)

            turn(("hn_n3", 2), hn_f, "nT_n3", "ylo_n3")
            pe.wait_ge(*W("ylo_n3", KD))
            out_proj("ple_gate", 2, yT, [("pg_out", 2)])
            u = BASE["ple_proj"]
            begin(u)
            take([0, 1, 2, 3], [("pm_out", 2)])
            pe.wait_ge(*W("pT_split", 1))
            for t in range(NT):
                for j in range(2):
                    for k in range(2):
                        c = k * D + j * 512
                        ins = three(ps[:, 2 * t + j, :], acts((pTh, pTl), k, t), w(u % RING, c, c + 512),
                                    k == 0, k == 1)
            ins.then_inc(S("unit_used"), 1)

            turn(("hn_n4", 2), hn_s, "nT_n4", "ylo_n4")
            pe.wait_ge(*W("ylo_n4", KD))
            for part in ("s_c", "s_x", "s_b"):
                for n in range(4):
                    b = take([4 + n], [(f"{part}_out", n + 1)])[0]
                    features(BASE[part] + n, b)
            pe.wait_ge(*W("sv_ready", KD))
            out_proj("sconv_proj", 2, (svh, svl), [("mgb_out", 4)])
            for j in range(2):
                bs = take([2 * j, 2 * j + 1], [("gb_out", 2 * (j + 1))])
                rows(BASE["g_b"] + 2 * j, 2, yT, bs)
            for n in range(12):
                b = take([4 + n % 4], [("conv_out", 2 * (n + 1))])[0]
                features(BASE["xbc"] + n, b)
            u = BASE["dt"]
            begin(u)
            take([0], [("dt_out", 1)])
            for t in range(NT):
                for k in range(KD):
                    ins = three(ps[:, 0, t * SSD_HEADS:(t + 1) * SSD_HEADS], acts(yT, k, t),
                                w(u % RING, k * SSD_HEADS, (k + 1) * SSD_HEADS), k == 0, k == KD - 1)
            ins.then_inc(S("unit_used"), 1)
            pe.wait_ge(*W("xs_ready", 24))
            for g in range(GROUPS):
                b = take([4 + g % 2], [("cb_out", 3 * (g + 1))])[0]
                pe.matmul(ps[:, b, 0:T], bc[:, g, 0:P], bc[:, GROUPS + g, :], start=True, stop=True)
                pe.matmul(ps[:, b, T:T + P], bc[:, g, P:T], bc[:, GROUPS + g, P:T],
                          start=True, stop=True).then_inc(S("cb_done"), 1)
            pe.wait_ge(*W("dtA_ready", 1))
            take([1], [("kd_sub", 1)])
            for t in range(NT):
                pe.matmul(ps[:, 1, t * 32:(t + 1) * 32], C("tri"), dts[:, 1, t, :], start=True, stop=True)
            pe.matmul(ps[:, 1, 64:96], C("ones"), dts[:, 1, 0, :], start=True, stop=True).then_inc(S("ac_done"), 1)
            for n in range(8):
                t, q = n // 4, n % 4
                b = take([2 + n % 2], [("xdt_out", n + 1)])[0]
                for r in range(4):
                    ins = pe.transpose(ps[:, b, r * P:(r + 1) * P], xs[:, 4 * q + r, t * P:(t + 1) * P], ident)
                ins.then_inc(S("xT_done"), 1)
            for q in range(8):
                bs = take([4, 5], [("seg_sub", 8 * (q + 1)), ("cross_exp", 2 * (q + 1))])
                for r in range(4):
                    for t in range(NT):
                        hd = 4 * q + r
                        ins = pe.matmul(ps[:, bs[r // 2], ((r % 2) * NT + t) * P:((r % 2) * NT + t + 1) * P],
                                        dts[:, 1, t, hd:hd + 1].to_broadcast([P, P]), C("tri"),
                                        start=True, stop=True)
                ins.then_inc(S("bc_done"), 1)
                pe.wait_ge(*W("sc_ready", q + 1))
                if q == 0:
                    pe.wait_ge(*W("xw_ready", 1))
                b = take([6 + q % 2], [("y_out", 2 * (q + 1))])[0]
                for r in range(4):
                    hd = 4 * q + r
                    a, c = 64 * (r % 2), (r // 2) * T
                    pe.matmul(ps[a:a + 64, b, c:c + P], xdt[:, 0, hd, :], seg[:, r, 0, :], start=True, stop=True)
                    pe.matmul(ps[a:a + 64, b, c + P:c + T], xw[:, hd, :], seg[:, r, 1, :], start=True, stop=False)
                    ins = pe.matmul(ps[a:a + 64, b, c + P:c + T], xdt[:, 1, hd, :], seg[:, r, 2, :],
                                    start=False, stop=True)
                ins.then_inc(S("y_done"), 1)
            for n in range(8):
                b = take([n % 4], [("z_out", n + 1)])[0]
                features(BASE["z"] + n, b)
            take([4], [("ss_ssd", 1)])
            for g in range(GROUPS):
                pe.wait_ge(*W("sq_ready", g + 1))
                for t in range(NT):
                    c = t * GROUPS + g
                    for k in range(GT):
                        ins = pe.matmul(ps[:, 4, c:c + 1], sq[:, k, t * P:(t + 1) * P], C("ones")[:, 0:1],
                                        start=(k == 0), stop=(k == GT - 1))
                ins.then_inc(S("ssg_done"), 1)
            for j in range(2):
                bs = take([2 * j, 2 * j + 1], [("ga_out", 2 * (j + 1))])
                rows(BASE["g_a"] + 2 * j, 2, yT, bs)
            pe.wait_ge(*W("rstd_ssd", 1))
            take([6, 7], [("yn_out", GROUPS)])
            for g in range(GROUPS):
                for t in range(NT):
                    c = 24 + t * GROUPS + g
                    m = g * NT + t
                    ins = pe.matmul(ps[:, 6 + m // 4, (m % 4) * P:(m % 4 + 1) * P],
                                    st[:, c:c + 1].to_broadcast([P, P]), ident, start=True, stop=True)
            ins.then_inc(S("rb_done"), 1)
            pe.wait_ge(*W("ylo_ssd", XT))
            out_proj("ssd_proj", 4, (yhi, ylo), [("mga_out", 8)])
            turn(("mga_out", 8), merged, "nT_m2", "ylo_m2")
            pe.wait_ge(*W("ylo_m2", KD))
            out_proj("w_o", 2, yT, [("h_n5", 2)])

            turn(("hn_n5", 2), hn_f, "nT_n5", "ylo_n5")
            ffn(3)

        @block.scalar
        def _(act):
            done = [0]
            count = [0]

            def link(ins):
                count[0] += 1
                ins.then_inc(S("act_chain"), 1)
                act.wait_ge(*W("act_chain", count[0]))

            def hi(u, slot):
                act.activation(whi[slot][:, :], raw[slot][:, :], ACT.Copy).then_inc(S("hi_ready"), 1)

            def through(part, n):
                act.wait_ge(*W("unit_used", BASE[part] + n))

            def ahead(n):
                while done[0] < min(n, N_UNITS):
                    u = done[0]
                    act.wait_ge(*W(f"raw_loaded{u % RING}", 16 * (u // RING + 1)))
                    if u >= RING:
                        act.wait_ge(*W("unit_used", u - RING + 1))
                    hi(u, u % RING)
                    done[0] += 1

            def sums(name, ready, src, a):
                for t in range(NT):
                    act.wait_ge(*W(ready[0], ready[1] * (t + 1) if ready[1] else 1))
                    act.activation(junk(t), src(t), ACT.Square, accum_out=st[:, a + t:a + t + 1])\
                       .then_inc(S(name), 1)

            cur = [hn_f]

            def junk(t):
                return cur[0][:, t, :]

            def turned(nT, g, out_name):
                for f in range(KD):
                    if f % 2 == 0:
                        act.wait_ge(*W(nT, f // 2 + 1))
                    src = ps[:, f // 2, (f % 2) * T:(f % 2 + 1) * T]
                    sc = 1.0 if g is None else M(g)[:, f:f + 1]
                    act.activation(yTh[:, f, :], src, ACT.Copy, scale=sc).then_inc(S(out_name), 1)

            def ffn(f):
                u0 = BASE[f"ffn{f}"]
                s0 = (u0 + 2) % RING
                SIL, HHI = S(f"sil_ready{f}"), S(f"hTh_ready{f}")

                def silu(used):
                    act.wait_ge(*W("unit_used", used))
                    for t in range(NT):
                        act.activation(sil[:, t, :], ps[:, t, 0:FCH], ACT.Silu).then_inc(SIL, 1)

                def hidden(c):
                    act.wait_ge(*W(f"tr_done{f}", c))
                    act.activation(hTh[:, :, :].rearrange("p a b -> p (a b)"), ps[:, 2, :], ACT.Copy).then_inc(HHI, 1)

                def split(u, slot, landed):
                    act.wait_ge(*W(f"raw_loaded{slot}", landed))
                    act.wait_ge(*W("unit_used", u - RING + 1))
                    hi(u, slot)

                ahead(u0 + 2)
                ahead(u0 + 3)
                silu(u0 + 2)
                ahead(u0 + 5)

                def step(c, splits):
                    u = 3 * c + (u0 + 2)
                    hidden(c)
                    for n in range(RING):
                        if n == 1:
                            silu(3 * c + (u0 + 1))
                        if n < splits:
                            split(u + n, (s0 + n) % RING, 16 * c + 16 * ((u0 + 2 + n) // RING + 1))

                with act.Fori(1, NCH - 1) as c:
                    step(c, RING)
                step(NCH - 1, min(RING, N_UNITS - (u0 + FFN_UNITS - 1)))
                done[0] = u0 + FFN_UNITS + 2
                hidden(NCH)

            act.wait_ge(*W("sm_loaded", 16))
            act.wait_ge(*W("lb_sub", 2))
            act.activation(st[:, 40:48], st[:, 40:48], ACT.Exp).then_inc(S("lb_exp"), 1)
            act.activation(M("a_log"), M("a_log"), ACT.Exp).then_inc(S("alog_exp"), 1)
            act.wait_ge(*W("rel_done", 1))
            act.activation(rel8[:, :], ps[0:HEADS, 3, 0:NREL], ACT.Copy).then_inc(S("rel_ready"), 1)

            act.wait_ge(*W("x_loaded", 16))
            for t in range(NT):
                act.activation(hn_f[:, t, :], h[:, t, :], ACT.Square, accum_out=st[:, t:t + 1])\
                   .then_inc(S("ss_n0"), 1)
            ahead(2)
            turned("nT_n0", "g_ffn1", "yhi_n0")
            ffn(1)

            def post_sums(part, n, name):
                through(part, n)
                for t in range(NT):
                    act.activation(junk(t), ps[:, 4 + 2 * t:6 + 2 * t, :].rearrange("p a b -> p (a b)"), ACT.Square,
                                   accum_out=st[:, 2 + t:3 + t]).then_inc(S(name), 1)

            def norm_sums(n, a=0):
                for t in range(NT):
                    act.wait_ge(*W(f"h_{n}", t + 1))
                    act.activation(junk(t), h[:, t, :], ACT.Square, accum_out=st[:, a + t:a + t + 1])\
                       .then_inc(S(f"ss_{n}"), 1)

            post_sums("ffn1", FFN_UNITS, "ss_p0")
            ahead(BASE["kv"] + 3)
            cur[0] = hn_m
            norm_sums("n1")
            turned("nT_n1", "g_mix", "yhi_n1")
            for t in range(NT):
                through("kv", 1)
                act.activation(hn_m[:, t, 0:LATENT], ps[:, t, 0:LATENT], ACT.Square,
                               accum_out=st[:, 8 + t:9 + t]).then_inc(S("ss_kv"), 1)
                act.activation(hn_m[:, t, LATENT:LATENT + 64], ps[:, t, LATENT:LATENT + 64], ACT.Square,
                               accum_out=st[:, 10 + t:11 + t]).then_inc(S("ss_kv"), 1)
            ahead(BASE["kv"] + 4)

            def both(t):
                return t.rearrange("p a b -> p (a b)")

            u = BASE["q_idx"]
            for n, (part, name, dst, fn) in enumerate((("q_idx", "qi", qiT, ACT.Copy), ("q_a", "qa", qaT, ACT.Copy),
                                                       ("f_h", "fh", sg, ACT.Sigmoid), ("q_h", "qh", qh, ACT.Silu))):
                for m in range(2):
                    through(part, m + 1)
                    act.activation(both(dst[:, 2 * m:2 * m + 2, :]), ps[:, 4 + m, :], fn).then_inc(S(f"{name}_out"), 1)
                    ahead(u + 2 * n + m + 1 + RING)
            act.wait_ge(*W("kvT_done", 1))
            act.activation(both(kvT[:, :, :]), ps[:, 6, :], ACT.Copy).then_inc(S("kvT_out"), 1)
            act.wait_ge(*W("f_ready", 1))
            act.activation(sg[:, :, :], sg[:, :, :], ACT.Ln).then_inc(S("lnf_ready"), 1)
            for hd in range(HEADS):
                act.wait_ge(*W("dots_done", hd + 1))
                if hd >= 2:
                    act.wait_ge(*W("score_acc", 2 * (hd - 1)))
                act.activation(both(relu[hd % 2]), ps[:, 6 + hd % 2, 0:3 * P], ACT.Relu).then_inc(S("relu_out"), 1)
            ahead(BASE["i_h"] + RING + 1)
            ahead(BASE["i_h"] + RING + 2)
            for t in range(NT):
                through("g_h", 2)
                act.activation(sgh[:, t, :], ps[:, 2 + t, :], ACT.Silu).then_inc(S("gh_out"), 1)
            ahead(BASE["gate_b"] + RING)
            for n in range(1, len(LEVELS) + 2):
                act.wait_ge(*W("X_sub", 2 * n))
                act.activation(X[:, :, :], X[:, :, :], ACT.Exp).then_inc(S("X_exp"), 1)

            def gate(j, part):
                through(part, 2 * (j + 1))
                for t in range(NT):
                    act.activation(gates[:, t, j * 512:(j + 1) * 512], ps[:, 2 * j + t, :], ACT.Sigmoid)\
                       .then_inc(S("gate_out"), 1)

            gate(0, "gate_b")
            ahead(BASE["gate_b"] + 2 + RING)
            gate(1, "gate_b")
            ahead(BASE["gate_b"] + 4 + RING)
            for t in range(NT):
                act.wait_ge(*W("hg_o", t + 1))
                act.activation(on[:, t, 512:1024], ps[:, 6 + t, :], ACT.Square).then_inc(S("osq_ready"), 1)
            for t in range(NT):
                act.wait_ge(*W("ybT_done", t + 1))
                act.activation(ybh[:, :, t * P:(t + 1) * P], ps[:, 4 + t, :].rearrange("p (a b) -> p a b", a=4),
                               ACT.Copy, scale=M("hg_norm")).then_inc(S("ybh_ready"), 1)
            ahead(BASE["br_b"] + 1 + RING)
            ahead(BASE["br_b"] + 2 + RING)
            for n in range(2):
                act.wait_ge(*W("ql_done", n + 1))
                for r in range(2):
                    q = qlat[:, 4 * n:4 * n + 4, :].rearrange("p (m r) t -> p r m t", r=2)
                    act.activation(q[:, r, :, :], ps[:, 4 + r, :].rearrange("p (m t) -> p m t", m=2), ACT.Copy,
                                   scale=ATT_SCALE)\
                       .then_inc(S("ql_out"), 1)
            act.wait_ge(*W("mb_out", 4))
            gate(0, "gate_a")
            ahead(BASE["gate_a"] + 2 + RING)
            gate(1, "gate_a")
            ahead(BASE["gate_a"] + 4 + RING)
            for qt in range(NT):
                nk = (qt + 1) * P
                act.wait_ge(*W("max_ready", qt + 1))
                for hd in range(HEADS):
                    act.activation(lg[:, hd, 0:nk], lg[:, hd, 0:nk], ACT.Exp, bias=st[:, 48 + hd:49 + hd],
                                   accum_out=st[:, 32 + hd:33 + hd]).then_inc(S("exp_ready"), 1)
                for n in range(2 * (qt + 1)):
                    kt, g = n // 2, n % 2
                    act.wait_ge(*W("pT_done", 2 * qt + n + 1))
                    act.activation(both(pT[:, kt, 4 * g:4 * g + 4, :]), ps[:, 4 + n % 2, :], ACT.Copy)\
                       .then_inc(S("pT_out"), 1)
                for g in range(2):
                    act.wait_ge(*W("ol_done", 2 * qt + g + 1))
                    act.activation(both(olat[:, 4 * g:4 * g + 4, :]), ps[:, 6 + g, :], ACT.Copy)\
                       .then_inc(S("ol_out"), 1)
                act.wait_ge(*W("oT_done", qt + 1))
                act.activation(yah[:, :, qt * P:(qt + 1) * P], ps[:, 4, :].rearrange("p (a b) -> p a b", a=4),
                               ACT.Copy).then_inc(S("yah_ready"), 1)
            ahead(BASE["br_a"] + 1 + RING)
            ahead(BASE["br_a"] + 2 + RING)
            turned("nT_m1", None, "yhi_m1")
            ahead(BASE["w_out"] + 1 + RING)
            ahead(BASE["w_out"] + 4 + RING)
            cur[0] = hn_f
            post_sums("w_out", 4, "ss_p1")
            norm_sums("n2")
            turned("nT_n2", "g_ffn2", "yhi_n2")
            ffn(2)
            post_sums("ffn2", FFN_UNITS, "ss_p2")
            norm_sums("n3")
            turned("nT_n3", "g_ple", "yhi_n3")
            act.wait_ge(*W("p_loaded", 16))
            act.activation(pTh[:, :, :], praw[:, :, :], ACT.Copy).then_inc(S("pTh_ready"), 1)
            ahead(BASE["ple_gate"] + 4 + RING)
            for t in range(NT):
                through("ple_gate", 4)
                act.activation(pgate[:, t, :], ps[:, 4 + 2 * t:6 + 2 * t, :].rearrange("p a b -> p (a b)"),
                               ACT.Sigmoid).then_inc(S("pg_out"), 1)
            ahead(BASE["ple_proj"] + 1 + RING)
            for t in range(NT):
                act.wait_ge(*W("pm_out", t + 1))
                act.activation(junk(t), pgate[:, t, :], ACT.Square, accum_out=st[:, 2 + t:3 + t])\
                   .then_inc(S("ss_p3"), 1)

            cur[0] = hn_s
            norm_sums("n4")
            turned("nT_n4", "g_mix2", "yhi_n4")
            w3 = M("sconv_w")
            for n in range(4):
                through("s_c", n + 1)
                act.activation(both(cx[:, 2 * n:2 * n + 2, :]), ps[:, 4 + n, :], ACT.Copy).then_inc(S("s_c_out"), 1)
                ahead(BASE["s_c"] + n + 1 + RING)
            for n in range(4):
                act.wait_ge(*W("s_x_out", n + 1))
                for f in (2 * n, 2 * n + 1):
                    act.activation(cv[:, f, :], cx[:, f, :], ACT.Copy, scale=w3[:, 3 * f + 2:3 * f + 3])\
                       .then_inc(S("cv_first"), 1)
                ahead(BASE["s_x"] + n + 1 + RING)
            for n in range(4):
                act.wait_ge(*W("s_b_out", n + 1))
                act.activation(both(svh[:, 2 * n:2 * n + 2, :]), both(cx[:, 2 * n:2 * n + 2, :]), ACT.Copy)\
                   .then_inc(S("svh_ready"), 1)
                ahead(BASE["s_b"] + n + 1 + RING)
            ahead(BASE["sconv_proj"] + 4 + RING)
            for j in range(2):
                for t in range(NT):
                    through("g_b", 2 * (j + 1))
                    act.activation(sga[:, t, j * 512:(j + 1) * 512], ps[:, 2 * j + t, :], ACT.Sigmoid)\
                       .then_inc(S("gb_out"), 1)
                ahead(BASE["g_b"] + 2 * j + 2 + RING)
            cw, cb = M("conv_w"), M("conv_b")

            def conv_silu(n):
                act.wait_ge(*W("conv_out", 2 * (n + 1)))
                dst = xs[:, 2 * n:2 * n + 2, :] if n < 8 else bc[:, 2 * n - 16:2 * n - 14, :]
                act.activation(both(dst), both(cvt[:, n % 2, :, :]), ACT.Silu).then_inc(S("xs_ready"), 2)

            for n in range(12):
                through("xbc", n + 1)
                if n >= 2:
                    act.wait_ge(*W("xs_ready", 2 * (n - 1)))
                for r in range(2):
                    f = 2 * n + r
                    act.activation(cvt[:, n % 2, r, :], ps[:, 4 + n % 4, r * T:(r + 1) * T], ACT.Identity,
                                   bias=cb[:, f:f + 1], scale=cw[:, 4 * f + 3:4 * f + 4]).then_inc(S("cvt_first"), 1)
                if n:
                    conv_silu(n - 1)
                ahead(BASE["xbc"] + n + 1 + RING)
            conv_silu(11)
            act.wait_ge(*W("sp_abs", 1))
            act.activation(dts[:, 3, :, :], dts[:, 3, :, :], ACT.Exp, scale=-1.0).then_inc(S("sp_exp"), 1)
            act.wait_ge(*W("kd_sub", 1))
            act.activation(dts[:, 8, 0, :], dts[:, 8, 0, :], ACT.Exp).then_inc(S("kd_exp"), 1)
            ahead(BASE["dt"] + 1 + RING)
            for q in range(8):
                act.wait_ge(*W("bc_done", q + 1))
                if q:
                    act.wait_ge(*W("y_done", q))
                for n in range(2):
                    act.activation(seg[:, 2 * n:2 * n + 2, 1, :],
                                   ps[:, 4 + n, :].rearrange("p (r t c) -> p r t c", r=2, t=NT)[:, :, 1, :], ACT.Exp)\
                       .then_inc(S("cross_exp"), 1)
                act.wait_ge(*W("seg_sub", 8 * (q + 1)))
                for n in (0, 2):
                    act.activation(seg[:, :, n, :], seg[:, :, n, :], ACT.Exp).then_inc(S("seg_exp"), 1)
            for n in range(8):
                through("z", n + 1)
                if n:
                    act.wait_ge(*W("z_out", n))
                act.activation(both(zs[:, :, :]), ps[:, n % 4, :], ACT.Silu).then_inc(S("zs_ready"), 1)
                ahead(BASE["z"] + n + 1 + RING)
            for g in range(GROUPS):
                act.wait_ge(*W("z_out", 8))
                if g:
                    act.wait_ge(*W("ssg_done", g))
                act.activation(both(sq[:, :, :]), both(xs[:, GT * g:GT * g + GT, :]), ACT.Square)\
                   .then_inc(S("sq_ready"), 1)
            for j in range(2):
                for t in range(NT):
                    through("g_a", 2 * (j + 1))
                    act.activation(sga[:, t, j * 512:(j + 1) * 512], ps[:, 2 * j + t, :], ACT.Sigmoid)\
                       .then_inc(S("ga_out"), 1)
                ahead(BASE["g_a"] + 2 * j + 2 + RING)
            nw = M("ssd_norm")
            for f in range(XT):
                act.wait_ge(*W("yn_out", f // GT + 1))
                act.activation(yhi[:, f, :], xs[:, f, :], ACT.Copy, scale=nw[:, f:f + 1]).then_inc(S("yhi_ssd"), 1)
            ahead(BASE["ssd_proj"] + 8 + RING)
            turned("nT_m2", None, "yhi_m2")
            ahead(BASE["w_o"] + 4 + RING)
            cur[0] = hn_f
            norm_sums("n5")
            turned("nT_n5", "g_ffn3", "yhi_n5")
            ffn(3)
            norm_sums("n6")

        @block.vector
        def _(dve):
            done = [0]
            count = [0]

            def link(ins):
                count[0] += 1
                ins.then_inc(S("dve_chain"), 1)
                dve.wait_ge(*W("dve_chain", count[0]))

            def lo(u, slot):
                dve.tensor_tensor(wlo[slot][:, :], raw[slot][:, :], f32(whi[slot][:, :]), ALU.subtract)\
                   .then_inc(S("lo_ready"), 1)

            def through(part, n):
                dve.wait_ge(*W("unit_used", BASE[part] + n))

            def ahead(n):
                while done[0] < min(n, N_UNITS):
                    u = done[0]
                    dve.wait_ge(*W("hi_ready", u + 1))
                    lo(u, u % RING)
                    done[0] += 1

            def normed(n, dst):
                dve.wait_ge(*W(f"rstd_{n}", 1))
                for t in range(NT):
                    dve.tensor_scalar(dst[:, t, :], h[:, t, :], st[:, t:t + 1], None, ALU.mult)\
                       .then_inc(S(f"hn_{n}"), 1)

            def turned(n, g):
                for f in range(KD):
                    src = ps[:, f // 2, (f % 2) * T:(f % 2 + 1) * T]
                    if f % 2 == 0:
                        dve.wait_ge(*W(f"yhi_{n}", f + 2))
                    if g is None:
                        ins = dve.tensor_tensor(yTl[:, f, :], src, f32(yTh[:, f, :]), ALU.subtract)
                    else:
                        ins = dve.scalar_tensor_tensor(yTl[:, f, :], src, M(g)[:, f:f + 1], f32(yTh[:, f, :]),
                                                       ALU.mult, ALU.subtract)
                    ins.then_inc(S(f"ylo_{n}"), 1)

            def ffn(f):
                u0 = BASE[f"ffn{f}"]
                s0 = (u0 + 2) % RING
                def gated(c2):
                    for t in range(NT):
                        dve.wait_ge(*W(f"sil_ready{f}", c2 + t + 1))
                        dve.tensor_tensor(prod[:, t, :], sil[:, t, :], ps[:, t, FCH:2 * FCH], ALU.mult)\
                           .then_inc(S(f"prod_ready{f}"), 1)

                def hidden(c):
                    dve.wait_ge(*W(f"hTh_ready{f}", c))
                    dve.tensor_tensor(hTl[:, :, :].rearrange("p a b -> p (a b)"), ps[:, 2, :],
                                      f32(hTh[:, :, :].rearrange("p a b -> p (a b)")), ALU.subtract)\
                       .then_inc(S(f"hT_ready{f}"), 1)

                ahead(u0 + 2)
                ahead(u0 + 3)
                gated(0)
                ahead(u0 + 5)

                def step(c, splits):
                    hidden(c)
                    for n in range(RING):
                        if n == 1:
                            gated(2 * c)
                        if n < splits:
                            dve.wait_ge(*W("hi_ready", 3 * c + (u0 + 2 + n + 1)))
                            lo(None, (s0 + n) % RING)

                with dve.Fori(1, NCH - 1) as c:
                    step(c, RING)
                step(NCH - 1, min(RING, N_UNITS - (u0 + FFN_UNITS - 1)))
                done[0] = u0 + FFN_UNITS + 2
                hidden(NCH)

            def post_norm(n, new, src, gain_loaded):
                dve.wait_ge(*W(f"rstd_{n}", 1))
                dve.wait_ge(*W("post_loaded", gain_loaded))
                for t in range(NT):
                    link(dve.scalar_tensor_tensor(scr[0][:, t, :], src(t), st[:, 2 + t:3 + t], post[:, :],
                                                  ALU.mult, ALU.mult))
                    dve.tensor_tensor(h[:, t, :], h[:, t, :], scr[0][:, t, :], ALU.add).then_inc(S(f"h_{new}"), 1)

            def acc(t):
                return ps[:, 4 + 2 * t:6 + 2 * t, :].rearrange("p a b -> p (a b)")

            scr = [hn_f]
            dve.wait_ge(*W("sm_loaded", 16))
            lbr = M("hg_lb").rearrange("p (a b) -> p a b", a=2)
            link(dve.tensor_tensor(st[:, 36:40], lbr[:, 0, :], lbr[:, 1, :], ALU.max))
            for r in range(2):
                dve.tensor_tensor(st[:, 40 + 4 * r:44 + 4 * r], lbr[:, r, :], st[:, 36:40], ALU.subtract)\
                   .then_inc(S("lb_sub"), 1)
            dve.wait_ge(*W("lb_exp", 1))
            link(dve.tensor_tensor(st[:, 44:48], st[:, 40:44], st[:, 44:48], ALU.add))
            link(dve.reciprocal(st[:, 44:48], st[:, 44:48]))
            link(dve.tensor_tensor(st[:, 40:44], st[:, 40:44], st[:, 44:48], ALU.mult))
            link(dve.tensor_scalar(st[:, 44:48], st[:, 40:44], -1.0, 1.0, ALU.mult, ALU.add))
            dve.wait_ge(*W("x_loaded", 16))
            normed("n0", hn_f)
            ahead(2)
            turned("n0", "g_ffn1")
            ffn(1)
            post_norm("p0", "n1", acc, 16)
            ahead(BASE["kv"] + 3)
            scr[0] = hn_m
            normed("n1", hn_m)
            turned("n1", "g_mix")
            dve.wait_ge(*W("rstd_kv", 1))
            for t in range(NT):
                dve.scalar_tensor_tensor(ckvn[:, t, :], ps[:, t, 0:LATENT], st[:, 8 + t:9 + t], M("kv_g"),
                                         ALU.mult, ALU.mult).then_inc(S("kvn"), 1)
                for r in range(2):
                    dve.scalar_tensor_tensor(kk2[:, t, r * 64:(r + 1) * 64], ps[:, t, LATENT:LATENT + 64],
                                             st[:, 10 + t:11 + t], M("ki_g"), ALU.mult, ALU.mult)\
                       .then_inc(S("kvn"), 1)
                dve.tensor_scalar(wi[:, t, :], ps[:, t, LATENT + 64:KV_COLS], IDX_W_SCALE, None, ALU.mult)\
                   .then_inc(S("kvn"), 1)
            ahead(BASE["kv"] + 4)
            u = BASE["q_idx"]
            for n in range(8):
                ahead(u + n + 1 + RING)
            dve.wait_ge(*W("fh_out", 2))
            for hd in range(HG):
                ins = dve.tensor_scalar(sg[:, hd, :], sg[:, hd, :], st[:, 44 + hd:45 + hd], st[:, 40 + hd:41 + hd],
                                        ALU.mult, ALU.add)
                link(ins)
            dve.tensor_scalar(kf[:, :, :], sg[:, :, :], -1.0, 1.0, ALU.mult, ALU.add).then_inc(S("kf_ready"), 1)
            dve.wait_ge(*W("kf_ready", 1))
            dve.tensor_scalar(sg[:, :, :], sg[:, :, :], 2.0 ** -64, None, ALU.max).then_inc(S("f_ready"), 1)
            dve.memset(AT[:, :, :, :], 0.0).then_inc(S("AT_zero"), 1)
            dve.wait_ge(*W("lnf_ready", 1))
            for hd in range(HG):
                link(dve.tensor_tensor_scan(G[:, hd, :], C("reset"), sg[:, hd, :], 0.0, ALU.mult, ALU.add))
            dve.wait_ge(*W("kvn", 8))
            score_init(dve, S, score, C)
            dve.wait_ge(*W("score_init", 3))
            for hd in range(HEADS):
                dve.wait_ge(*W("relu_out", hd + 1))
                for qt in range(NT):
                    v = score[:, 0:1, :] if qt == 0 else score[:, 1:3, :]
                    r = relu[hd % 2][:, 0:1, :] if qt == 0 else relu[hd % 2][:, 1:3, :]
                    if hd:
                        dve.wait_ge(*W("score_acc", 2 * (hd - 1) + qt + 1))
                    dve.scalar_tensor_tensor(v, r, wi[:, qt, hd:hd + 1], v, ALU.mult, ALU.add)\
                       .then_inc(S("score_acc"), 1)
            dve.wait_ge(*W("score_acc", 2 * HEADS))
            ahead(BASE["i_h"] + RING + 1)
            through("i_h", 2)
            for t in range(NT):
                dve.tensor_copy(vv[:, t, :], ps[:, t, :]).then_inc(S("ih_out"), 1)
            ahead(BASE["i_h"] + RING + 2)
            ahead(BASE["gate_b"] + RING)

            def blocks(x, b):
                return x.rearrange("p h (n r b) -> p (h n) r b", r=2, b=b)

            def exponents(n):
                if n <= len(LEVELS):
                    b = LEVELS[n - 1]
                    g, x = blocks(G[:, :, :], b), blocks(X[:, :, :], b)
                    nb = HG * T // (2 * b)
                    ref = g[:, :, 0, b - 1:b].to_broadcast([P, nb, b])
                    if b < CHUNK:
                        dve.tensor_tensor(x[:, :, 1, :], g[:, :, 1, :], ref, ALU.subtract).then_inc(S("X_sub"), 1)
                    else:
                        dve.tensor_copy(x[:, :, 1, :], g[:, :, 1, :]).then_inc(S("X_sub"), 1)
                    dve.tensor_tensor(x[:, :, 0, :], ref, g[:, :, 0, :], ALU.subtract).then_inc(S("X_sub"), 1)
                else:
                    g = G[:, :, :].rearrange("p h (n c) -> p h n c", c=CHUNK)
                    x = X[:, :, :].rearrange("p h (n c) -> p h n c", c=CHUNK)

                    def last(c):
                        return g[:, :, c, CHUNK - 1:CHUNK].to_broadcast([P, HG, CHUNK])

                    link(dve.tensor_copy(x[:, :, 2, :], g[:, :, 2, :]))
                    link(dve.tensor_tensor(x[:, :, 3, :], g[:, :, 3, :], last(2), ALU.add))
                    link(dve.tensor_tensor(x[:, :, 1, :], last(1), g[:, :, 1, :], ALU.subtract))
                    link(dve.tensor_tensor(x[:, :, 0, :], last(0), g[:, :, 0, :], ALU.subtract))
                    dve.tensor_tensor(x[:, :, 0, :], x[:, :, 0, :], last(1), ALU.add).then_inc(S("X_sub"), 2)

            def level_out(n):
                mask = C("levels")[:, n * P:(n + 1) * P].bitcast(U32)
                dve.wait_ge(*W("level_done", n + 1))
                if n == 0:
                    dve.wait_ge(*W("AT_zero", 1))
                else:
                    dve.wait_ge(*W("level_out", n))
                a = AT[:, :, :, :].rearrange("p h t c -> p (h t) c")
                dve.copy_predicated(a, mask.rearrange("p (a b) -> p a b", a=1).to_broadcast([P, HG * NT, P]),
                                    ps[:, 4:6, :].rearrange("p n (m c) -> p (n m) c", c=P)).then_inc(S("level_out"), 1)

            dve.wait_ge(*W("qh_out", 2))
            for n in range(1, len(LEVELS) + 2):
                if n > 1:
                    dve.wait_ge(*W("E_ready", 2 * (n - 1)))
                exponents(n)
                level_out(n - 1)
                dve.wait_ge(*W("X_exp", n))
                e = E[n % 2]
                b = LEVELS[n - 1] if n <= len(LEVELS) else P
                x, eb = blocks(X[:, :, :], b), blocks(e[:, :, :], b)
                dve.tensor_tensor(eb[:, :, 1, :], x[:, :, 1, :], blocks(qh[:, :, :], b)[:, :, 1, :], ALU.mult)\
                   .then_inc(S("E_ready"), 1)
                dve.tensor_tensor(eb[:, :, 0, :], x[:, :, 0, :], blocks(kf[:, :, :], b)[:, :, 0, :], ALU.mult)\
                   .then_inc(S("E_ready"), 1)
            dve.wait_ge(*W("cross_done", 1))
            dve.tensor_copy(ATx[:, :, :].rearrange("p a b -> p (a b)"), ps[:, 4, :]).then_inc(S("cross_out"), 1)
            ahead(BASE["gate_b"] + 2 + RING)
            ahead(BASE["gate_b"] + 4 + RING)

            def wide(t):
                return on[:, t, 0:512].rearrange("p (a b) -> p a b", a=HG)

            for t in range(NT):
                dve.wait_ge(*W("osq_ready", t + 1))
                dve.tensor_reduce(st[:, 16 + 4 * t:20 + 4 * t], on[:, t, 512:1024].rearrange("p (a b) -> p a b", a=HG),
                                  AX.X, ALU.add).then_inc(S("ss_hg"), 1)
            for t in range(NT):
                dve.wait_ge(*W("rstd_hg", t + 1))
                dve.wait_ge(*W("gh_out", t + 1))
                r = st[:, 16 + 4 * t:20 + 4 * t].rearrange("p (a b) -> p a b", b=1).to_broadcast([P, HG, P])
                dve.tensor_tensor(wide(t), ps[:, 6 + t, :].rearrange("p (a b) -> p a b", a=HG), r, ALU.mult)\
                   .then_inc(S("on_ready"), 1)
                dve.wait_ge(*W("on_ready", 2 * t + 1))
                dve.tensor_tensor(on[:, t, 0:512], on[:, t, 0:512], sgh[:, t, :], ALU.mult)\
                   .then_inc(S("on_ready"), 1)
            for t in range(NT):
                dve.wait_ge(*W("ybh_ready", t + 1))
                v = slice(t * P, (t + 1) * P)
                dve.scalar_tensor_tensor(ybl[:, :, v], ps[:, 4 + t, :].rearrange("p (a b) -> p a b", a=4),
                                         M("hg_norm"), f32(ybh[:, :, v]), ALU.mult, ALU.subtract)\
                   .then_inc(S("yb_ready"), 1)
            ahead(BASE["br_b"] + 1 + RING)
            for j in range(2):
                for t in range(NT):
                    through("br_b", j + 1)
                    c = slice(j * 512, (j + 1) * 512)
                    if j == 0 and t == 0:
                        dve.wait_ge(*W("gate_out", 4))
                        dve.wait_ge(*W("ybT_done", 2))
                    dve.tensor_tensor(hn_m[:, t, c], ps[:, 2 * j + t, :], gates[:, t, c], ALU.mult)\
                       .then_inc(S("mb_out"), 1)
                ahead(BASE["br_b"] + j + 1 + RING)

            def best(qt):
                v = (score[:, 0:1, :] if qt == 0 else score[:, 1:3, :]).rearrange("p a b -> p (a b)")
                for _ in range(TOPK // 8):
                    link(dve.max(top8[:, :], v))
                    link(dve.match_replace(v, top8[:, :], v, -3.0e38))
                link(dve.tensor_scalar(v, v, -2.0e38, -1.0e30, ALU.is_gt, ALU.mult))
                d = score[:, 2 * qt, :]
                link(dve.tensor_tensor(d, d, C("causal"), ALU.add))

            best(0)
            ahead(BASE["gate_a"] + 2 + RING)
            best(1)
            ahead(BASE["gate_a"] + 4 + RING)
            for qt in range(NT):
                nk = (qt + 1) * P
                v = (score[:, 0:1, :] if qt == 0 else score[:, 1:3, :]).rearrange("p a b -> p (a b)")
                if qt:
                    dve.wait_ge(*W("pT_done", 2))
                sel = v.rearrange("p (a b) -> p a b", a=1).to_broadcast([P, 2, nk])
                for n in range(HEADS // 2):
                    dve.wait_ge(*W("lg_done", 4 * qt + n + 1))
                    src = ps[:, 4 + n % 2, :].rearrange("p (a b) -> p a b", a=2)[:, :, 0:nk]
                    dve.tensor_tensor(lg[:, 2 * n:2 * n + 2, 0:nk], src, sel, ALU.add).then_inc(S("lg_out"), 1)
                dve.wait_ge(*W("lg_out", 4 * (qt + 1)))
                if qt:
                    dve.wait_ge(*W("exp_ready", 8))
                dve.tensor_reduce(st[:, 48:56], lg[:, :, 0:nk], AX.X, ALU.max, negate=True).then_inc(S("max_ready"), 1)
                dve.wait_ge(*W("exp_ready", 8 * (qt + 1)))
                link(dve.reciprocal(st[:, 32:40], st[:, 32:40]))
                r = st[:, 32:40].rearrange("p (a b) -> p a b", b=1).to_broadcast([P, HEADS, nk])
                dve.tensor_tensor(lg[:, :, 0:nk], lg[:, :, 0:nk], r, ALU.mult).then_inc(S("probs_ready"), 1)
                dve.wait_ge(*W("yah_ready", qt + 1))
                q = slice(qt * P, (qt + 1) * P)
                dve.tensor_tensor(yal[:, :, q], ps[:, 4, :].rearrange("p (a b) -> p a b", a=4), f32(yah[:, :, q]),
                                  ALU.subtract).then_inc(S("ya_ready"), 1)
            ahead(BASE["br_a"] + 1 + RING)
            for j in range(2):
                for t in range(NT):
                    through("br_a", j + 1)
                    dve.wait_ge(*W("gate_out", 8))
                    c = slice(j * 512, (j + 1) * 512)
                    n = 2 * (2 * j + t)
                    dve.tensor_tensor(gates[:, t, c], ps[:, 2 * j + t, :], gates[:, t, c], ALU.mult)\
                       .then_inc(S("ma_out"), 1)
                    dve.wait_ge(*W("ma_out", n + 1))
                    dve.tensor_tensor(hn_m[:, t, c], hn_m[:, t, c], gates[:, t, c], ALU.add)\
                       .then_inc(S("ma_out"), 1)
                ahead(BASE["br_a"] + j + 1 + RING)
            turned("m1", None)
            ahead(BASE["w_out"] + 1 + RING)
            ahead(BASE["w_out"] + 4 + RING)
            scr[0] = hn_f
            post_norm("p1", "n2", acc, 32)
            normed("n2", hn_f)
            turned("n2", "g_ffn2")
            ffn(2)
            post_norm("p2", "n3", acc, 48)
            normed("n3", hn_f)
            turned("n3", "g_ple")
            dve.wait_ge(*W("pTh_ready", 1))
            dve.tensor_tensor(pTl[:, :, :], praw[:, :, :], f32(pTh[:, :, :]), ALU.subtract).then_inc(S("pT_split"), 1)
            ahead(BASE["ple_gate"] + 4 + RING)
            through("ple_proj", 1)
            dve.wait_ge(*W("pg_out", 2))
            for t in range(NT):
                dve.tensor_tensor(pgate[:, t, :], pgate[:, t, :],
                                  ps[:, 2 * t:2 * t + 2, :].rearrange("p a b -> p (a b)"), ALU.mult)\
                   .then_inc(S("pm_out"), 1)
            ahead(BASE["ple_proj"] + 1 + RING)
            dve.wait_ge(*W("pm_out", 2))
            post_norm("p3", "n4", lambda t: pgate[:, t, :], 64)
            normed("n4", hn_s)
            turned("n4", "g_mix2")

            w3 = M("sconv_w")
            for n in range(4):
                ahead(BASE["s_c"] + n + 1 + RING)
            for n in range(4):
                f = slice(2 * n, 2 * n + 2)
                through("s_x", n + 1)
                dve.wait_ge(*W("s_c_out", n + 1))
                dve.tensor_tensor(cx[:, f, :], cx[:, f, :], ps[:, 4 + n, :].rearrange("p (a b) -> p a b", a=2),
                                  ALU.mult).then_inc(S("s_x_out"), 1)
                ahead(BASE["s_x"] + n + 1 + RING)
            for f in range(KD):
                dve.wait_ge(*W("cv_first", f + 1))
                for s in (1, 2):
                    link(dve.scalar_tensor_tensor(cv[:, f, s:T], cx[:, f, 0:T - s], w3[:, 3 * f + 2 - s:3 * f + 3 - s],
                                                  cv[:, f, s:T], ALU.mult, ALU.add))
            for n in range(4):
                f = slice(2 * n, 2 * n + 2)
                through("s_b", n + 1)
                dve.tensor_tensor(cx[:, f, :], cv[:, f, :], ps[:, 4 + n, :].rearrange("p (a b) -> p a b", a=2),
                                  ALU.mult).then_inc(S("s_b_out"), 1)
                dve.wait_ge(*W("svh_ready", n + 1))
                dve.tensor_tensor(svl[:, f, :], cx[:, f, :], f32(svh[:, f, :]), ALU.subtract)\
                   .then_inc(S("sv_ready"), 2)
                ahead(BASE["s_b"] + n + 1 + RING)
            ahead(BASE["sconv_proj"] + 4 + RING)
            for j in range(2):
                for t in range(NT):
                    c = slice(j * 512, (j + 1) * 512)
                    dve.wait_ge(*W("gb_out", 2 * j + t + 1))
                    through("sconv_proj", 4)
                    if j == 0 and t == 0:
                        dve.wait_ge(*W("nT_n4", 4))
                    dve.tensor_tensor(merged[:, t, c], ps[:, 4 + 2 * t + j, :], sga[:, t, c], ALU.mult)\
                       .then_inc(S("mgb_out"), 1)
                ahead(BASE["g_b"] + 2 * j + 2 + RING)
            cw = M("conv_w")
            for n in range(12):
                for r in range(2):
                    f = 2 * n + r
                    if r == 0:
                        dve.wait_ge(*W("cvt_first", f + 2))
                    v = cvt[:, n % 2, r, :]
                    for s in (1, 2, 3):
                        ins = dve.scalar_tensor_tensor(v[:, s:T], ps[:, 4 + n % 4, r * T:(r + 1) * T - s],
                                                       cw[:, 4 * f + 3 - s:4 * f + 4 - s], v[:, s:T],
                                                       ALU.mult, ALU.add)
                        if s < 3:
                            link(ins)
                        else:
                            ins.then_inc(S("conv_out"), 1)
                ahead(BASE["xbc"] + n + 1 + RING)
            through("dt", 1)
            x, dt_, dtA, e, z, z2, p_ = (dts[:, i, :, :] for i in (2, 0, 1, 3, 4, 5, 6))
            bb = M("dt_bias").rearrange("p (a b) -> p a b", a=1).to_broadcast([P, NT, SSD_HEADS])
            dve.tensor_tensor(x, ps[:, 0, 0:NT * SSD_HEADS].rearrange("p (a b) -> p a b", a=NT), bb, ALU.add)\
               .then_inc(S("dt_out"), 1)
            dve.wait_ge(*W("dt_out", 1))
            dve.scalar_tensor_tensor(e, x, -1.0, x, ALU.mult, ALU.max).then_inc(S("sp_abs"), 1)
            dve.wait_ge(*W("sp_exp", 1))
            link(dve.tensor_scalar(z, e, 2.0, None, ALU.add))
            link(dve.reciprocal(z, z))
            link(dve.tensor_tensor(z, z, e, ALU.mult))
            link(dve.tensor_tensor(z2, z, z, ALU.mult))
            link(dve.tensor_scalar(p_, z2, 1.0 / 15, None, ALU.mult))
            for d in (13, 11, 9, 7, 5, 3):
                link(dve.scalar_tensor_tensor(p_, p_, 1.0 / d, z2, ALU.add, ALU.mult))
            link(dve.scalar_tensor_tensor(p_, p_, 1.0, z, ALU.add, ALU.mult))
            link(dve.tensor_scalar(x, x, 0.0, None, ALU.max))
            link(dve.scalar_tensor_tensor(dt_, p_, 2.0, x, ALU.mult, ALU.add))
            dve.wait_ge(*W("alog_exp", 1))
            al = M("a_log").rearrange("p (a b) -> p a b", a=1).to_broadcast([P, NT, SSD_HEADS])
            dve.scalar_tensor_tensor(dtA, dt_, -1.0, al, ALU.mult, ALU.mult).then_inc(S("dtA_ready"), 1)
            tri = C("tri")
            for g in range(GROUPS):
                dve.wait_ge(*W("cb_done", g + 1))
                b = 4 + g % 2
                dve.tensor_tensor(cbm[:, g, 0, :], ps[:, b, 0:P], tri, ALU.mult).then_inc(S("cb_out"), 1)
                dve.tensor_copy(cbm[:, g, 1, :], ps[:, b, P:2 * P]).then_inc(S("cb_out"), 1)
                dve.tensor_tensor(cbm[:, g, 2, :], ps[:, b, 2 * P:3 * P], tri, ALU.mult).then_inc(S("cb_out"), 1)
            dve.wait_ge(*W("ac_done", 1))
            ac = dts[:, 7, :, :]
            link(dve.tensor_copy(ac, ps[:, 1, 0:64].rearrange("p (a b) -> p a b", a=NT)))
            dve.tensor_tensor(dts[:, 8, 0, :], ps[:, 1, 64:96], ac[:, 0, :], ALU.subtract).then_inc(S("kd_sub"), 1)
            ahead(BASE["dt"] + 1 + RING)
            for n in range(8):
                t, q = n // 4, n % 4
                dve.wait_ge(*W("xT_done", n + 1))
                d = dts[:, 0, t, 8 * q:8 * q + 8].rearrange("p (a b) -> p a b", b=1).to_broadcast([P, 8, SSD_HD])
                dve.tensor_tensor(xdt[:, t, 8 * q:8 * q + 8, :],
                                  ps[:, 2 + n % 2, :].rearrange("p (a b) -> p a b", a=8), d, ALU.mult)\
                   .then_inc(S("xdt_out"), 1)
            dve.wait_ge(*W("xdt_out", 8))
            dve.wait_ge(*W("kd_exp", 1))
            d = dts[:, 8, 0, :].rearrange("p (a b) -> p a b", b=1).to_broadcast([P, SSD_HEADS, SSD_HD])
            dve.tensor_tensor(xw[:, :, :], xdt[:, 0, :, :], d, ALU.mult).then_inc(S("xw_ready"), 1)
            ds = M("d_skip")
            for q in range(8):
                dve.wait_ge(*W("bc_done", q + 1))
                if q:
                    dve.wait_ge(*W("y_done", q))
                dve.wait_ge(*W("cross_exp", 2 * (q + 1)))
                for r in range(4):
                    for t in range(NT):
                        c = ((r % 2) * NT + t) * P
                        hd = 4 * q + r
                        dve.tensor_scalar(seg[:, r, 2 * t, :], ps[:, 4 + r // 2, c:c + P], ac[:, t, hd:hd + 1], 0.0,
                                          ALU.subtract, ALU.min).then_inc(S("seg_sub"), 1)
                if q:
                    y_out(dve, S, xs, ps, ds, q - 1)
                dve.wait_ge(*W("seg_exp", 2 * (q + 1)))
                m = cbm[:, q // 2:q // 2 + 1, :, :].rearrange("p a b c -> p a (b c)").to_broadcast([P, 4, 3 * P])
                sv = seg[:, :, :, :].rearrange("p a b c -> p a (b c)")
                dve.tensor_tensor(sv, sv, m, ALU.mult).then_inc(S("sc_ready"), 1)
            dve.wait_ge(*W("y_done", 8))
            y_out(dve, S, xs, ps, ds, 7)
            for n in range(8):
                dve.wait_ge(*W("zs_ready", n + 1))
                dve.wait_ge(*W("y_out", 16))
                v = xs[:, 2 * n:2 * n + 2, :]
                dve.tensor_tensor(v, v, zs[:, :, :], ALU.mult).then_inc(S("z_out"), 1)
                ahead(BASE["z"] + n + 1 + RING)
            dve.wait_ge(*W("ssg_done", GROUPS))
            dve.tensor_copy(st[:, 24:32], ps[:, 4, 0:8]).then_inc(S("ss_ssd"), 1)
            for j in range(2):
                dve.wait_ge(*W("ga_out", 2 * j + 1))
                ahead(BASE["g_a"] + 2 * j + 2 + RING)
            dve.wait_ge(*W("rb_done", 1))
            for g in range(GROUPS):
                v = xs[:, GT * g:GT * g + GT, :]
                r = ps[:, 6 + g // 2:7 + g // 2, (g % 2) * T:(g % 2 + 1) * T].to_broadcast([P, GT, T])
                dve.tensor_tensor(v, v, r, ALU.mult).then_inc(S("yn_out"), 1)
            nw = M("ssd_norm")
            for f in range(XT):
                dve.wait_ge(*W("yhi_ssd", f + 1))
                dve.scalar_tensor_tensor(ylo[:, f, :], xs[:, f, :], nw[:, f:f + 1], f32(yhi[:, f, :]),
                                         ALU.mult, ALU.subtract).then_inc(S("ylo_ssd"), 1)
            ahead(BASE["ssd_proj"] + 8 + RING)
            for j in range(2):
                for t in range(NT):
                    c = slice(j * 512, (j + 1) * 512)
                    n = 2 * (2 * j + t)
                    dve.wait_ge(*W("ga_out", 4))
                    through("ssd_proj", 4 * (j + 1))
                    dve.tensor_tensor(sga[:, t, c], ps[:, 4 + 2 * t + j, :], sga[:, t, c], ALU.mult)\
                       .then_inc(S("mga_out"), 1)
                    dve.wait_ge(*W("mga_out", n + 1))
                    dve.tensor_tensor(merged[:, t, c], merged[:, t, c], sga[:, t, c], ALU.add)\
                       .then_inc(S("mga_out"), 1)
            turned("m2", None)
            ahead(BASE["w_o"] + 4 + RING)
            through("w_o", 4)
            for t in range(NT):
                dve.tensor_tensor(h[:, t, :], h[:, t, :], acc(t), ALU.add).then_inc(S("h_n5"), 1)
            scr[0] = hn_f
            normed("n5", hn_f)
            turned("n5", "g_ffn3")
            ffn(3)
            through("ffn3", FFN_UNITS)
            for t in range(NT):
                dve.tensor_tensor(h[:, t, :], h[:, t, :], acc(t), ALU.add).then_inc(S("h_n6"), 1)
            dve.wait_ge(*W("rstd_n6", 1))
            dve.wait_ge(*W("post_loaded", 80))
            for t in range(NT):
                dve.scalar_tensor_tensor(hn_f[:, t, :], h[:, t, :], st[:, t:t + 1], post[:, :], ALU.mult, ALU.mult)\
                   .then_inc(S("final_ready"), 1)


def score_init(dve, S, score, C):
    for n in (0, 2):
        dve.tensor_copy(score[:, n, :], C("causal")).then_inc(S("score_init"), 1)
    dve.memset(score[:, 1, :], 0.0).then_inc(S("score_init"), 1)


def y_out(dve, S, xs, ps, ds, q):
    for r in range(2):
        f = 2 * q + r
        dve.scalar_tensor_tensor(xs[:, f, :], xs[:, f, :], ds[:, f:f + 1], ps[:, 6 + q % 2, r * T:(r + 1) * T],
                                 ALU.mult, ALU.add).then_inc(S("y_out"), 1)


def by_rows(w, n):
    k = w.shape[0] // 512
    a = w.reshape(k, 4, P, n, 512).transpose(3, 0, 2, 1, 4)
    return a.reshape(n * k, P, UNIT)


def by_features(w):
    n = w.shape[1] // 256
    return w.reshape(KD, P, n, 256).transpose(2, 1, 0, 3).reshape(n, P, UNIT)


def feed_forward(gate, up, down):
    g = gate.reshape(2, 4, P, NCH, FCH).transpose(3, 0, 2, 1, 4)
    u = up.reshape(2, 4, P, NCH, FCH).transpose(3, 0, 2, 1, 4)
    gu = np.concatenate([g, u], axis=-1).reshape(NCH, 2, P, UNIT)
    dn = down.reshape(NCH, 2, P, D).transpose(0, 2, 1, 3).reshape(NCH, P, UNIT)
    out = [gu[0, 0], gu[0, 1]]
    for c in range(1, NCH):
        out += [gu[c, 0], gu[c, 1], dn[c - 1]]
    return np.stack(out + [dn[NCH - 1]])


def padded(w, cols):
    a = w.reshape(KD, P, w.shape[1]).transpose(1, 0, 2)
    a = np.concatenate([a, np.zeros((P, KD, cols - a.shape[2]), np.float32)], axis=2).reshape(P, KD * cols)
    return np.concatenate([a, np.zeros((P, UNIT - KD * cols), np.float32)], axis=1)[None]


def weight_stream(i):
    w, w2 = i["w_in"][0], i["w_in_2"][0]
    cuts = np.cumsum([0, 512, 128, 512, 64, 8, 512, 512, 512, 512, 1024, 1024])
    c = dict(zip(("q_a", "kv", "q_idx", "ki", "wi", "q_h", "f_h", "i_h", "g_h", "gate_a", "gate_b"),
                 (w[:, a:b] for a, b in zip(cuts[:-1], cuts[1:]))))
    cuts = np.cumsum([0, 2048, 3072, 32, 1024, 1024, 1024, 1024, 1024])
    d = dict(zip(("z", "xbc", "dt", "s_b", "s_c", "s_x", "g_a", "g_b"),
                 (w2[:, a:b] for a, b in zip(cuts[:-1], cuts[1:]))))
    pp = i["w_ple_proj"][0].reshape(2, P, D).transpose(1, 0, 2).reshape(1, P, UNIT)
    parts = {
        "ffn1": feed_forward(i["ffn1_w_gate"][0], i["ffn1_w_up"][0], i["ffn1_w_down"][0]),
        "kv": padded(np.concatenate([c["kv"], c["ki"], c["wi"]], axis=1), 256),
        "q_idx": by_features(c["q_idx"]), "q_a": by_features(c["q_a"]),
        "f_h": by_features(c["f_h"]), "q_h": by_features(c["q_h"]),
        "i_h": by_rows(c["i_h"], 1), "g_h": by_rows(c["g_h"], 1),
        "gate_b": by_rows(c["gate_b"], 2), "br_b": by_rows(i["w_br_b"][0], 2),
        "gate_a": by_rows(c["gate_a"], 2), "br_a": by_rows(i["w_br_a"][0], 2),
        "w_out": by_rows(i["w_out"][0], 2),
        "ffn2": feed_forward(i["ffn2_w_gate"][0], i["ffn2_w_up"][0], i["ffn2_w_down"][0]),
        "ple_gate": by_rows(i["w_ple_gate"][0], 2), "ple_proj": pp,
        "s_c": by_features(d["s_c"]), "s_x": by_features(d["s_x"]), "s_b": by_features(d["s_b"]),
        "sconv_proj": by_rows(i["w_sconv_proj_2"][0], 2), "g_b": by_rows(d["g_b"], 2),
        "xbc": by_features(d["xbc"]), "dt": padded(d["dt"], 32), "z": by_features(d["z"]),
        "g_a": by_rows(d["g_a"], 2), "ssd_proj": by_rows(i["w_ssd_proj_2"][0], 2),
        "w_o": by_rows(i["w_o_2"][0], 2),
        "ffn3": feed_forward(i["w_gate_2"][0], i["w_up_2"][0], i["w_down_2"][0]),
    }
    for name, n in PARTS:
        assert parts[name].shape[0] == n, name
    return np.concatenate([parts[name] for name, _ in PARTS])


def small_parameters(i):
    def tiles(v):
        return v.reshape(-1, P).T

    def all_rows(v):
        return np.broadcast_to(v.reshape(1, -1), (P, v.size))

    conv = i["ssd_conv_w_2"][0].T.reshape(24, P, CONV_K).transpose(1, 0, 2).reshape(P, -1)
    sconv = i["sconv_w_2"][0].T.reshape(KD, P, SCONV_K).transpose(1, 0, 2).reshape(P, -1)
    uk = i["w_uk"][0].transpose(0, 2, 1).reshape(PAIRS, 2 * HEAD_DIM, LATENT).transpose(1, 0, 2).reshape(P, -1)
    uv = i["w_uv"][0].transpose(1, 0, 2).reshape(P, -1)
    rel = np.concatenate([i["rel_bias"], np.zeros((P - BUCKETS, HEADS), np.float32)])
    parts = {
        "g_ffn1": tiles(i["ffn1_pre_g"][0]), "g_mix": tiles(i["mix_pre_g"][0]), "g_ffn2": tiles(i["ffn2_pre_g"][0]),
        "g_ple": tiles(i["ple_pre_g"][0]), "g_mix2": tiles(i["norm_mix_w_2"][0]), "g_ffn3": tiles(i["norm_ffn_w_2"][0]),
        "ssd_norm": tiles(i["ssd_norm_w_2"][0]), "conv_w": conv, "conv_b": tiles(i["ssd_conv_b_2"][0]),
        "sconv_w": sconv, "d_skip": tiles(np.repeat(i["d_skip_2"][0], SSD_HD)),
        "hg_lb": i["hgrn_lb"].reshape(2, HG, P).transpose(2, 0, 1).reshape(P, 2 * HG),
        "hg_norm": i["hgrn_norm_g"][0].reshape(P, 1), "dt_bias": all_rows(i["dt_bias_2"][0]),
        "a_log": all_rows(i["a_log_2"][0]), "kv_g": all_rows(i["kv_norm_g"][0]), "ki_g": all_rows(i["kidx_norm_g"][0]),
        "w_uk": uk, "w_uv": uv, "rel": rel,
    }
    return np.ascontiguousarray(np.concatenate([parts[name] for name, _ in SMALL], axis=1), dtype=np.float32)


def shape_constants():
    s, t = np.arange(P)[:, None], np.arange(P)[None, :]
    levels = [s == t]
    for b in LEVELS:
        levels.append((s // (2 * b) == t // (2 * b)) & ((s // b) % 2 == 0) & ((t // b) % 2 == 1))
    dist = np.maximum(T - 1 - np.arange(NREL), 0)
    exact = BUCKETS // 2
    log_b = exact + (np.log(np.maximum(dist, 1).astype(np.float32) / exact) / math.log(MAX_DIST / exact)
                     * (BUCKETS - exact)).astype(np.int32)
    bucket = np.where(dist < exact, dist, np.minimum(log_b, BUCKETS - 1))
    parts = {
        "ident": s == t, "tri": s <= t, "ones": np.ones((P, P)),
        "causal": np.where(t <= s, 0.0, -1.0e38),
        "reset": np.broadcast_to((np.arange(T) % CHUNK != 0)[None, :], (P, T)),
        "flip": s + t == P - 1,
        "levels": np.concatenate(levels, axis=1),
        "onehot": np.arange(P)[:, None] == bucket[None, :],
    }
    return np.ascontiguousarray(np.concatenate([parts[name] for name, _ in CONSTS], axis=1), dtype=np.float32)


def kernel(**inputs):
    import concourse.bacc as bacc
    from concourse.bass_utils import run_bass_kernel_spmd

    i = {k: np.asarray(v) for k, v in inputs.items()}
    posts = np.stack([i["ffn1_post_g"][0], i["mix_post_g"][0], i["ffn2_post_g"][0], i["ple_post_g"][0],
                      i["final_norm_w_2"]])
    arrays = {
        "stream": weight_stream(i), "small": small_parameters(i), "consts": shape_constants(),
        "bgate": np.ascontiguousarray(i["b_gate"][0].reshape(4, 512)), "posts": posts,
        "x": np.ascontiguousarray(i["x"][0]), "p_turned": np.ascontiguousarray(i["p"][0, 0].T),
    }
    nc = bacc.Bacc("TRN2", target_bir_lowering=False, num_devices=1)
    aps = [nc.dram_tensor(n, a.shape, F32, kind="ExternalInput").ap() for n, a in arrays.items()]
    out = nc.dram_tensor("out", (T, D), F32, kind="ExternalOutput").ap()
    build(nc, *aps, out)
    r = run_bass_kernel_spmd(nc, [arrays], core_ids=[0])
    return r.results[0]["out"].reshape(1, T, D)
```

```python
from contextlib import ExitStack
import math

import numpy as np

import concourse.bass as bass
from concourse import mybir

F32 = mybir.dt.float32
F32R = mybir.dt.float32r
U32 = mybir.dt.uint32
ALU = mybir.AluOpType
ACT = mybir.ActivationFunctionType
AX = mybir.AxisListType

P = 128
T = 256
NT = T // P
D = 1024
KD = D // P
D_FF = 2816
EPS = 1e-6
PLE_DIM = 256
HEADS, HEAD_DIM, LATENT = 8, 64, 128
PAIRS = HEADS // 2
TOPK = 64
ATT_SCALE = HEAD_DIM ** -0.5
IDX_W_SCALE = (HEADS ** -0.5) * (HEAD_DIM ** -0.5)
BUCKETS, MAX_DIST = 32, 128
HG = 4
HGD = 128
CHUNK = 64
SSD_HEADS, SSD_HD, GROUPS = 32, 64, 4
HPG = SSD_HEADS // GROUPS
XT = SSD_HEADS * SSD_HD // P
GT = XT // GROUPS
CONV_K, SCONV_K = 4, 3

UNIT = 2048
RING = 3
FCH = 256
NCH = D_FF // FCH
FFN_UNITS = 3 * NCH
KV_COLS = LATENT + HEAD_DIM + HEADS

PARTS = [
    ("ffn1", FFN_UNITS), ("f_h", 2), ("q_h", 2), ("kv", 1), ("q_idx", 2), ("q_a", 2), ("i_h", 2), ("g_h", 2),
    ("gate_b", 4), ("gate_a", 4), ("br_b", 2), ("br_a", 2), ("w_out", 4), ("ffn2", FFN_UNITS),
    ("ple_gate", 4), ("ple_proj", 1), ("s_c", 4), ("s_x", 4), ("s_b", 4), ("g_b", 4), ("sconv_proj", 4),
    ("dt", 1), ("xbc", 12), ("z", 8), ("g_a", 4), ("ssd_proj", 8), ("w_o", 4), ("ffn3", FFN_UNITS),
]
BASE = {}
N_UNITS = 0
for _name, _n in PARTS:
    BASE[_name] = N_UNITS
    N_UNITS += _n
BETWEEN = [(part, n) for part, count in (("g_h", 2), ("gate_b", 4), ("gate_a", 2)) for n in range(count)]

SMALL = [
    ("g_ffn1", 8), ("g_mix", 8), ("g_ffn2", 8), ("g_ple", 8), ("g_mix2", 8), ("g_ffn3", 8),
    ("ssd_norm", XT), ("conv_w", 24 * CONV_K), ("conv_b", 24), ("sconv_w", KD * SCONV_K), ("d_skip", XT),
    ("hg_lb", 2 * HG), ("hg_norm", 1), ("dt_bias", SSD_HEADS), ("a_log", SSD_HEADS),
    ("kv_g", LATENT), ("ki_g", HEAD_DIM), ("w_uk", PAIRS * LATENT), ("w_uv", HEADS * HEAD_DIM),
    ("rel", HEADS),
]
MAXIMA = [48, 56]
TOTALS = [32, 24]
LEVELS = [1, 2, 4, 8, 16, 32, 64]
NREL = 384
CONSTS = [("ident", P), ("tri", P), ("ones", P), ("causal", P), ("reset", T), ("flip", P), ("levels", (len(LEVELS) + 1) * P),
          ("onehot", NREL)]


def columns(table):
    at, out = 0, {}
    for name, n in table:
        out[name] = (at, at + n)
        at += n
    return out, at



def in_series():
    out = {}

    def add(name, n, members):
        for i, m in enumerate(members):
            out[f"{name}{m}"] = (f"{name}s", n * i)

    norms = ["_n0", "_n1", "_n2", "_n3", "_n4", "_n5", "_n6"]
    turned = ["_n0", "_n1", "_m1", "_n2", "_n3", "_n4", "_m2", "_n5"]
    add("nT", 4, turned)
    add("yhi", KD, turned)
    add("ylo", KD, turned)
    add("hn", NT, norms[:6])
    add("h", NT, norms[1:])
    roots = ["_n0", "_p0", "_n1", "_p1", "_n2", "_p2", "_n3", "_p3", "_n4", "_n5", "_n6"]
    add("ss", NT, roots)
    add("rstd", 1, roots)
    for f in (1, 2, 3):
        for name, n in (("tr_done", NCH), ("prod_ready", 2 * NCH), ("hT_ready", NCH), ("sil_ready", 2 * NCH),
                        ("hTh_ready", NCH)):
            out[f"{name}{f}"] = (name, n * (f - 1))
    return out


SERIES = in_series()
SMALL_AT, N_SMALL = columns(SMALL)
CONST_AT, N_CONST = columns(CONSTS)


def build(nc, stream, small, consts, bgate, posts, xin, pin, out):
    ctx = ExitStack()
    with ctx:
        sems = {}
        series = SERIES

        def S(name):
            name = series.get(name, (name, 0))[0]
            if name not in sems:
                sems[name] = ctx.enter_context(nc.semaphore(name))
            return sems[name]

        def W(name, n):
            return S(name), n + series.get(name, (name, 0))[1]

        def sb(name, shape, dt=F32):
            return ctx.enter_context(nc.sbuf_tensor(name, shape, dt))

        raw = [sb(f"raw{i}", [P, UNIT]) for i in range(RING)]
        whi = [sb(f"whi{i}", [P, UNIT], F32R) for i in range(RING)]
        wlo = [sb(f"wlo{i}", [P, UNIT], F32R) for i in range(RING)]
        h = sb("h", [P, NT, D])
        yTh = sb("yTh", [P, KD, T], F32R)
        yTl = sb("yTl", [P, KD, T], F32R)
        post = sb("post", [P, D])
        sm = sb("sm", [P, N_SMALL])
        cn = sb("cn", [P, N_CONST])
        bg = sb("bg", [4, 512])
        st = sb("st", [P, 64])
        half = sb("half", [P, 8])
        ps = ctx.enter_context(nc.psum_tensor("ps", [P, 8, 512], F32))

        def C(name):
            a, b = CONST_AT[name]
            return cn[:, a:b]

        def M(name):
            a, b = SMALL_AT[name]
            return sm[:, a:b]

        ident = C("ident")

        base = (nc.sbuf_base + 63) // 64 * 64
        room = nc.sbuf_usable_end - base - 64 if nc.sbuf_usable_end < nc.sbuf_top else nc.sbuf_top - base - 64
        top = {}

        def at(phase, name, shape, dt=F32, over=None):
            size = 4 * int(np.prod(shape[1:]))
            off = top.get(phase, 0) if over is None else over
            if over is None:
                top[phase] = off + size
                assert off + size <= room, (phase, name, off + size, room)
            t = nc.alloc_sbuf_tensor_at(f"{phase}_{name}", shape, dt, offset=base + off)
            return t

        def here(phase):
            return top.get(phase, 0)

        def scratch(phase):
            return at(phase, "hn", [P, NT, D])

        hn_f = scratch("f")
        sil = at("f", "sil", [P, NT, FCH])
        prod = at("f", "prod", [P, NT, FCH])
        hTh = at("f", "hTh", [P, 2, T], F32R)
        hTl = at("f", "hTl", [P, 2, T], F32R)
        pgate = at("f", "pgate", [P, NT, D])
        praw = at("f", "praw", [P, 2, T])
        pTh = at("f", "pTh", [P, 2, T], F32R)
        pTl = at("f", "pTl", [P, 2, T], F32R)

        hn_m = scratch("m")
        qiT = at("m", "qiT", [P, PAIRS, T])
        olat = nc.alloc_sbuf_tensor_at("m_olat", [P, HEADS, P], F32, offset=base + here("m") - 4096)
        qa_at = here("m")
        qaT = at("m", "qaT", [P, PAIRS, T])
        kvT = at("m", "kvT", [P, 2, T])
        ckvn = at("m", "ckvn", [P, NT, P])
        kk2 = at("m", "kk2", [P, NT, P])
        wi = at("m", "wi", [P, NT, HEADS])
        vv = at("m", "vv", [P, NT, 512])
        sgh = at("m", "sgh", [P, NT, 512])
        ybh = at("m", "ybh", [P, 4, T], F32R)
        ybl = at("m", "ybl", [P, 4, T], F32R)
        yah = at("m", "yah", [P, 4, T], F32R)
        yal = at("m", "yal", [P, 4, T], F32R)
        gates = at("m", "gates", [P, NT, D])
        gates_a = [vv, sgh]
        score = at("m", "score", [P, 3, P])
        rel8 = at("m", "rel8", [HEADS, NREL])
        top8 = at("m", "top8", [P, 8])
        r_at = here("m")
        at("m", "region", [P, 34 * 256])
        sg = at("m", "sg", [P, HG, T], over=r_at)
        kf = at("m", "kf", [P, HG, T], over=r_at + 4096)
        qh = at("m", "qh", [P, HG, T], over=r_at + 2 * 4096)
        G = at("m", "G", [P, HG, T], over=r_at + 3 * 4096)
        X = at("m", "X", [P, HG, T], over=r_at + 4 * 4096)
        E = [at("m", f"E{i}", [P, HG, T], over=r_at + (5 + i) * 4096) for i in range(2)]
        AT = at("m", "AT", [P, HG, NT, P], over=r_at + 7 * 4096)
        ATx = at("m", "ATx", [P, HG, P], over=r_at + 8 * 4096)
        on = hn_m
        bias = at("m", "bias", [P, HEADS, T], over=r_at)
        qlat = at("m", "qlat", [P, HEADS, T], over=r_at + 8192)
        lg = [nc.alloc_sbuf_tensor_at("m_lg0", [P, HEADS, P], F32, offset=base + qa_at),
              at("m", "lg1", [P, HEADS, T], over=r_at + 2 * 8192)]
        pT = at("m", "pT", [P, NT, HEADS, P], over=r_at + 3 * 8192)
        relu = [hn_m[:, 0, 0:384].rearrange("p (a b) -> p a b", a=3), hn_m[:, 0, 512:896].rearrange("p (a b) -> p a b", a=3)]

        hn_s = scratch("s")
        merged = hn_s
        xs = at("s", "xs", [P, XT, T])
        bc = at("s", "bc", [P, 2 * GROUPS, T])
        sga = at("s", "sga", [P, NT, D])
        cbm = at("s", "cbm", [P, GROUPS, 3, P])
        dts = at("s", "dts", [P, 16, NT, SSD_HEADS])
        v_at = here("s")
        at("s", "region", [P, 36 * 256])
        xdt = at("s", "xdt", [P, NT, SSD_HEADS, SSD_HD], over=v_at)
        xw = at("s", "xw", [P, SSD_HEADS, SSD_HD], over=v_at + 16384)
        seg = at("s", "seg", [P, 4, 3, P], over=v_at + 24576)
        yhi = at("s", "yhi", [P, XT, T], F32R, over=v_at)
        ylo = at("s", "ylo", [P, XT, T], F32R, over=v_at + 16384)
        sq = at("s", "sq", [P, GT, T], over=v_at + 32768)
        cx = at("s", "cx", [P, KD, T], over=v_at)
        cv = at("s", "cv", [P, KD, T], over=v_at + 8192)
        svh = at("s", "svh", [P, KD, T], F32R, over=v_at + 16384)
        svl = at("s", "svl", [P, KD, T], F32R, over=v_at + 24576)
        cvt = at("s", "cvt", [P, 2, 2, T], over=v_at + 32768)
        zs = at("s", "zs", [P, 2, T], over=v_at + 30720)

        rscr = nc.dram_tensor("rel_scratch", (HEADS, NREL), F32).ap()

        block = ctx.enter_context(nc.Block())

        def f32(ap):
            return ap.bitcast(F32)

        @block.sync
        def _(sp):
            def unit(u, slot):
                sp.dma_start(raw[slot][:, :], stream[u, :, :]).then_inc(S(f"raw_loaded{slot}"), 16)

            sp.dma_start(h[:, :, :], xin.rearrange("(t p) d -> p t d", p=P)).then_inc(S("x_loaded"), 16)
            sp.dma_start(sm[:, :], small).then_inc(S("sm_loaded"), 16)
            for s in range(RING):
                unit(s, s)
            full = N_UNITS // RING
            with sp.Fori(1, full) as i:
                for s in range(RING):
                    sp.wait_ge(*W("lo_ready", i * RING + (s + 1 - RING)))
                    sp.dma_start(raw[s][:, :], stream[i * RING + s, :, :]).then_inc(S(f"raw_loaded{s}"), 16)
            for u in range(full * RING, N_UNITS):
                sp.wait_ge(*W("lo_ready", u + 1 - RING))
                unit(u, u % RING)
            for t in range(NT):
                sp.wait_ge(*W("final_ready", t + 1))
                sp.dma_start(out[t * P:(t + 1) * P, :], hn_f[:, t, :]).then_inc(S("out_written"), 16)
            sp.wait_ge(*W("out_written", 16 * NT))

        @block.gpsimd
        def _(pool):
            count = [0]

            def link(ins):
                count[0] += 1
                ins.then_inc(S("pool_chain"), 1)
                pool.wait_ge(*W("pool_chain", count[0]))

            pool.dma_start(cn[:, :], consts).then_inc(S("cn_loaded"), 16)
            pool.dma_start(bg[:, :], bgate).then_inc(S("bg_loaded"), 16)
            link(pool.memset(half[:, :], -0.5))

            def load_post(n, free):
                if free is not None:
                    pool.wait_ge(*W(free[0], free[1]))
                pool.dma_start(post[:, :], posts[n:n + 1, :].to_broadcast([P, D])).then_inc(S("post_loaded"), 16)

            def rstd(name, ready, a, b, width, scale=None):
                pool.wait_ge(*W(ready[0], ready[1]))
                link(pool.tensor_scalar(st[:, a:b], st[:, a:b], 1.0 / width, EPS, ALU.mult, ALU.add))
                if scale is None:
                    pool.tensor_tensor(st[:, a:b], st[:, a:b], half[:, 0:b - a], ALU.pow).then_inc(S(name), 1)
                else:
                    link(pool.tensor_tensor(st[:, a:b], st[:, a:b], half[:, 0:b - a], ALU.pow))
                    pool.tensor_scalar(st[:, a:b], st[:, a:b], scale, None, ALU.mult).then_inc(S(name), 1)

            load_post(0, None)
            rstd("rstd_n0", ("ss_n0", 2), 0, 2, D)
            rstd("rstd_p0", ("ss_p0", 2), 2, 4, D, 0.5)
            rstd("rstd_n1", ("ss_n1", 2), 0, 2, D)
            load_post(1, ("h_n1", 2))
            pool.wait_ge(*W("ss_kv", 4))
            link(pool.tensor_scalar(st[:, 8:10], st[:, 8:10], 1.0 / LATENT, EPS, ALU.mult, ALU.add))
            link(pool.tensor_scalar(st[:, 10:12], st[:, 10:12], 1.0 / HEAD_DIM, EPS, ALU.mult, ALU.add))
            pool.tensor_tensor(st[:, 8:12], st[:, 8:12], half[:, 0:4], ALU.pow).then_inc(S("rstd_kv"), 1)
            pool.wait_ge(*W("rel_ready", 1))
            pool.dma_start(rscr, rel8[:, :]).then_inc(S("rel_written"), 16)
            pool.wait_ge(*W("rel_written", 16))
            pool.wait_ge(*W("hg_o", 2))
            src = rscr[:, 0:T]
            src = bass.AP(tensor=src.tensor, offset=src.offset, ap=[[1, P], [NREL, HEADS], [1, T]])
            pool.dma_start(bias[:, :, :], src).then_inc(S("bias_loaded"), 16)
            for t in range(NT):
                rstd("rstd_hg", ("ss_hg", t + 1), 16 + 4 * t, 20 + 4 * t, HGD)
            rstd("rstd_p1", ("ss_p1", 2), 2, 4, D)
            rstd("rstd_n2", ("ss_n2", 2), 0, 2, D)
            load_post(2, ("h_n2", 2))
            pool.dma_start(praw[:, :, :], pin.rearrange("(k p) t -> p k t", p=P)).then_inc(S("p_loaded"), 16)
            rstd("rstd_p2", ("ss_p2", 2), 2, 4, D, 0.5)
            rstd("rstd_n3", ("ss_n3", 2), 0, 2, D)
            load_post(3, ("h_n3", 2))
            rstd("rstd_p3", ("ss_p3", 2), 2, 4, D)
            rstd("rstd_n4", ("ss_n4", 2), 0, 2, D)
            load_post(4, ("h_n4", 2))
            rstd("rstd_ssd", ("ss_ssd", 1), 24, 32, GT * P)
            rstd("rstd_n5", ("ss_n5", 2), 0, 2, D)
            rstd("rstd_n6", ("ss_n6", 2), 0, 2, D)

        @block.tensor
        def _(pe):
            drained = {}

            def take(banks, by):
                for b in banks:
                    for name, n in drained.get(b, []):
                        pe.wait_ge(*W(name, n))
                    drained[b] = by
                return banks

            def begin(u, reg=None):
                pe.wait_ge(*W("lo_ready", u + 1))

            def three(o, a, b, start, stop, swap=False):
                (ah, al), (bh, bl) = a, b
                pe.matmul(o, ah, bh, start=start, stop=False)
                pe.matmul(o, ah, bl, start=False, stop=False)
                return pe.matmul(o, al, bh, start=False, stop=stop)

            def w(slot, a, b):
                return whi[slot][:, a:b], wlo[slot][:, a:b]

            def acts(hl, k, t=None):
                hi, lo = hl
                if t is None:
                    return hi[:, k, :], lo[:, k, :]
                return hi[:, k, t * P:(t + 1) * P], lo[:, k, t * P:(t + 1) * P]

            yT = (yTh, yTl)

            def row_unit(u0, n, nk, hl, banks, bias_row=None):
                begin(u0 + n)
                s = (u0 + n) % RING
                for t in range(NT):
                    o = ps[:, banks[t], :]
                    for k in range(4):
                        last = n == nk - 1 and k == 3
                        ins = three(o, acts(hl, 4 * n + k, t), w(s, k * 512, (k + 1) * 512),
                                    n == 0 and k == 0, last and bias_row is None)
                    if n == nk - 1 and bias_row is not None:
                        ins = pe.matmul(o, ident[0:4, bias_row:bias_row + 1].to_broadcast([4, P]),
                                        bg[:, :], start=False, stop=True)
                ins.then_inc(S("unit_used"), 1)

            def rows(u0, nk, hl, banks, ready=None):
                for n in range(nk):
                    if ready:
                        pe.wait_ge(*W(ready, 4 * n + 4))
                    row_unit(u0, n, nk, hl, banks)

            def features(u, bank):
                begin(u)
                s = u % RING
                for j in range(2):
                    for k in range(KD):
                        c = k * 256 + j * P
                        ins = three(ps[:, bank, j * T:(j + 1) * T], w(s, c, c + P), acts(yT, k), k == 0, k == KD - 1)
                ins.then_inc(S("unit_used"), 1)

            def turn(ready, src, done, by):
                for j in range(4):
                    take([j], [(by, 2 * (j + 1))])
                    if j == 0:
                        pe.wait_ge(*W(ready[0], ready[1]))
                    for f in range(2):
                        for t in range(NT):
                            c = (2 * j + f) * P
                            ins = pe.transpose(ps[:, j, (f * NT + t) * P:(f * NT + t + 1) * P],
                                               src[:, t, c:c + P], ident)
                    ins.then_inc(S(done), 1)

            def ffn(f):
                u0 = BASE[f"ffn{f}"]
                acc = take([4, 5, 6, 7], [({1: "h_n1", 2: "h_n3", 3: "h_n6"}[f], 2)])
                gu = take([0, 1], [])
                tr = take([2], [])[0]
                TRN = S(f"tr_done{f}")

                def up(s, half_, c):
                    for t in range(NT):
                        for k in range(4):
                            ins = three(ps[:, gu[t], :], acts(yT, 4 * half_ + k, t), w(s, k * 512, (k + 1) * 512),
                                        half_ == 0 and k == 0, half_ == 1 and k == 3)
                    ins.then_inc(S("unit_used"), 1)
                    return ins

                def turn_hidden():
                    for k in range(2):
                        for t in range(NT):
                            ins = pe.transpose(ps[:, tr, (k * NT + t) * P:(k * NT + t + 1) * P],
                                               prod[:, t, k * P:(k + 1) * P], ident)
                    ins.then_inc(TRN, 1)

                def down(s, first, last=False):
                    for k in range(2):
                        for t in range(NT):
                            for j in range(2):
                                c = k * D + j * 512
                                ins = three(ps[:, acc[2 * t + j], :], acts((hTh, hTl), k, t), w(s, c, c + 512),
                                            first and k == 0, last and k == 1)
                    ins.then_inc(S("unit_used"), 1)

                def step(c, s0, first):
                    u = 3 * c - 1 + u0
                    pe.wait_ge(*W("lo_ready", u + 1))
                    pe.wait_ge(*W(f"prod_ready{f}", 2 * c))
                    up(s0, 0, c)
                    turn_hidden()
                    pe.wait_ge(*W("lo_ready", u + 2))
                    up((s0 + 1) % RING, 1, c)
                    pe.wait_ge(*W("lo_ready", u + 3))
                    pe.wait_ge(*W(f"hT_ready{f}", c))
                    down((s0 + 2) % RING, first)

                begin(u0)
                pe.wait_ge(*W({1: "ylo_n0", 2: "ylo_n2", 3: "ylo_n5"}[f], KD))
                up(u0 % RING, 0, 0)
                begin(u0 + 1)
                up((u0 + 1) % RING, 1, 0)
                s0 = (u0 + 2) % RING
                step(1, s0, True)
                with pe.Fori(2, NCH) as c:
                    step(c, s0, False)
                pe.wait_ge(*W(f"prod_ready{f}", 2 * NCH))
                turn_hidden()
                pe.wait_ge(*W("lo_ready", u0 + FFN_UNITS))
                pe.wait_ge(*W(f"hT_ready{f}", NCH))
                down((u0 + FFN_UNITS - 1) % RING, False, True)
                drained[0] = drained[1] = [(f"prod_ready{f}", 2 * NCH)]
                drained[2] = [(f"hT_ready{f}", NCH)]

            pe.wait_ge(*W("cn_loaded", 16))
            pe.wait_ge(*W("sm_loaded", 16))

            take([3], [("rel_ready", 1)])
            pe.matmul(ps[0:HEADS, 3, 0:NREL], M("rel")[0:BUCKETS, :], C("onehot")[0:BUCKETS, :],
                      start=True, stop=True).then_inc(S("rel_done"), 1)

            turn(("hn_n0", 2), hn_f, "nT_n0", "ylo_n0")
            ffn(1)

            turn(("hn_n1", 2), hn_m, "nT_n1", "ylo_n1")
            pe.wait_ge(*W("ylo_n1", KD))
            for part, name, b in (("f_h", "fh", 4), ("q_h", "qh", 6)):
                for n in range(2):
                    take([b + n], [(f"{name}_out", n + 1)])
                    features(BASE[part] + n, b + n)
            u = BASE["kv"]
            begin(u)
            take([0, 1], [("kvn", 8)])
            for t in range(NT):
                for k in range(KD):
                    ins = three(ps[:, t, 0:KV_COLS], acts(yT, k, t), w(u % RING, k * 256, k * 256 + KV_COLS),
                                k == 0, k == KD - 1)
            ins.then_inc(S("unit_used"), 1)
            for part, name, b in (("q_idx", "qi", 4), ("q_a", "qa", 6)):
                for n in range(2):
                    take([b + n], [(f"{name}_out", n + 1)])
                    features(BASE[part] + n, b + n)
            take([2], [("kvT_out", 1)])
            pe.wait_ge(*W("kvn", 8))
            for m, src in enumerate((ckvn, kk2)):
                for t in range(NT):
                    ins = pe.transpose(ps[:, 2, (m * NT + t) * P:(m * NT + t + 1) * P], src[:, t, :], ident)
            ins.then_inc(S("kvT_done"), 1)

            def level(n):
                e = E[n % 2]
                if n > len(LEVELS):
                    b = take([4], [("cross_out", 1)])[0]
                    pe.wait_ge(*W("E_ready", 2 * n))
                    for hd in range(HG):
                        ins = pe.matmul(ps[:, b, hd * P:(hd + 1) * P], e[:, hd, 0:P], e[:, hd, P:T],
                                        start=True, stop=True)
                    ins.then_inc(S("cross_done"), 1)
                    return
                bs = take([4, 5], [("level_out", n + 1)])
                a, q = (e, e) if n else (kf, qh)
                if n:
                    pe.wait_ge(*W("E_ready", 2 * n))
                else:
                    pe.wait_ge(*W("qh_out", 2))
                    pe.wait_ge(*W("kf_ready", 1))
                for hd in range(HG):
                    for t in range(NT):
                        m = hd * NT + t
                        ins = pe.matmul(ps[:, bs[m // 4], (m % 4) * P:(m % 4 + 1) * P],
                                        a[:, hd, t * P:(t + 1) * P], q[:, hd, t * P:(t + 1) * P],
                                        start=True, stop=True)
                ins.then_inc(S("level_done"), 1)

            level(0)
            take([0, 1], [("ih_out", 2)])
            pe.wait_ge(*W("kvT_out", 1))
            pe.wait_ge(*W("qi_out", 2))
            for n in range(2):
                for hd in range(4 * n, 4 * n + 4):
                    b = take([6 + hd % 2], [("relu_out", hd + 1)])[0]
                    a = HEAD_DIM * (hd % 2)
                    pe.matmul(ps[:, b, 0:P], qiT[a:a + 64, hd // 2, 0:P], kvT[a:a + 64, 1, 0:P],
                              start=True, stop=True)
                    pe.matmul(ps[:, b, P:3 * P], qiT[a:a + 64, hd // 2, P:T], kvT[a:a + 64, 1, :],
                              start=True, stop=True).then_inc(S("dots_done"), 1)
                row_unit(BASE["i_h"], n, 2, yT, [0, 1])
            banks = {("g_h", 0): ([2, 3], [("gh_out", 2)]), ("gate_b", 0): ([0, 1], [("gate_b_out", 2)]),
                     ("gate_b", 2): ([2, 3], [("gate_b_out", 4)]), ("gate_a", 0): ([6, 7], [("gate_a_out", 2)])}
            for n, (part, m) in enumerate(BETWEEN):
                level(n + 1)
                if m % 2 == 0:
                    bs = take(*banks[part, m])
                row = {"g_h": None, "gate_b": 2 + m // 2, "gate_a": m // 2}[part]
                row_unit(BASE[part] + m // 2 * 2, m % 2, 2, yT, bs, row)
            pe.wait_ge(*W("level_out", len(LEVELS) + 1))
            pe.wait_ge(*W("cross_out", 1))
            pe.wait_ge(*W("ih_out", 2))
            for t in range(NT):
                b = take([t], [("on_ready", 2 * (t + 1))])[0]
                for hd in range(HG):
                    c = slice(hd * P, (hd + 1) * P)
                    ins = pe.matmul(ps[:, b, c], AT[:, hd, t, :], vv[:, t, c], start=True, stop=(t == 0))
                    if t:
                        ins = pe.matmul(ps[:, b, c], ATx[:, hd, :], vv[:, 0, c], start=False, stop=True)
                ins.then_inc(S("hg_o"), 1)

            def latent_queries(n):
                bs = take([4, 5], [("ql_out", 2 * (n + 1))])
                for m in range(2):
                    for r in range(2):
                        a, pair = HEAD_DIM * r, 2 * n + m
                        ins = pe.matmul(ps[:, bs[r], m * T:(m + 1) * T],
                                        M("w_uk")[a:a + 64, pair * LATENT:(pair + 1) * LATENT],
                                        qaT[a:a + 64, pair, :], start=True, stop=True)
                ins.then_inc(S("ql_done"), 1)

            pe.wait_ge(*W("qa_out", 2))
            latent_queries(0)
            bs = take([2, 3], [("gate_a_out", 4)])
            row_unit(BASE["gate_a"] + 2, 0, 2, yT, bs, 1)
            latent_queries(1)
            row_unit(BASE["gate_a"] + 2, 1, 2, yT, bs, 1)
            for t in range(NT):
                b = take([6 + t], [("yb_ready", t + 1)])[0]
                pe.wait_ge(*W("on_ready", 2 * (t + 1)))
                for hd in range(HG):
                    ins = pe.transpose(ps[:, b, hd * P:(hd + 1) * P], on[:, t, hd * P:(hd + 1) * P], ident)
                ins.then_inc(S("ybT_done"), 1)

            def logits(qt):
                nk = (qt + 1) * P
                for n in range(4):
                    b = take([4 + n], [("lg_out", 4 * qt + n + 1)])[0]
                    for r in range(2):
                        o, hd = ps[:, b, r * T:r * T + nk], 2 * n + r
                        pe.matmul(o, qlat[:, hd, qt * P:(qt + 1) * P], kvT[:, 0, 0:nk], start=True, stop=False)
                        ins = pe.matmul(o, C("flip"), bias[:, hd, T - nk:T], start=False, stop=True)
                    ins.then_inc(S("lg_done"), 1)

            pe.wait_ge(*W("ql_out", 4))
            pe.wait_ge(*W("bias_loaded", 16))
            for j in range(2):
                logits(j)
                if j == 0:
                    pe.wait_ge(*W("yb_ready", 2))
                bs = take([2 * j, 2 * j + 1], [("mb_out", 2 * (j + 1))])
                rows(BASE["br_b"] + j, 1, (ybh, ybl), bs)
            for qt in range(NT):
                pe.wait_ge(*W("probs_ready", qt + 1))
                for n in range(2 * (qt + 1)):
                    kt, g = n // 2, n % 2
                    m = 2 * qt + n
                    b = take([4 + n % 2], [("pT_out", m + 1)])[0]
                    for r in range(4):
                        ins = pe.transpose(ps[:, b, r * P:(r + 1) * P], lg[qt][:, 4 * g + r, kt * P:(kt + 1) * P],
                                           ident)
                    ins.then_inc(S("pT_done"), 1)
                pe.wait_ge(*W("pT_out", 2 + 4 * qt))
                for g in range(2):
                    b = take([6 + g], [("ol_out", 2 * qt + g + 1)])[0]
                    for kt in range(qt + 1):
                        ins = pe.matmul(ps[:, b, :], ckvn[:, kt, :],
                                        pT[:, kt, 4 * g:4 * g + 4, :].rearrange("p a b -> p (a b)"),
                                        start=(kt == 0), stop=(kt == qt))
                    ins.then_inc(S("ol_done"), 1)
                b = take([4], [("ya_ready", qt + 1)])[0]
                pe.wait_ge(*W("ol_out", 2 * (qt + 1)))
                for hd in range(HEADS):
                    a = HEAD_DIM * (hd % 2)
                    ins = pe.matmul(ps[a:a + 64, b, (hd // 2) * P:(hd // 2 + 1) * P],
                                    M("w_uv")[:, hd * 64:(hd + 1) * 64], olat[:, hd, :], start=True, stop=True)
                ins.then_inc(S("oT_done"), 1)
            pe.wait_ge(*W("ya_ready", 2))
            for j in range(2):
                bs = take([2 * j, 2 * j + 1], [("ma_out", 4 * (j + 1))])
                rows(BASE["br_a"] + j, 1, (yah, yal), bs)
            turn(("ma_out", 8), hn_m, "nT_m1", "ylo_m1")
            def out_proj(part, nk, hl, by, ready):
                take([4, 5, 6, 7], by)
                for j in range(2):
                    rows(BASE[part] + nk * j, nk, hl, [4 + j, 6 + j], ready)

            out_proj("w_out", 2, yT, [("h_n2", 2)], "ylo_m1")

            turn(("hn_n2", 2), hn_f, "nT_n2", "ylo_n2")
            ffn(2)

            turn(("hn_n3", 2), hn_f, "nT_n3", "ylo_n3")
            out_proj("ple_gate", 2, yT, [("pg_out", 2)], "ylo_n3")
            u = BASE["ple_proj"]
            begin(u)
            take([0, 1, 2, 3], [("pm_out", 2)])
            pe.wait_ge(*W("pT_split", 1))
            for t in range(NT):
                for j in range(2):
                    for k in range(2):
                        c = k * D + j * 512
                        ins = three(ps[:, 2 * t + j, :], acts((pTh, pTl), k, t), w(u % RING, c, c + 512),
                                    k == 0, k == 1)
            ins.then_inc(S("unit_used"), 1)

            turn(("hn_n4", 2), hn_s, "nT_n4", "ylo_n4")
            pe.wait_ge(*W("ylo_n4", KD))
            for part in ("s_c", "s_x", "s_b"):
                for n in range(4):
                    b = take([4 + n], [(f"{part}_out", n + 1)])[0]
                    features(BASE[part] + n, b)
            for j in range(2):
                bs = take([2 * j, 2 * j + 1], [("gb_out", 2 * (j + 1))])
                rows(BASE["g_b"] + 2 * j, 2, yT, bs)
            out_proj("sconv_proj", 2, (svh, svl), [("mgb_out", 4)], "sv_ready")
            u = BASE["dt"]
            begin(u)
            take([0], [("dt_out", 1)])
            for t in range(NT):
                for k in range(KD):
                    ins = three(ps[:, 0, t * SSD_HEADS:(t + 1) * SSD_HEADS], acts(yT, k, t),
                                w(u % RING, k * SSD_HEADS, (k + 1) * SSD_HEADS), k == 0, k == KD - 1)
            ins.then_inc(S("unit_used"), 1)
            for n in range(12):
                b = take([4 + n % 4], [("conv_out", 2 * (n + 1))])[0]
                features(BASE["xbc"] + n, b)
                if n == 3:
                    pe.wait_ge(*W("dtA_ready", 1))
                    take([1], [("kd_sub", 1)])
                    for t in range(NT):
                        pe.matmul(ps[:, 1, t * 32:(t + 1) * 32], C("tri"), dts[:, 1, t, :], start=True, stop=True)
                    pe.matmul(ps[:, 1, 64:96], C("ones"), dts[:, 1, 0, :], start=True, stop=True)\
                      .then_inc(S("ac_done"), 1)
                elif n >= 4:
                    q, t = (n - 4) // 2, (n - 4) % 2
                    b = take([2 + n % 2], [("xdt_out", n - 3)])[0]
                    pe.wait_ge(*W("xs_ready", 4 * q + 4))
                    for r in range(4):
                        ins = pe.transpose(ps[:, b, r * P:(r + 1) * P], xs[:, 4 * q + r, t * P:(t + 1) * P], ident)
                    ins.then_inc(S("xT_done"), 1)

            def sums_ahead(q):
                bs = take([4, 5], [("seg_sub", 8 * (q + 1)), ("cross_exp", 2 * (q + 1))])
                for r in range(4):
                    for t in range(NT):
                        hd = 4 * q + r
                        ins = pe.matmul(ps[:, bs[r // 2], ((r % 2) * NT + t) * P:((r % 2) * NT + t + 1) * P],
                                        dts[:, 1, t, hd:hd + 1].to_broadcast([P, P]), C("tri"),
                                        start=True, stop=True)
                ins.then_inc(S("bc_done"), 1)

            def group_sums(g):
                pe.wait_ge(*W("sq_ready", g + 1))
                for t in range(NT):
                    c = t * GROUPS + g
                    for k in range(GT):
                        ins = pe.matmul(ps[:, 3, c:c + 1], sq[:, k, t * P:(t + 1) * P], C("ones")[:, 0:1],
                                        start=(k == 0), stop=(k == GT - 1))
                ins.then_inc(S("ssg_done"), 1)

            sums_ahead(0)
            pe.wait_ge(*W("xs_ready", 24))
            for g in range(GROUPS):
                b = take([6 + g % 2], [("cb_out", 3 * (g + 1))])[0]
                pe.matmul(ps[:, b, 0:T], bc[:, g, 0:P], bc[:, GROUPS + g, :], start=True, stop=True)
                pe.matmul(ps[:, b, T:T + P], bc[:, g, P:T], bc[:, GROUPS + g, P:T],
                          start=True, stop=True).then_inc(S("cb_done"), 1)
            for q in range(8):
                take([q % 3], [("z_out", q + 1)])
                features(BASE["z"] + q, q % 3)
                if q < 7:
                    sums_ahead(q + 1)
                if q == 3:
                    take([3], [("ss_ssd", 1)])
                if q >= 3 and q % 2:
                    group_sums((q - 3) // 2)
                pe.wait_ge(*W("sc_ready", q + 1))
                if q == 0:
                    pe.wait_ge(*W("xw_ready", 1))
                b = take([6 + q % 2], [("y_out", 2 * (q + 1))])[0]
                for r in range(4):
                    hd = 4 * q + r
                    a, c = 64 * (r % 2), (r // 2) * T
                    pe.matmul(ps[a:a + 64, b, c:c + P], xdt[:, 0, hd, :], seg[:, r, 0, :], start=True, stop=True)
                    pe.matmul(ps[a:a + 64, b, c + P:c + T], xw[:, hd, :], seg[:, r, 1, :], start=True, stop=False)
                    ins = pe.matmul(ps[a:a + 64, b, c + P:c + T], xdt[:, 1, hd, :], seg[:, r, 2, :],
                                    start=False, stop=True)
                ins.then_inc(S("y_done"), 1)
            bs = take([0, 1], [("ga_out", 2)])
            row_unit(BASE["g_a"], 0, 2, yT, bs)
            group_sums(GROUPS - 1)
            row_unit(BASE["g_a"], 1, 2, yT, bs)
            pe.wait_ge(*W("rstd_ssd", 1))
            take([6, 7], [("yn_out", GROUPS)])
            for g in range(GROUPS):
                for t in range(NT):
                    c = 24 + t * GROUPS + g
                    m = g * NT + t
                    ins = pe.matmul(ps[:, 6 + m // 4, (m % 4) * P:(m % 4 + 1) * P],
                                    st[:, c:c + 1].to_broadcast([P, P]), ident, start=True, stop=True)
            ins.then_inc(S("rb_done"), 1)
            rows(BASE["g_a"] + 2, 2, yT, take([2, 3], [("ga_out", 4)]))
            out_proj("ssd_proj", 4, (yhi, ylo), [("mga_out", 8)], "ylo_ssd")
            turn(("mga_out", 8), merged, "nT_m2", "ylo_m2")
            out_proj("w_o", 2, yT, [("h_n5", 2)], "ylo_m2")

            turn(("hn_n5", 2), hn_f, "nT_n5", "ylo_n5")
            ffn(3)

        @block.scalar
        def _(act):
            done = [0]
            count = [0]

            def link(ins):
                count[0] += 1
                ins.then_inc(S("act_chain"), 1)
                act.wait_ge(*W("act_chain", count[0]))

            def hi(u, slot):
                act.activation(whi[slot][:, :], raw[slot][:, :], ACT.Copy).then_inc(S("hi_ready"), 1)

            def through(part, n):
                act.wait_ge(*W("unit_used", BASE[part] + n))

            def ahead(n):
                while done[0] < min(n, N_UNITS):
                    u = done[0]
                    act.wait_ge(*W(f"raw_loaded{u % RING}", 16 * (u // RING + 1)))
                    if u >= RING:
                        act.wait_ge(*W("unit_used", u - RING + 1))
                    hi(u, u % RING)
                    done[0] += 1

            def sums(name, ready, src, a):
                for t in range(NT):
                    act.wait_ge(*W(ready[0], ready[1] * (t + 1) if ready[1] else 1))
                    act.activation(junk(t), src(t), ACT.Square, accum_out=st[:, a + t:a + t + 1])\
                       .then_inc(S(name), 1)

            cur = [hn_f]

            def junk(t):
                return cur[0][:, t, :]

            def turned(nT, g, out_name):
                for f in range(KD):
                    if f % 2 == 0:
                        act.wait_ge(*W(nT, f // 2 + 1))
                    src = ps[:, f // 2, (f % 2) * T:(f % 2 + 1) * T]
                    sc = 1.0 if g is None else M(g)[:, f:f + 1]
                    act.activation(yTh[:, f, :], src, ACT.Copy, scale=sc).then_inc(S(out_name), 1)

            def ffn(f):
                u0 = BASE[f"ffn{f}"]
                s0 = (u0 + 2) % RING
                SIL, HHI = S(f"sil_ready{f}"), S(f"hTh_ready{f}")

                def silu(used):
                    act.wait_ge(*W("unit_used", used))
                    for t in range(NT):
                        act.activation(sil[:, t, :], ps[:, t, 0:FCH], ACT.Silu).then_inc(SIL, 1)

                def hidden(c):
                    act.wait_ge(*W(f"tr_done{f}", c))
                    act.activation(hTh[:, :, :].rearrange("p a b -> p (a b)"), ps[:, 2, :], ACT.Copy).then_inc(HHI, 1)

                def split(u, slot, landed):
                    act.wait_ge(*W(f"raw_loaded{slot}", landed))
                    act.wait_ge(*W("unit_used", u - RING + 1))
                    hi(u, slot)

                ahead(u0 + 2)
                ahead(u0 + 3)
                silu(u0 + 2)
                ahead(u0 + 5)

                def step(c, splits):
                    u = 3 * c + (u0 + 2)
                    hidden(c)
                    for n in range(RING):
                        if n == 1:
                            silu(3 * c + (u0 + 1))
                        if n < splits:
                            split(u + n, (s0 + n) % RING, 16 * c + 16 * ((u0 + 2 + n) // RING + 1))

                with act.Fori(1, NCH - 1) as c:
                    step(c, RING)
                step(NCH - 1, min(RING, N_UNITS - (u0 + FFN_UNITS - 1)))
                done[0] = u0 + FFN_UNITS + 2
                hidden(NCH)

            act.wait_ge(*W("sm_loaded", 16))
            act.wait_ge(*W("lb_sub", 2))
            act.activation(st[:, 40:48], st[:, 40:48], ACT.Exp).then_inc(S("lb_exp"), 1)
            act.activation(M("a_log"), M("a_log"), ACT.Exp).then_inc(S("alog_exp"), 1)
            act.wait_ge(*W("rel_done", 1))
            act.activation(rel8[:, :], ps[0:HEADS, 3, 0:NREL], ACT.Copy).then_inc(S("rel_ready"), 1)

            act.wait_ge(*W("x_loaded", 16))
            for t in range(NT):
                act.activation(hn_f[:, t, :], h[:, t, :], ACT.Square, accum_out=st[:, t:t + 1])\
                   .then_inc(S("ss_n0"), 1)
            ahead(2)
            turned("nT_n0", "g_ffn1", "yhi_n0")
            ffn(1)

            def post_sums(part, n, name):
                through(part, n)
                for t in range(NT):
                    act.activation(junk(t), ps[:, 4 + 2 * t:6 + 2 * t, :].rearrange("p a b -> p (a b)"), ACT.Square,
                                   accum_out=st[:, 2 + t:3 + t]).then_inc(S(name), 1)

            def norm_sums(n, a=0):
                for t in range(NT):
                    act.wait_ge(*W(f"h_{n}", t + 1))
                    act.activation(junk(t), h[:, t, :], ACT.Square, accum_out=st[:, a + t:a + t + 1])\
                       .then_inc(S(f"ss_{n}"), 1)

            post_sums("ffn1", FFN_UNITS, "ss_p0")
            ahead(BASE["f_h"] + 3)
            cur[0] = hn_m
            norm_sums("n1")
            turned("nT_n1", "g_mix", "yhi_n1")

            def both(t):
                return t.rearrange("p a b -> p (a b)")

            def project(part, name, dst, fn, b):
                for m in range(2):
                    through(part, m + 1)
                    act.activation(both(dst[:, 2 * m:2 * m + 2, :]), ps[:, b + m, :], fn).then_inc(S(f"{name}_out"), 1)
                    ahead(BASE[part] + m + 1 + RING)

            project("f_h", "fh", sg, ACT.Sigmoid, 4)
            project("q_h", "qh", qh, ACT.Silu, 6)
            act.wait_ge(*W("f_ready", 1))
            act.activation(sg[:, :, :], sg[:, :, :], ACT.Ln).then_inc(S("lnf_ready"), 1)
            for t in range(NT):
                through("kv", 1)
                act.activation(hn_m[:, t, 0:LATENT], ps[:, t, 0:LATENT], ACT.Square,
                               accum_out=st[:, 8 + t:9 + t]).then_inc(S("ss_kv"), 1)
                act.activation(hn_m[:, t, LATENT:LATENT + 64], ps[:, t, LATENT:LATENT + 64], ACT.Square,
                               accum_out=st[:, 10 + t:11 + t]).then_inc(S("ss_kv"), 1)
            ahead(BASE["kv"] + 1 + RING)
            project("q_idx", "qi", qiT, ACT.Copy, 4)
            project("q_a", "qa", qaT, ACT.Copy, 6)
            act.wait_ge(*W("kvT_done", 1))
            act.activation(both(kvT[:, :, :]), ps[:, 2, :], ACT.Copy).then_inc(S("kvT_out"), 1)

            def exponential(n):
                act.wait_ge(*W("X_sub", 2 * n))
                act.activation(X[:, :, :], X[:, :, :], ACT.Exp).then_inc(S("X_exp"), 1)

            def gate(j, part, dst, b):
                through(part, 2 * (j + 1))
                for t in range(NT):
                    act.activation(dst[:, t, :], ps[:, b + t, :], ACT.Sigmoid).then_inc(S(f"{part}_out"), 1)

            exponential(1)
            for n in range(2):
                for hd in range(4 * n, 4 * n + 4):
                    act.wait_ge(*W("dots_done", hd + 1))
                    if hd >= 2:
                        act.wait_ge(*W("score_acc", 2 * (hd - 1)))
                    act.activation(both(relu[hd % 2]), ps[:, 6 + hd % 2, 0:3 * P], ACT.Relu)\
                       .then_inc(S("relu_out"), 1)
                if n == 0:
                    ahead(BASE["i_h"] + n + 1 + RING)
                    exponential(2)
            for n, (part, m) in enumerate(BETWEEN):
                if n + 3 <= len(LEVELS) + 1:
                    exponential(n + 3)
                if n == 0:
                    through("i_h", 2)
                    for t in range(NT):
                        act.activation(vv[:, t, :], ps[:, t, :], ACT.Copy).then_inc(S("ih_out"), 1)
                elif (part, m) == ("gate_b", 0):
                    through("g_h", 2)
                    for t in range(NT):
                        act.activation(sgh[:, t, :], ps[:, 2 + t, :], ACT.Silu).then_inc(S("gh_out"), 1)
                elif (part, m) == ("gate_b", 2):
                    gate(0, "gate_b", gates[:, :, 0:512], 0)
                elif (part, m) == ("gate_a", 0):
                    gate(1, "gate_b", gates[:, :, 512:1024], 2)
                ahead(BASE[part] + m + RING)
            for t in range(NT):
                act.wait_ge(*W("hg_o", t + 1))
                act.activation(on[:, t, 512:1024], ps[:, t, :], ACT.Square).then_inc(S("osq_ready"), 1)

            def latent_queries(n):
                act.wait_ge(*W("ql_done", n + 1))
                for r in range(2):
                    q = qlat[:, 4 * n:4 * n + 4, :].rearrange("p (m r) t -> p r m t", r=2)
                    act.activation(q[:, r, :, :], ps[:, 4 + r, :].rearrange("p (m t) -> p m t", m=2), ACT.Copy,
                                   scale=ATT_SCALE)\
                       .then_inc(S("ql_out"), 1)

            latent_queries(0)
            ahead(BASE["gate_a"] + 2 + RING)
            gate(0, "gate_a", gates_a[0], 6)
            latent_queries(1)
            ahead(BASE["gate_a"] + 3 + RING)
            for t in range(NT):
                act.wait_ge(*W("ybT_done", t + 1))
                act.activation(ybh[:, :, t * P:(t + 1) * P], ps[:, 6 + t, :].rearrange("p (a b) -> p a b", a=4),
                               ACT.Copy, scale=M("hg_norm")).then_inc(S("ybh_ready"), 1)
            act.wait_ge(*W("on_ready", 4))
            gate(1, "gate_a", gates_a[1], 2)
            ahead(BASE["gate_a"] + 4 + RING)
            for qt in range(NT):
                nk = (qt + 1) * P
                act.wait_ge(*W("max_ready", qt + 1))
                for hd in range(HEADS):
                    act.activation(lg[qt][:, hd, 0:nk], lg[qt][:, hd, 0:nk], ACT.Exp,
                                   bias=st[:, MAXIMA[qt] + hd:MAXIMA[qt] + hd + 1],
                                   accum_out=st[:, TOTALS[qt] + hd:TOTALS[qt] + hd + 1]).then_inc(S("exp_ready"), 1)
                ahead(BASE["br_b"] + qt + 1 + RING)
            for qt in range(NT):
                for n in range(2 * (qt + 1)):
                    kt, g = n // 2, n % 2
                    act.wait_ge(*W("pT_done", 2 * qt + n + 1))
                    act.activation(both(pT[:, kt, 4 * g:4 * g + 4, :]), ps[:, 4 + n % 2, :], ACT.Copy)\
                       .then_inc(S("pT_out"), 1)
                for g in range(2):
                    act.wait_ge(*W("ol_done", 2 * qt + g + 1))
                    act.activation(both(olat[:, 4 * g:4 * g + 4, :]), ps[:, 6 + g, :], ACT.Copy)\
                       .then_inc(S("ol_out"), 1)
                act.wait_ge(*W("oT_done", qt + 1))
                act.activation(yah[:, :, qt * P:(qt + 1) * P], ps[:, 4, :].rearrange("p (a b) -> p a b", a=4),
                               ACT.Copy).then_inc(S("yah_ready"), 1)
            ahead(BASE["br_a"] + 1 + RING)
            ahead(BASE["br_a"] + 2 + RING)
            turned("nT_m1", None, "yhi_m1")
            ahead(BASE["w_out"] + 1 + RING)
            ahead(BASE["w_out"] + 4 + RING)
            cur[0] = hn_f
            post_sums("w_out", 4, "ss_p1")
            norm_sums("n2")
            turned("nT_n2", "g_ffn2", "yhi_n2")
            ffn(2)
            post_sums("ffn2", FFN_UNITS, "ss_p2")
            norm_sums("n3")
            turned("nT_n3", "g_ple", "yhi_n3")
            act.wait_ge(*W("p_loaded", 16))
            act.activation(pTh[:, :, :], praw[:, :, :], ACT.Copy).then_inc(S("pTh_ready"), 1)
            ahead(BASE["ple_gate"] + 4 + RING)
            for t in range(NT):
                through("ple_gate", 4)
                act.activation(pgate[:, t, :], ps[:, 4 + 2 * t:6 + 2 * t, :].rearrange("p a b -> p (a b)"),
                               ACT.Sigmoid).then_inc(S("pg_out"), 1)
            ahead(BASE["ple_proj"] + 1 + RING)
            for t in range(NT):
                act.wait_ge(*W("pm_out", t + 1))
                act.activation(junk(t), pgate[:, t, :], ACT.Square, accum_out=st[:, 2 + t:3 + t])\
                   .then_inc(S("ss_p3"), 1)

            cur[0] = hn_s
            norm_sums("n4")
            turned("nT_n4", "g_mix2", "yhi_n4")
            w3 = M("sconv_w")
            for n in range(4):
                through("s_c", n + 1)
                act.activation(both(cx[:, 2 * n:2 * n + 2, :]), ps[:, 4 + n, :], ACT.Copy).then_inc(S("s_c_out"), 1)
                ahead(BASE["s_c"] + n + 1 + RING)
            for n in range(4):
                act.wait_ge(*W("s_x_out", n + 1))
                for f in (2 * n, 2 * n + 1):
                    act.activation(cv[:, f, :], cx[:, f, :], ACT.Copy, scale=w3[:, 3 * f + 2:3 * f + 3])\
                       .then_inc(S("cv_first"), 1)
                ahead(BASE["s_x"] + n + 1 + RING)
            for n in range(4):
                act.wait_ge(*W("s_b_out", n + 1))
                act.activation(both(svh[:, 2 * n:2 * n + 2, :]), both(cx[:, 2 * n:2 * n + 2, :]), ACT.Copy)\
                   .then_inc(S("svh_ready"), 1)
                ahead(BASE["s_b"] + n + 1 + RING)
            for j in range(2):
                through("g_b", 2 * (j + 1))
                for t in range(NT):
                    act.activation(sga[:, t, j * 512:(j + 1) * 512], ps[:, 2 * j + t, :], ACT.Sigmoid)\
                       .then_inc(S("gb_out"), 1)
                ahead(BASE["g_b"] + 2 * j + 2 + RING)
            ahead(BASE["sconv_proj"] + 4 + RING)
            ahead(BASE["dt"] + 1 + RING)
            act.wait_ge(*W("sp_abs", 1))
            act.activation(dts[:, 3, :, :], dts[:, 3, :, :], ACT.Exp, scale=-1.0).then_inc(S("sp_exp"), 1)
            cw, cb = M("conv_w"), M("conv_b")

            def conv_silu(n):
                act.wait_ge(*W("conv_out", 2 * (n + 1)))
                dst = xs[:, 2 * n:2 * n + 2, :] if n < 8 else bc[:, 2 * n - 16:2 * n - 14, :]
                act.activation(both(dst), both(cvt[:, n % 2, :, :]), ACT.Silu).then_inc(S("xs_ready"), 2)

            for n in range(12):
                through("xbc", n + 1)
                if n >= 2:
                    act.wait_ge(*W("xs_ready", 2 * (n - 1)))
                for r in range(2):
                    f = 2 * n + r
                    act.activation(cvt[:, n % 2, r, :], ps[:, 4 + n % 4, r * T:(r + 1) * T], ACT.Identity,
                                   bias=cb[:, f:f + 1], scale=cw[:, 4 * f + 3:4 * f + 4]).then_inc(S("cvt_first"), 1)
                if n:
                    conv_silu(n - 1)
                ahead(BASE["xbc"] + n + 1 + RING)
            conv_silu(11)
            act.wait_ge(*W("kd_sub", 1))
            act.activation(dts[:, 8, 0, :], dts[:, 8, 0, :], ACT.Exp).then_inc(S("kd_exp"), 1)

            def group_squares(g):
                act.wait_ge(*W("z_out", 2 * g + 2))
                if g:
                    act.wait_ge(*W("ssg_done", g))
                act.activation(both(sq[:, :, :]), both(xs[:, GT * g:GT * g + GT, :]), ACT.Square)\
                   .then_inc(S("sq_ready"), 1)

            for q in range(8):
                act.wait_ge(*W("bc_done", q + 1))
                if q:
                    act.wait_ge(*W("y_done", q))
                for n in range(2):
                    act.activation(seg[:, 2 * n:2 * n + 2, 1, :],
                                   ps[:, 4 + n, :].rearrange("p (r t c) -> p r t c", r=2, t=NT)[:, :, 1, :], ACT.Exp)\
                       .then_inc(S("cross_exp"), 1)
                act.wait_ge(*W("seg_sub", 8 * (q + 1)))
                for n in (0, 2):
                    act.activation(seg[:, :, n, :], seg[:, :, n, :], ACT.Exp).then_inc(S("seg_exp"), 1)
                if q >= 2 and q % 2 == 0:
                    group_squares(q // 2 - 1)
                through("z", q + 1)
                if q:
                    act.wait_ge(*W("z_out", q))
                act.activation(both(zs[:, :, :]), ps[:, q % 3, :], ACT.Silu).then_inc(S("zs_ready"), 1)
                ahead(BASE["z"] + q + 1 + RING)
            group_squares(GROUPS - 1)

            def gates_out(j):
                through("g_a", 2 * (j + 1))
                for t in range(NT):
                    act.activation(sga[:, t, j * 512:(j + 1) * 512], ps[:, 2 * j + t, :], ACT.Sigmoid)\
                       .then_inc(S("ga_out"), 1)

            ahead(BASE["g_a"] + 1 + RING)
            gates_out(0)
            ahead(BASE["g_a"] + 2 + RING)
            nw = M("ssd_norm")
            for f in range(XT):
                act.wait_ge(*W("yn_out", f // GT + 1))
                act.activation(yhi[:, f, :], xs[:, f, :], ACT.Copy, scale=nw[:, f:f + 1]).then_inc(S("yhi_ssd"), 1)
                if f == 2 * GT - 1:
                    ahead(BASE["g_a"] + 3 + RING)
            gates_out(1)
            ahead(BASE["ssd_proj"] + 8 + RING)
            turned("nT_m2", None, "yhi_m2")
            ahead(BASE["w_o"] + 4 + RING)
            cur[0] = hn_f
            norm_sums("n5")
            turned("nT_n5", "g_ffn3", "yhi_n5")
            ffn(3)
            norm_sums("n6")

        @block.vector
        def _(dve):
            done = [0]
            count = [0]

            def link(ins):
                count[0] += 1
                ins.then_inc(S("dve_chain"), 1)
                dve.wait_ge(*W("dve_chain", count[0]))

            def lo(u, slot):
                dve.tensor_tensor(wlo[slot][:, :], raw[slot][:, :], f32(whi[slot][:, :]), ALU.subtract)\
                   .then_inc(S("lo_ready"), 1)

            def through(part, n):
                dve.wait_ge(*W("unit_used", BASE[part] + n))

            def ahead(n):
                while done[0] < min(n, N_UNITS):
                    u = done[0]
                    dve.wait_ge(*W("hi_ready", u + 1))
                    lo(u, u % RING)
                    done[0] += 1

            def normed(n, dst):
                dve.wait_ge(*W(f"rstd_{n}", 1))
                for t in range(NT):
                    dve.tensor_scalar(dst[:, t, :], h[:, t, :], st[:, t:t + 1], None, ALU.mult)\
                       .then_inc(S(f"hn_{n}"), 1)

            def turned(n, g):
                for f in range(KD):
                    src = ps[:, f // 2, (f % 2) * T:(f % 2 + 1) * T]
                    if f % 2 == 0:
                        dve.wait_ge(*W(f"yhi_{n}", f + 2))
                    if g is None:
                        ins = dve.tensor_tensor(yTl[:, f, :], src, f32(yTh[:, f, :]), ALU.subtract)
                    else:
                        ins = dve.scalar_tensor_tensor(yTl[:, f, :], src, M(g)[:, f:f + 1], f32(yTh[:, f, :]),
                                                       ALU.mult, ALU.subtract)
                    ins.then_inc(S(f"ylo_{n}"), 1)

            def ffn(f):
                u0 = BASE[f"ffn{f}"]
                s0 = (u0 + 2) % RING
                def gated(c2):
                    for t in range(NT):
                        dve.wait_ge(*W(f"sil_ready{f}", c2 + t + 1))
                        dve.tensor_tensor(prod[:, t, :], sil[:, t, :], ps[:, t, FCH:2 * FCH], ALU.mult)\
                           .then_inc(S(f"prod_ready{f}"), 1)

                def hidden(c):
                    dve.wait_ge(*W(f"hTh_ready{f}", c))
                    dve.tensor_tensor(hTl[:, :, :].rearrange("p a b -> p (a b)"), ps[:, 2, :],
                                      f32(hTh[:, :, :].rearrange("p a b -> p (a b)")), ALU.subtract)\
                       .then_inc(S(f"hT_ready{f}"), 1)

                ahead(u0 + 2)
                ahead(u0 + 3)
                gated(0)
                ahead(u0 + 5)

                def step(c, splits):
                    hidden(c)
                    for n in range(RING):
                        if n == 1:
                            gated(2 * c)
                        if n < splits:
                            dve.wait_ge(*W("hi_ready", 3 * c + (u0 + 2 + n + 1)))
                            lo(None, (s0 + n) % RING)

                with dve.Fori(1, NCH - 1) as c:
                    step(c, RING)
                step(NCH - 1, min(RING, N_UNITS - (u0 + FFN_UNITS - 1)))
                done[0] = u0 + FFN_UNITS + 2
                hidden(NCH)

            def post_norm(n, new, src, gain_loaded):
                dve.wait_ge(*W(f"rstd_{n}", 1))
                dve.wait_ge(*W("post_loaded", gain_loaded))
                for t in range(NT):
                    link(dve.scalar_tensor_tensor(scr[0][:, t, :], src(t), st[:, 2 + t:3 + t], post[:, :],
                                                  ALU.mult, ALU.mult))
                    dve.tensor_tensor(h[:, t, :], h[:, t, :], scr[0][:, t, :], ALU.add).then_inc(S(f"h_{new}"), 1)

            def acc(t):
                return ps[:, 4 + 2 * t:6 + 2 * t, :].rearrange("p a b -> p (a b)")

            scr = [hn_f]
            dve.wait_ge(*W("sm_loaded", 16))
            lbr = M("hg_lb").rearrange("p (a b) -> p a b", a=2)
            link(dve.tensor_tensor(st[:, 36:40], lbr[:, 0, :], lbr[:, 1, :], ALU.max))
            for r in range(2):
                dve.tensor_tensor(st[:, 40 + 4 * r:44 + 4 * r], lbr[:, r, :], st[:, 36:40], ALU.subtract)\
                   .then_inc(S("lb_sub"), 1)
            dve.wait_ge(*W("lb_exp", 1))
            link(dve.tensor_tensor(st[:, 44:48], st[:, 40:44], st[:, 44:48], ALU.add))
            link(dve.reciprocal(st[:, 44:48], st[:, 44:48]))
            link(dve.tensor_tensor(st[:, 40:44], st[:, 40:44], st[:, 44:48], ALU.mult))
            link(dve.tensor_scalar(st[:, 44:48], st[:, 40:44], -1.0, 1.0, ALU.mult, ALU.add))
            dve.wait_ge(*W("x_loaded", 16))
            normed("n0", hn_f)
            ahead(2)
            turned("n0", "g_ffn1")
            ffn(1)
            post_norm("p0", "n1", acc, 16)
            ahead(BASE["f_h"] + 3)
            scr[0] = hn_m
            normed("n1", hn_m)
            turned("n1", "g_mix")
            ahead(BASE["f_h"] + 1 + RING)
            dve.wait_ge(*W("fh_out", 2))
            for hd in range(HG):
                link(dve.tensor_scalar(sg[:, hd, :], sg[:, hd, :], st[:, 44 + hd:45 + hd], st[:, 40 + hd:41 + hd],
                                       ALU.mult, ALU.add))
            dve.tensor_scalar(kf[:, :, :], sg[:, :, :], -1.0, 1.0, ALU.mult, ALU.add).then_inc(S("kf_ready"), 1)
            dve.wait_ge(*W("kf_ready", 1))
            dve.tensor_scalar(sg[:, :, :], sg[:, :, :], 2.0 ** -64, None, ALU.max).then_inc(S("f_ready"), 1)
            for n in range(1, 4):
                ahead(BASE["f_h"] + n + 1 + RING)
            dve.memset(AT[:, :, :, :], 0.0).then_inc(S("AT_zero"), 1)
            dve.wait_ge(*W("lnf_ready", 1))
            for hd in range(HG):
                link(dve.tensor_tensor_scan(G[:, hd, :], C("reset"), sg[:, hd, :], 0.0, ALU.mult, ALU.add))
            dve.wait_ge(*W("rstd_kv", 1))
            for t in range(NT):
                dve.scalar_tensor_tensor(ckvn[:, t, :], ps[:, t, 0:LATENT], st[:, 8 + t:9 + t], M("kv_g"),
                                         ALU.mult, ALU.mult).then_inc(S("kvn"), 1)
                for r in range(2):
                    dve.scalar_tensor_tensor(kk2[:, t, r * 64:(r + 1) * 64], ps[:, t, LATENT:LATENT + 64],
                                             st[:, 10 + t:11 + t], M("ki_g"), ALU.mult, ALU.mult)\
                       .then_inc(S("kvn"), 1)
                dve.tensor_scalar(wi[:, t, :], ps[:, t, LATENT + 64:KV_COLS], IDX_W_SCALE, None, ALU.mult)\
                   .then_inc(S("kvn"), 1)
            ahead(BASE["kv"] + 1 + RING)

            def blocks(x, b):
                return x.rearrange("p h (n r b) -> p (h n) r b", r=2, b=b)

            def exponents(n):
                if n > 1:
                    dve.wait_ge(*W("E_ready", 2 * (n - 1)))
                if n <= len(LEVELS):
                    b = LEVELS[n - 1]
                    g, x = blocks(G[:, :, :], b), blocks(X[:, :, :], b)
                    nb = HG * T // (2 * b)
                    ref = g[:, :, 0, b - 1:b].to_broadcast([P, nb, b])
                    if b < CHUNK:
                        dve.tensor_tensor(x[:, :, 1, :], g[:, :, 1, :], ref, ALU.subtract).then_inc(S("X_sub"), 1)
                    else:
                        dve.tensor_copy(x[:, :, 1, :], g[:, :, 1, :]).then_inc(S("X_sub"), 1)
                    dve.tensor_tensor(x[:, :, 0, :], ref, g[:, :, 0, :], ALU.subtract).then_inc(S("X_sub"), 1)
                else:
                    g = G[:, :, :].rearrange("p h (n c) -> p h n c", c=CHUNK)
                    x = X[:, :, :].rearrange("p h (n c) -> p h n c", c=CHUNK)

                    def last(c):
                        return g[:, :, c, CHUNK - 1:CHUNK].to_broadcast([P, HG, CHUNK])

                    link(dve.tensor_copy(x[:, :, 2, :], g[:, :, 2, :]))
                    link(dve.tensor_tensor(x[:, :, 3, :], g[:, :, 3, :], last(2), ALU.add))
                    link(dve.tensor_tensor(x[:, :, 1, :], last(1), g[:, :, 1, :], ALU.subtract))
                    link(dve.tensor_tensor(x[:, :, 0, :], last(0), g[:, :, 0, :], ALU.subtract))
                    dve.tensor_tensor(x[:, :, 0, :], x[:, :, 0, :], last(1), ALU.add).then_inc(S("X_sub"), 2)

            def decayed(n):
                dve.wait_ge(*W("X_exp", n))
                if n == 1:
                    dve.wait_ge(*W("qh_out", 2))
                e = E[n % 2]
                b = LEVELS[n - 1] if n <= len(LEVELS) else P
                x, eb = blocks(X[:, :, :], b), blocks(e[:, :, :], b)
                dve.tensor_tensor(eb[:, :, 1, :], x[:, :, 1, :], blocks(qh[:, :, :], b)[:, :, 1, :], ALU.mult)\
                   .then_inc(S("E_ready"), 1)
                dve.tensor_tensor(eb[:, :, 0, :], x[:, :, 0, :], blocks(kf[:, :, :], b)[:, :, 0, :], ALU.mult)\
                   .then_inc(S("E_ready"), 1)

            def level_out(n):
                if n > len(LEVELS):
                    dve.wait_ge(*W("cross_done", 1))
                    dve.tensor_copy(ATx[:, :, :].rearrange("p a b -> p (a b)"), ps[:, 4, :])\
                       .then_inc(S("cross_out"), 1)
                    return
                mask = C("levels")[:, n * P:(n + 1) * P].bitcast(U32)
                dve.wait_ge(*W("level_done", n + 1))
                if n == 0:
                    dve.wait_ge(*W("AT_zero", 1))
                else:
                    dve.wait_ge(*W("level_out", n))
                a = AT[:, :, :, :].rearrange("p h t c -> p (h t) c")
                dve.copy_predicated(a, mask.rearrange("p (a b) -> p a b", a=1).to_broadcast([P, HG * NT, P]),
                                    ps[:, 4:6, :].rearrange("p n (m c) -> p (n m) c", c=P)).then_inc(S("level_out"), 1)

            def scores(hd):
                dve.wait_ge(*W("relu_out", hd + 1))
                for qt in range(NT):
                    v = score[:, 0:1, :] if qt == 0 else score[:, 1:3, :]
                    r = relu[hd % 2][:, 0:1, :] if qt == 0 else relu[hd % 2][:, 1:3, :]
                    if hd:
                        dve.wait_ge(*W("score_acc", 2 * (hd - 1) + qt + 1))
                    dve.scalar_tensor_tensor(v, r, wi[:, qt, hd:hd + 1], v, ALU.mult, ALU.add)\
                       .then_inc(S("score_acc"), 1)

            def rivals(qt):
                return (score[:, 0:1, :] if qt == 0 else score[:, 1:3, :]).rearrange("p a b -> p (a b)")

            def best(qt, n=1):
                v = rivals(qt)
                for _ in range(n):
                    link(dve.max(top8[:, :], v))
                    link(dve.match_replace(v, top8[:, :], v, -3.0e38))

            def chosen(qt):
                v = rivals(qt)
                link(dve.tensor_scalar(v, v, -2.0e38, -1.0e30, ALU.is_gt, ALU.mult))
                d = score[:, 2 * qt, :]
                link(dve.tensor_tensor(d, d, C("causal"), ALU.add))

            exponents(1)
            for n in range(2):
                ahead(BASE["q_idx"] + n + 1 + RING)
            score_init(dve, S, score, C)
            for n in range(2):
                ahead(BASE["q_a"] + n + 1 + RING)
            decayed(1)
            exponents(2)
            level_out(0)
            dve.wait_ge(*W("score_init", 3))
            for n in range(2):
                for hd in range(4 * n, 4 * n + 4):
                    scores(hd)
                if n == 0:
                    ahead(BASE["i_h"] + n + 1 + RING)
            dve.wait_ge(*W("score_acc", 2 * HEADS))
            for n, (part, m) in enumerate(BETWEEN):
                if n + 2 <= len(LEVELS) + 1:
                    decayed(n + 2)
                if n + 3 <= len(LEVELS) + 1:
                    exponents(n + 3)
                level_out(n + 1)
                best(0)
                ahead(BASE[part] + m + RING)
            chosen(0)

            def wide(t):
                return on[:, t, 0:512].rearrange("p (a b) -> p a b", a=HG)

            for t in range(NT):
                dve.wait_ge(*W("osq_ready", t + 1))
                dve.tensor_reduce(st[:, 16 + 4 * t:20 + 4 * t], on[:, t, 512:1024].rearrange("p (a b) -> p a b", a=HG),
                                  AX.X, ALU.add).then_inc(S("ss_hg"), 1)
            best(1, 2)
            for t in range(NT):
                dve.wait_ge(*W("rstd_hg", t + 1))
                dve.wait_ge(*W("gh_out", t + 1))
                r = st[:, 16 + 4 * t:20 + 4 * t].rearrange("p (a b) -> p a b", b=1).to_broadcast([P, HG, P])
                dve.tensor_tensor(wide(t), ps[:, t, :].rearrange("p (a b) -> p a b", a=HG), r, ALU.mult)\
                   .then_inc(S("on_ready"), 1)
                dve.wait_ge(*W("on_ready", 2 * t + 1))
                dve.tensor_tensor(on[:, t, 0:512], on[:, t, 0:512], sgh[:, t, :], ALU.mult)\
                   .then_inc(S("on_ready"), 1)
            ahead(BASE["gate_a"] + 2 + RING)
            best(1, 3)
            ahead(BASE["gate_a"] + 3 + RING)
            for t in range(NT):
                dve.wait_ge(*W("ybh_ready", t + 1))
                v = slice(t * P, (t + 1) * P)
                dve.scalar_tensor_tensor(ybl[:, :, v], ps[:, 6 + t, :].rearrange("p (a b) -> p a b", a=4),
                                         M("hg_norm"), f32(ybh[:, :, v]), ALU.mult, ALU.subtract)\
                   .then_inc(S("yb_ready"), 1)
            best(1, 3)
            chosen(1)
            for qt in range(NT):
                nk = (qt + 1) * P
                sel = rivals(qt).rearrange("p (a b) -> p a b", a=1).to_broadcast([P, 2, nk])
                for n in range(HEADS // 2):
                    dve.wait_ge(*W("lg_done", 4 * qt + n + 1))
                    src = ps[:, 4 + n, :].rearrange("p (a b) -> p a b", a=2)[:, :, 0:nk]
                    dve.tensor_tensor(lg[qt][:, 2 * n:2 * n + 2, 0:nk], src, sel, ALU.add).then_inc(S("lg_out"), 1)
                dve.wait_ge(*W("lg_out", 4 * (qt + 1)))
                dve.tensor_reduce(st[:, MAXIMA[qt]:MAXIMA[qt] + 8], lg[qt][:, :, 0:nk], AX.X, ALU.max, negate=True)\
                   .then_inc(S("max_ready"), 1)
                if qt == 0:
                    ahead(BASE["gate_a"] + 4 + RING)
                for t in range(NT):
                    through("br_b", qt + 1)
                    c = slice(qt * 512, (qt + 1) * 512)
                    if qt == 0 and t == 0:
                        dve.wait_ge(*W("gate_b_out", 4))
                        dve.wait_ge(*W("ybT_done", 2))
                    dve.tensor_tensor(hn_m[:, t, c], ps[:, 2 * qt + t, :], gates[:, t, c], ALU.mult)\
                       .then_inc(S("mb_out"), 1)
                dve.wait_ge(*W("exp_ready", 8 * (qt + 1)))
                total = st[:, TOTALS[qt]:TOTALS[qt] + 8]
                link(dve.reciprocal(total, total))
                r = total.rearrange("p (a b) -> p a b", b=1).to_broadcast([P, HEADS, nk])
                dve.tensor_tensor(lg[qt][:, :, 0:nk], lg[qt][:, :, 0:nk], r, ALU.mult).then_inc(S("probs_ready"), 1)
                ahead(BASE["br_b"] + qt + 1 + RING)
            for qt in range(NT):
                dve.wait_ge(*W("yah_ready", qt + 1))
                q = slice(qt * P, (qt + 1) * P)
                dve.tensor_tensor(yal[:, :, q], ps[:, 4, :].rearrange("p (a b) -> p a b", a=4), f32(yah[:, :, q]),
                                  ALU.subtract).then_inc(S("ya_ready"), 1)
            ahead(BASE["br_a"] + 1 + RING)
            for j in range(2):
                for t in range(NT):
                    through("br_a", j + 1)
                    dve.wait_ge(*W("gate_a_out", 4))
                    c = slice(j * 512, (j + 1) * 512)
                    n = 2 * (2 * j + t)
                    dve.tensor_tensor(gates_a[j][:, t, :], ps[:, 2 * j + t, :], gates_a[j][:, t, :], ALU.mult)\
                       .then_inc(S("ma_out"), 1)
                    dve.wait_ge(*W("ma_out", n + 1))
                    dve.tensor_tensor(hn_m[:, t, c], hn_m[:, t, c], gates_a[j][:, t, :], ALU.add)\
                       .then_inc(S("ma_out"), 1)
                ahead(BASE["br_a"] + j + 1 + RING)
            turned("m1", None)
            ahead(BASE["w_out"] + 1 + RING)
            ahead(BASE["w_out"] + 4 + RING)
            scr[0] = hn_f
            post_norm("p1", "n2", acc, 32)
            normed("n2", hn_f)
            turned("n2", "g_ffn2")
            ffn(2)
            post_norm("p2", "n3", acc, 48)
            normed("n3", hn_f)
            turned("n3", "g_ple")
            dve.wait_ge(*W("pTh_ready", 1))
            dve.tensor_tensor(pTl[:, :, :], praw[:, :, :], f32(pTh[:, :, :]), ALU.subtract).then_inc(S("pT_split"), 1)
            ahead(BASE["ple_gate"] + 4 + RING)
            through("ple_proj", 1)
            dve.wait_ge(*W("pg_out", 2))
            for t in range(NT):
                dve.tensor_tensor(pgate[:, t, :], pgate[:, t, :],
                                  ps[:, 2 * t:2 * t + 2, :].rearrange("p a b -> p (a b)"), ALU.mult)\
                   .then_inc(S("pm_out"), 1)
            ahead(BASE["ple_proj"] + 1 + RING)
            dve.wait_ge(*W("pm_out", 2))
            post_norm("p3", "n4", lambda t: pgate[:, t, :], 64)
            normed("n4", hn_s)
            turned("n4", "g_mix2")

            w3 = M("sconv_w")
            for n in range(4):
                ahead(BASE["s_c"] + n + 1 + RING)
            def short_conv(n):
                for f in (2 * n, 2 * n + 1):
                    dve.wait_ge(*W("cv_first", f + 1))
                    for s in (1, 2):
                        link(dve.scalar_tensor_tensor(cv[:, f, s:T], cx[:, f, 0:T - s],
                                                      w3[:, 3 * f + 2 - s:3 * f + 3 - s], cv[:, f, s:T],
                                                      ALU.mult, ALU.add))

            for n in range(4):
                f = slice(2 * n, 2 * n + 2)
                through("s_x", n + 1)
                dve.wait_ge(*W("s_c_out", n + 1))
                dve.tensor_tensor(cx[:, f, :], cx[:, f, :], ps[:, 4 + n, :].rearrange("p (a b) -> p a b", a=2),
                                  ALU.mult).then_inc(S("s_x_out"), 1)
                if n:
                    short_conv(n - 1)
                ahead(BASE["s_x"] + n + 1 + RING)
            short_conv(3)
            for n in range(4):
                f = slice(2 * n, 2 * n + 2)
                through("s_b", n + 1)
                dve.tensor_tensor(cx[:, f, :], cv[:, f, :], ps[:, 4 + n, :].rearrange("p (a b) -> p a b", a=2),
                                  ALU.mult).then_inc(S("s_b_out"), 1)
                dve.wait_ge(*W("svh_ready", n + 1))
                dve.tensor_tensor(svl[:, f, :], cx[:, f, :], f32(svh[:, f, :]), ALU.subtract)\
                   .then_inc(S("sv_ready"), 2)
                ahead(BASE["s_b"] + n + 1 + RING)
            ahead(BASE["g_b"] + 4 + RING)
            for j in range(2):
                for t in range(NT):
                    c = slice(j * 512, (j + 1) * 512)
                    dve.wait_ge(*W("gb_out", 2 * j + t + 1))
                    through("sconv_proj", 2 * (j + 1))
                    if j == 0 and t == 0:
                        dve.wait_ge(*W("nT_n4", 4))
                    dve.tensor_tensor(merged[:, t, c], ps[:, 4 + 2 * t + j, :], sga[:, t, c], ALU.mult)\
                       .then_inc(S("mgb_out"), 1)
                ahead(BASE["sconv_proj"] + 2 * j + 2 + RING)
            through("dt", 1)
            x, dt_, dtA, e, z, z2, p_ = (dts[:, i, :, :] for i in (2, 0, 1, 3, 4, 5, 6))
            bb = M("dt_bias").rearrange("p (a b) -> p a b", a=1).to_broadcast([P, NT, SSD_HEADS])
            dve.tensor_tensor(x, ps[:, 0, 0:NT * SSD_HEADS].rearrange("p (a b) -> p a b", a=NT), bb, ALU.add)\
               .then_inc(S("dt_out"), 1)
            dve.wait_ge(*W("dt_out", 1))
            dve.scalar_tensor_tensor(e, x, -1.0, x, ALU.mult, ALU.max).then_inc(S("sp_abs"), 1)
            dve.wait_ge(*W("sp_exp", 1))
            link(dve.tensor_scalar(z, e, 2.0, None, ALU.add))
            link(dve.reciprocal(z, z))
            link(dve.tensor_tensor(z, z, e, ALU.mult))
            link(dve.tensor_tensor(z2, z, z, ALU.mult))
            link(dve.tensor_scalar(p_, z2, 1.0 / 15, None, ALU.mult))
            for d in (13, 11, 9, 7, 5, 3):
                link(dve.scalar_tensor_tensor(p_, p_, 1.0 / d, z2, ALU.add, ALU.mult))
            link(dve.scalar_tensor_tensor(p_, p_, 1.0, z, ALU.add, ALU.mult))
            link(dve.tensor_scalar(x, x, 0.0, None, ALU.max))
            link(dve.scalar_tensor_tensor(dt_, p_, 2.0, x, ALU.mult, ALU.add))
            dve.wait_ge(*W("alog_exp", 1))
            al = M("a_log").rearrange("p (a b) -> p a b", a=1).to_broadcast([P, NT, SSD_HEADS])
            dve.scalar_tensor_tensor(dtA, dt_, -1.0, al, ALU.mult, ALU.mult).then_inc(S("dtA_ready"), 1)
            ahead(BASE["dt"] + 1 + RING)
            cw = M("conv_w")

            def times_dt(n):
                q, t = n // 2, n % 2
                dve.wait_ge(*W("xT_done", n + 1))
                d = dts[:, 0, t, 8 * q:8 * q + 8].rearrange("p (a b) -> p a b", b=1).to_broadcast([P, 8, SSD_HD])
                dve.tensor_tensor(xdt[:, t, 8 * q:8 * q + 8, :],
                                  ps[:, 2 + n % 2, :].rearrange("p (a b) -> p a b", a=8), d, ALU.mult)\
                   .then_inc(S("xdt_out"), 1)

            for n in range(12):
                for r in range(2):
                    f = 2 * n + r
                    if r == 0:
                        dve.wait_ge(*W("cvt_first", f + 2))
                    v = cvt[:, n % 2, r, :]
                    for s in (1, 2, 3):
                        ins = dve.scalar_tensor_tensor(v[:, s:T], ps[:, 4 + n % 4, r * T:(r + 1) * T - s],
                                                       cw[:, 4 * f + 3 - s:4 * f + 4 - s], v[:, s:T],
                                                       ALU.mult, ALU.add)
                        if s < 3:
                            link(ins)
                        else:
                            ins.then_inc(S("conv_out"), 1)
                if n == 4:
                    dve.wait_ge(*W("ac_done", 1))
                    ac = dts[:, 7, :, :]
                    link(dve.tensor_copy(ac, ps[:, 1, 0:64].rearrange("p (a b) -> p a b", a=NT)))
                    dve.tensor_tensor(dts[:, 8, 0, :], ps[:, 1, 64:96], ac[:, 0, :], ALU.subtract)\
                       .then_inc(S("kd_sub"), 1)
                if n >= 5:
                    times_dt(n - 5)
                ahead(BASE["xbc"] + n + 1 + RING)
            times_dt(7)
            tri = C("tri")
            for g in range(GROUPS):
                dve.wait_ge(*W("cb_done", g + 1))
                b = 6 + g % 2
                dve.tensor_tensor(cbm[:, g, 0, :], ps[:, b, 0:P], tri, ALU.mult).then_inc(S("cb_out"), 1)
                dve.tensor_copy(cbm[:, g, 1, :], ps[:, b, P:2 * P]).then_inc(S("cb_out"), 1)
                dve.tensor_tensor(cbm[:, g, 2, :], ps[:, b, 2 * P:3 * P], tri, ALU.mult).then_inc(S("cb_out"), 1)
            dve.wait_ge(*W("xdt_out", 8))
            dve.wait_ge(*W("kd_exp", 1))
            d = dts[:, 8, 0, :].rearrange("p (a b) -> p a b", b=1).to_broadcast([P, SSD_HEADS, SSD_HD])
            dve.tensor_tensor(xw[:, :, :], xdt[:, 0, :, :], d, ALU.mult).then_inc(S("xw_ready"), 1)
            ds = M("d_skip")

            def gated(n):
                dve.wait_ge(*W("zs_ready", n + 1))
                dve.wait_ge(*W("y_out", 2 * n + 2))
                v = xs[:, 2 * n:2 * n + 2, :]
                dve.tensor_tensor(v, v, zs[:, :, :], ALU.mult).then_inc(S("z_out"), 1)

            for q in range(8):
                dve.wait_ge(*W("bc_done", q + 1))
                if q:
                    dve.wait_ge(*W("y_done", q))
                dve.wait_ge(*W("cross_exp", 2 * (q + 1)))
                for r in range(4):
                    for t in range(NT):
                        c = ((r % 2) * NT + t) * P
                        hd = 4 * q + r
                        dve.tensor_scalar(seg[:, r, 2 * t, :], ps[:, 4 + r // 2, c:c + P], ac[:, t, hd:hd + 1], 0.0,
                                          ALU.subtract, ALU.min).then_inc(S("seg_sub"), 1)
                if q:
                    y_out(dve, S, xs, ps, ds, q - 1)
                    gated(q - 1)
                dve.wait_ge(*W("seg_exp", 2 * (q + 1)))
                m = cbm[:, q // 2:q // 2 + 1, :, :].rearrange("p a b c -> p a (b c)").to_broadcast([P, 4, 3 * P])
                sv = seg[:, :, :, :].rearrange("p a b c -> p a (b c)")
                dve.tensor_tensor(sv, sv, m, ALU.mult).then_inc(S("sc_ready"), 1)
                ahead(BASE["z"] + q + RING)
            dve.wait_ge(*W("y_done", 8))
            y_out(dve, S, xs, ps, ds, 7)
            gated(7)
            ahead(BASE["z"] + 8 + RING)
            dve.wait_ge(*W("ssg_done", GROUPS))
            dve.tensor_copy(st[:, 24:32], ps[:, 3, 0:8]).then_inc(S("ss_ssd"), 1)
            ahead(BASE["g_a"] + 2 + RING)
            dve.wait_ge(*W("rb_done", 1))
            nw = M("ssd_norm")

            def low_halves(g):
                for f in range(GT * g, GT * g + GT):
                    dve.wait_ge(*W("yhi_ssd", f + 1))
                    dve.scalar_tensor_tensor(ylo[:, f, :], xs[:, f, :], nw[:, f:f + 1], f32(yhi[:, f, :]),
                                             ALU.mult, ALU.subtract).then_inc(S("ylo_ssd"), 1)

            for g in range(GROUPS):
                v = xs[:, GT * g:GT * g + GT, :]
                r = ps[:, 6 + g // 2:7 + g // 2, (g % 2) * T:(g % 2 + 1) * T].to_broadcast([P, GT, T])
                dve.tensor_tensor(v, v, r, ALU.mult).then_inc(S("yn_out"), 1)
                if g:
                    low_halves(g - 1)
                if g == 2:
                    ahead(BASE["g_a"] + 3 + RING)
            low_halves(GROUPS - 1)
            ahead(BASE["ssd_proj"] + 8 + RING)
            for j in range(2):
                for t in range(NT):
                    c = slice(j * 512, (j + 1) * 512)
                    n = 2 * (2 * j + t)
                    dve.wait_ge(*W("ga_out", 4))
                    through("ssd_proj", 4 * (j + 1))
                    dve.tensor_tensor(sga[:, t, c], ps[:, 4 + 2 * t + j, :], sga[:, t, c], ALU.mult)\
                       .then_inc(S("mga_out"), 1)
                    dve.wait_ge(*W("mga_out", n + 1))
                    dve.tensor_tensor(merged[:, t, c], merged[:, t, c], sga[:, t, c], ALU.add)\
                       .then_inc(S("mga_out"), 1)
            turned("m2", None)
            ahead(BASE["w_o"] + 4 + RING)
            through("w_o", 4)
            for t in range(NT):
                dve.tensor_tensor(h[:, t, :], h[:, t, :], acc(t), ALU.add).then_inc(S("h_n5"), 1)
            scr[0] = hn_f
            normed("n5", hn_f)
            turned("n5", "g_ffn3")
            ffn(3)
            through("ffn3", FFN_UNITS)
            for t in range(NT):
                dve.tensor_tensor(h[:, t, :], h[:, t, :], acc(t), ALU.add).then_inc(S("h_n6"), 1)
            dve.wait_ge(*W("rstd_n6", 1))
            dve.wait_ge(*W("post_loaded", 80))
            for t in range(NT):
                dve.scalar_tensor_tensor(hn_f[:, t, :], h[:, t, :], st[:, t:t + 1], post[:, :], ALU.mult, ALU.mult)\
                   .then_inc(S("final_ready"), 1)


def score_init(dve, S, score, C):
    for n in (0, 2):
        dve.tensor_copy(score[:, n, :], C("causal")).then_inc(S("score_init"), 1)
    dve.memset(score[:, 1, :], 0.0).then_inc(S("score_init"), 1)


def y_out(dve, S, xs, ps, ds, q):
    for r in range(2):
        f = 2 * q + r
        dve.scalar_tensor_tensor(xs[:, f, :], xs[:, f, :], ds[:, f:f + 1], ps[:, 6 + q % 2, r * T:(r + 1) * T],
                                 ALU.mult, ALU.add).then_inc(S("y_out"), 1)


def by_rows(w, n):
    k = w.shape[0] // 512
    a = w.reshape(k, 4, P, n, 512).transpose(3, 0, 2, 1, 4)
    return a.reshape(n * k, P, UNIT)


def by_features(w):
    n = w.shape[1] // 256
    return w.reshape(KD, P, n, 256).transpose(2, 1, 0, 3).reshape(n, P, UNIT)


def feed_forward(gate, up, down):
    g = gate.reshape(2, 4, P, NCH, FCH).transpose(3, 0, 2, 1, 4)
    u = up.reshape(2, 4, P, NCH, FCH).transpose(3, 0, 2, 1, 4)
    gu = np.concatenate([g, u], axis=-1).reshape(NCH, 2, P, UNIT)
    dn = down.reshape(NCH, 2, P, D).transpose(0, 2, 1, 3).reshape(NCH, P, UNIT)
    out = [gu[0, 0], gu[0, 1]]
    for c in range(1, NCH):
        out += [gu[c, 0], gu[c, 1], dn[c - 1]]
    return np.stack(out + [dn[NCH - 1]])


def padded(w, cols):
    a = w.reshape(KD, P, w.shape[1]).transpose(1, 0, 2)
    a = np.concatenate([a, np.zeros((P, KD, cols - a.shape[2]), np.float32)], axis=2).reshape(P, KD * cols)
    return np.concatenate([a, np.zeros((P, UNIT - KD * cols), np.float32)], axis=1)[None]


def weight_stream(i):
    w, w2 = i["w_in"][0], i["w_in_2"][0]
    cuts = np.cumsum([0, 512, 128, 512, 64, 8, 512, 512, 512, 512, 1024, 1024])
    c = dict(zip(("q_a", "kv", "q_idx", "ki", "wi", "q_h", "f_h", "i_h", "g_h", "gate_a", "gate_b"),
                 (w[:, a:b] for a, b in zip(cuts[:-1], cuts[1:]))))
    cuts = np.cumsum([0, 2048, 3072, 32, 1024, 1024, 1024, 1024, 1024])
    d = dict(zip(("z", "xbc", "dt", "s_b", "s_c", "s_x", "g_a", "g_b"),
                 (w2[:, a:b] for a, b in zip(cuts[:-1], cuts[1:]))))
    pp = i["w_ple_proj"][0].reshape(2, P, D).transpose(1, 0, 2).reshape(1, P, UNIT)
    parts = {
        "ffn1": feed_forward(i["ffn1_w_gate"][0], i["ffn1_w_up"][0], i["ffn1_w_down"][0]),
        "kv": padded(np.concatenate([c["kv"], c["ki"], c["wi"]], axis=1), 256),
        "q_idx": by_features(c["q_idx"]), "q_a": by_features(c["q_a"]),
        "f_h": by_features(c["f_h"]), "q_h": by_features(c["q_h"]),
        "i_h": by_rows(c["i_h"], 1), "g_h": by_rows(c["g_h"], 1),
        "gate_b": by_rows(c["gate_b"], 2), "br_b": by_rows(i["w_br_b"][0], 2),
        "gate_a": by_rows(c["gate_a"], 2), "br_a": by_rows(i["w_br_a"][0], 2),
        "w_out": by_rows(i["w_out"][0], 2),
        "ffn2": feed_forward(i["ffn2_w_gate"][0], i["ffn2_w_up"][0], i["ffn2_w_down"][0]),
        "ple_gate": by_rows(i["w_ple_gate"][0], 2), "ple_proj": pp,
        "s_c": by_features(d["s_c"]), "s_x": by_features(d["s_x"]), "s_b": by_features(d["s_b"]),
        "sconv_proj": by_rows(i["w_sconv_proj_2"][0], 2), "g_b": by_rows(d["g_b"], 2),
        "xbc": by_features(d["xbc"]), "dt": padded(d["dt"], 32), "z": by_features(d["z"]),
        "g_a": by_rows(d["g_a"], 2), "ssd_proj": by_rows(i["w_ssd_proj_2"][0], 2),
        "w_o": by_rows(i["w_o_2"][0], 2),
        "ffn3": feed_forward(i["w_gate_2"][0], i["w_up_2"][0], i["w_down_2"][0]),
    }
    for name, n in PARTS:
        assert parts[name].shape[0] == n, name
    return np.concatenate([parts[name] for name, _ in PARTS])


def small_parameters(i):
    def tiles(v):
        return v.reshape(-1, P).T

    def all_rows(v):
        return np.broadcast_to(v.reshape(1, -1), (P, v.size))

    conv = i["ssd_conv_w_2"][0].T.reshape(24, P, CONV_K).transpose(1, 0, 2).reshape(P, -1)
    sconv = i["sconv_w_2"][0].T.reshape(KD, P, SCONV_K).transpose(1, 0, 2).reshape(P, -1)
    uk = i["w_uk"][0].transpose(0, 2, 1).reshape(PAIRS, 2 * HEAD_DIM, LATENT).transpose(1, 0, 2).reshape(P, -1)
    uv = i["w_uv"][0].transpose(1, 0, 2).reshape(P, -1)
    rel = np.concatenate([i["rel_bias"], np.zeros((P - BUCKETS, HEADS), np.float32)])
    parts = {
        "g_ffn1": tiles(i["ffn1_pre_g"][0]), "g_mix": tiles(i["mix_pre_g"][0]), "g_ffn2": tiles(i["ffn2_pre_g"][0]),
        "g_ple": tiles(i["ple_pre_g"][0]), "g_mix2": tiles(i["norm_mix_w_2"][0]), "g_ffn3": tiles(i["norm_ffn_w_2"][0]),
        "ssd_norm": tiles(i["ssd_norm_w_2"][0]), "conv_w": conv, "conv_b": tiles(i["ssd_conv_b_2"][0]),
        "sconv_w": sconv, "d_skip": tiles(np.repeat(i["d_skip_2"][0], SSD_HD)),
        "hg_lb": i["hgrn_lb"].reshape(2, HG, P).transpose(2, 0, 1).reshape(P, 2 * HG),
        "hg_norm": i["hgrn_norm_g"][0].reshape(P, 1), "dt_bias": all_rows(i["dt_bias_2"][0]),
        "a_log": all_rows(i["a_log_2"][0]), "kv_g": all_rows(i["kv_norm_g"][0]), "ki_g": all_rows(i["kidx_norm_g"][0]),
        "w_uk": uk, "w_uv": uv, "rel": rel,
    }
    return np.ascontiguousarray(np.concatenate([parts[name] for name, _ in SMALL], axis=1), dtype=np.float32)


def shape_constants():
    s, t = np.arange(P)[:, None], np.arange(P)[None, :]
    levels = [s == t]
    for b in LEVELS:
        levels.append((s // (2 * b) == t // (2 * b)) & ((s // b) % 2 == 0) & ((t // b) % 2 == 1))
    dist = np.maximum(T - 1 - np.arange(NREL), 0)
    exact = BUCKETS // 2
    log_b = exact + (np.log(np.maximum(dist, 1).astype(np.float32) / exact) / math.log(MAX_DIST / exact)
                     * (BUCKETS - exact)).astype(np.int32)
    bucket = np.where(dist < exact, dist, np.minimum(log_b, BUCKETS - 1))
    parts = {
        "ident": s == t, "tri": s <= t, "ones": np.ones((P, P)),
        "causal": np.where(t <= s, 0.0, -1.0e38),
        "reset": np.broadcast_to((np.arange(T) % CHUNK != 0)[None, :], (P, T)),
        "flip": s + t == P - 1,
        "levels": np.concatenate(levels, axis=1),
        "onehot": np.arange(P)[:, None] == bucket[None, :],
    }
    return np.ascontiguousarray(np.concatenate([parts[name] for name, _ in CONSTS], axis=1), dtype=np.float32)


def kernel(**inputs):
    import concourse.bacc as bacc
    from concourse.bass_utils import run_bass_kernel_spmd

    i = {k: np.asarray(v) for k, v in inputs.items()}
    posts = np.stack([i["ffn1_post_g"][0], i["mix_post_g"][0], i["ffn2_post_g"][0], i["ple_post_g"][0],
                      i["final_norm_w_2"]])
    arrays = {
        "stream": weight_stream(i), "small": small_parameters(i), "consts": shape_constants(),
        "bgate": np.ascontiguousarray(i["b_gate"][0].reshape(4, 512)), "posts": posts,
        "x": np.ascontiguousarray(i["x"][0]), "p_turned": np.ascontiguousarray(i["p"][0, 0].T),
    }
    nc = bacc.Bacc("TRN2", target_bir_lowering=False, num_devices=1)
    aps = [nc.dram_tensor(n, a.shape, F32, kind="ExternalInput").ap() for n, a in arrays.items()]
    out = nc.dram_tensor("out", (T, D), F32, kind="ExternalOutput").ap()
    build(nc, *aps, out)
    r = run_bass_kernel_spmd(nc, [arrays], core_ids=[0])
    return r.results[0]["out"].reshape(1, T, D)
```

```python
from contextlib import ExitStack
import math

import numpy as np

import concourse.bass as bass
from concourse import mybir

F32 = mybir.dt.float32
F32R = mybir.dt.float32r
U32 = mybir.dt.uint32
ALU = mybir.AluOpType
ACT = mybir.ActivationFunctionType
AX = mybir.AxisListType

P = 128
T = 256
NT = T // P
D = 1024
KD = D // P
D_FF = 2816
EPS = 1e-6
PLE_DIM = 256
HEADS, HEAD_DIM, LATENT = 8, 64, 128
PAIRS = HEADS // 2
TOPK = 64
ATT_SCALE = HEAD_DIM ** -0.5
IDX_W_SCALE = (HEADS ** -0.5) * (HEAD_DIM ** -0.5)
BUCKETS, MAX_DIST = 32, 128
HG = 4
HGD = 128
CHUNK = 64
SSD_HEADS, SSD_HD, GROUPS = 32, 64, 4
HPG = SSD_HEADS // GROUPS
XT = SSD_HEADS * SSD_HD // P
GT = XT // GROUPS
CONV_K, SCONV_K = 4, 3

UNIT = 2048
DT_UNIT = KD * 32
RING = 3
FCH = 256
NCH = D_FF // FCH
FFN_UNITS = 3 * NCH
KV_COLS = LATENT + HEAD_DIM + HEADS

PARTS = [
    ("ffn1", FFN_UNITS), ("f_h", 2), ("q_h", 2), ("kv", 1), ("q_idx", 2), ("q_a", 2), ("i_h", 2), ("g_h", 2),
    ("gate_b", 4), ("gate_a", 4), ("br_b", 2), ("br_a", 2), ("w_out", 4), ("ffn2", FFN_UNITS),
    ("ple_proj", 1), ("ple_gate", 4), ("s_c", 4), ("s_x", 4), ("s_b", 4), ("dt", 1), ("g_b", 4), ("sconv_proj", 4),
    ("xbc", 12), ("z_first", 1), ("g_a0", 2), ("z", 7), ("g_a1", 2), ("ssd_proj", 8), ("w_o", 4), ("ffn3", FFN_UNITS),
]
BASE = {}
N_UNITS = 0
for _name, _n in PARTS:
    BASE[_name] = N_UNITS
    N_UNITS += _n
Z_UNITS = [BASE["z_first"]] + [BASE["z"] + n for n in range(7)]
Z_BANKS = [0, 0, 1, 2, 0, 1, 2, 0]
BETWEEN = [(part, n) for part, count in (("g_h", 2), ("gate_b", 4), ("gate_a", 2)) for n in range(count)]

SMALL = [
    ("g_ffn1", 8), ("g_mix", 8), ("g_ffn2", 8), ("g_ple", 8), ("g_mix2", 8), ("g_ffn3", 8),
    ("ssd_norm", XT), ("conv_w", 24 * CONV_K), ("conv_b", 24), ("sconv_w", KD * SCONV_K), ("d_skip", XT),
    ("hg_lb", 2 * HG), ("hg_norm", 1), ("dt_bias", SSD_HEADS), ("a_log", SSD_HEADS),
    ("kv_g", LATENT), ("ki_g", HEAD_DIM), ("w_uk", PAIRS * LATENT), ("w_uv", HEADS * HEAD_DIM),
    ("rel", HEADS),
]
MAXIMA = [48, 56]
TOTALS = [32, 24]
GAINS = 48
NET_NORM = {1: "n0", 2: "n2", 3: "n5"}
LEVELS = [1, 2, 4, 8, 16, 32, 64]
NREL = 384
CONSTS = [("ident", P), ("tri", P), ("ones", P), ("causal", P), ("reset", T), ("flip", P), ("levels", (len(LEVELS) + 1) * P),
          ("onehot", NREL)]


def columns(table):
    at, out = 0, {}
    for name, n in table:
        out[name] = (at, at + n)
        at += n
    return out, at



def in_series():
    out = {}

    def add(name, members):
        before = 0
        for m, n in members:
            out[f"{name}{m}"] = (f"{name}s", before)
            before += n

    turned = ["_n0", "_n1", "_m1", "_n2", "_n3", "_n4", "_m2", "_n5"]
    add("nT", [(m, 4) for m in turned])
    add("yhi", [(m, KD) for m in turned])
    add("ylo", [(m, KD) for m in turned])
    add("hn", [("_n1", NT), ("_n4", NT)])
    add("h", [("_n1", NT), ("_n2", 2 * NT), ("_n3", 2 * NT), ("_n4", NT), ("_n5", 2 * NT), ("_n6", NT)])
    roots = ["_n0", "_p0", "_n1", "_p1", "_n2", "_p2", "_n3", "_p3", "_n4", "_n5", "_n6"]
    add("ss", [(m, NT) for m in roots])
    add("rstd", [(m, NT) for m in roots])
    add("t0", [("_ffn1", 1), ("_w_out", 1), ("_ffn2", 1), ("_ple_gate", 1), ("_ffn3", 1)])
    for f in (1, 2, 3):
        for name, n in (("tr_done", NCH), ("prod_ready", 2 * NCH), ("hT_ready", NCH), ("sil_ready", 2 * NCH),
                        ("hTh_ready", NCH)):
            out[f"{name}{f}"] = (name, n * (f - 1))
    return out


SERIES = in_series()
SMALL_AT, N_SMALL = columns(SMALL)
CONST_AT, N_CONST = columns(CONSTS)


def build(nc, stream, small, consts, bgate, posts, xin, pin, out):
    ctx = ExitStack()
    with ctx:
        sems = {}
        series = SERIES

        def S(name):
            name = series.get(name, (name, 0))[0]
            if name not in sems:
                sems[name] = ctx.enter_context(nc.semaphore(name))
            return sems[name]

        def W(name, n):
            return S(name), n + series.get(name, (name, 0))[1]

        def sb(name, shape, dt=F32):
            return ctx.enter_context(nc.sbuf_tensor(name, shape, dt))

        raw = [sb(f"raw{i}", [P, UNIT]) for i in range(RING)]
        whi = [sb(f"whi{i}", [P, UNIT], F32R) for i in range(RING)]
        wlo = [sb(f"wlo{i}", [P, UNIT], F32R) for i in range(RING)]
        h = sb("h", [P, NT, D])
        yTh = sb("yTh", [P, KD, T], F32R)
        yTl = sb("yTl", [P, KD, T], F32R)
        post = sb("post", [P, D])
        sm = sb("sm", [P, N_SMALL])
        cn = sb("cn", [P, N_CONST])
        bg = sb("bg", [4, 512])
        st = sb("st", [P, 64])
        half = sb("half", [P, 8])
        identr = sb("identr", [P, P], F32R)
        ps = ctx.enter_context(nc.psum_tensor("ps", [P, 8, 512], F32))

        def C(name):
            a, b = CONST_AT[name]
            return cn[:, a:b]

        def M(name):
            a, b = SMALL_AT[name]
            return sm[:, a:b]

        ident = C("ident")

        base = (nc.sbuf_base + 63) // 64 * 64
        room = nc.sbuf_usable_end - base - 64 if nc.sbuf_usable_end < nc.sbuf_top else nc.sbuf_top - base - 64
        top = {}

        def at(phase, name, shape, dt=F32, over=None):
            size = 4 * int(np.prod(shape[1:]))
            off = top.get(phase, 0) if over is None else over
            if over is None:
                top[phase] = off + size
                assert off + size <= room, (phase, name, off + size, room)
            t = nc.alloc_sbuf_tensor_at(f"{phase}_{name}", shape, dt, offset=base + off)
            return t

        def here(phase):
            return top.get(phase, 0)

        def scratch(phase):
            return at(phase, "hn", [P, NT, D])

        hn_f = scratch("f")
        sil = at("f", "sil", [P, NT, FCH])
        prod = at("f", "prod", [P, NT, FCH])
        hTh = at("f", "hTh", [P, 2, T], F32R)
        hTl = at("f", "hTl", [P, 2, T], F32R)
        hTh_last = at("f", "hTh_last", [P, 2, T], F32R)
        hTl_last = at("f", "hTl_last", [P, 2, T], F32R)
        pgate = at("f", "pgate", [P, NT, D])
        squares = at("f", "squares", [P, NT, D])
        praw = at("f", "praw", [P, 2, T])
        pTh = at("f", "pTh", [P, 2, T], F32R)
        pTl = at("f", "pTl", [P, 2, T], F32R)

        hn_m = scratch("m")
        qiT = at("m", "qiT", [P, PAIRS, T])
        olat = nc.alloc_sbuf_tensor_at("m_olat", [P, HEADS, P], F32, offset=base + here("m") - 4096)
        qa_at = here("m")
        qaT = at("m", "qaT", [P, PAIRS, T])
        kvT = at("m", "kvT", [P, 2, T])
        ckvn = at("m", "ckvn", [P, NT, P])
        kk2 = at("m", "kk2", [P, NT, P])
        wi = at("m", "wi", [P, NT, HEADS])
        vv = at("m", "vv", [P, NT, 512])
        sgh = at("m", "sgh", [P, NT, 512])
        ybh = at("m", "ybh", [P, 4, T], F32R)
        ybl = at("m", "ybl", [P, 4, T], F32R)
        ya_at = here("m")
        yah = at("m", "yah", [P, 4, T], F32R)
        yal = at("m", "yal", [P, 4, T], F32R)
        bgh = at("m", "bgh", [4, 512], F32R, over=ya_at)
        bgl = at("m", "bgl", [4, 512], F32R, over=ya_at + 4096)
        gates = at("m", "gates", [P, NT, D])
        gates_a = [vv, sgh]
        score = at("m", "score", [P, 3, P])
        rel8 = at("m", "rel8", [HEADS, NREL])
        top8 = at("m", "top8", [P, 8])
        r_at = here("m")
        at("m", "region", [P, 34 * 256])
        sg = at("m", "sg", [P, HG, T], over=r_at)
        kf = at("m", "kf", [P, HG, T], over=r_at + 4096)
        qh = at("m", "qh", [P, HG, T], over=r_at + 2 * 4096)
        G = at("m", "G", [P, HG, T], over=r_at + 3 * 4096)
        X = at("m", "X", [P, HG, T], over=r_at + 4 * 4096)
        E = [at("m", f"E{i}", [P, HG, T], over=r_at + (5 + i) * 4096) for i in range(2)]
        AT = at("m", "AT", [P, HG, NT, P], over=r_at + 7 * 4096)
        ATx = at("m", "ATx", [P, HG, P], over=r_at + 8 * 4096)
        on = hn_m
        bias = at("m", "bias", [P, HEADS, T], over=r_at)
        qlat = at("m", "qlat", [P, HEADS, T], over=r_at + 8192)
        lg = [nc.alloc_sbuf_tensor_at("m_lg0", [P, HEADS, P], F32, offset=base + qa_at),
              at("m", "lg1", [P, HEADS, T], over=r_at + 2 * 8192)]
        pT = at("m", "pT", [P, NT, HEADS, P], over=r_at + 3 * 8192)
        relu = [hn_m[:, 0, 0:384].rearrange("p (a b) -> p a b", a=3), hn_m[:, 0, 512:896].rearrange("p (a b) -> p a b", a=3)]

        hn_s = scratch("s")
        merged = hn_s
        xs = at("s", "xs", [P, XT, T])
        bc = at("s", "bc", [P, 2 * GROUPS, T])
        sga = at("s", "sga", [P, NT, D])
        cbm = at("s", "cbm", [P, GROUPS, 3, P])
        dts = at("s", "dts", [P, 16, NT, SSD_HEADS])
        dtT = at("s", "dtT", [SSD_HEADS, T])
        acTh = at("s", "acTh", [SSD_HEADS, T], F32R)
        acTl = at("s", "acTl", [SSD_HEADS, T], F32R)
        v_at = here("s")
        at("s", "region", [P, 36 * 256])
        xdt = at("s", "xdt", [P, NT, SSD_HEADS, SSD_HD], over=v_at)
        xw = at("s", "xw", [P, SSD_HEADS, SSD_HD], over=v_at + 16384)
        seg = at("s", "seg", [P, 4, 3, P], over=v_at + 24576)
        yhi = at("s", "yhi", [P, XT, T], F32R, over=v_at)
        ylo = at("s", "ylo", [P, XT, T], F32R, over=v_at + 16384)
        sq = at("s", "sq", [P, GT, T], over=v_at + 32768)
        cx = at("s", "cx", [P, KD, T], over=v_at)
        cv = at("s", "cv", [P, KD, T], over=v_at + 8192)
        svh = at("s", "svh", [P, KD, T], F32R, over=v_at + 16384)
        svl = at("s", "svl", [P, KD, T], F32R, over=v_at + 24576)
        cvt = at("s", "cvt", [P, 2, 2, T], over=v_at + 32768)
        zs = at("s", "zs", [P, 2, T], over=v_at + 30720)

        rscr = nc.dram_tensor("rel_scratch", (HEADS, NREL), F32).ap()

        block = ctx.enter_context(nc.Block())

        def f32(ap):
            return ap.bitcast(F32)

        @block.sync
        def _(sp):
            def unit(u, slot):
                sp.dma_start(raw[slot][:, :], stream[u, :, :]).then_inc(S(f"raw_loaded{slot}"), 16)

            sp.dma_start(raw[0][:, 0:UNIT // 2], stream[0, :, 0:UNIT // 2]).then_inc(S("raw_first"), 16)
            sp.dma_start(raw[0][:, UNIT // 2:UNIT], stream[0, :, UNIT // 2:UNIT]).then_inc(S("raw_loaded0"), 16)
            sp.dma_start(cn[:, 0:P], consts[:, 0:P]).then_inc(S("ident_loaded"), 16)
            x = xin.rearrange("(t p) d -> p t d", p=P)
            for j in range(2):
                c = slice(j * 512, (j + 1) * 512)
                sp.dma_start(h[:, :, c], x[:, :, c]).then_inc(S(f"x_loaded{j}"), 16)
                if j == 0:
                    sp.dma_start(sm[:, 0:GAINS], small[:, 0:GAINS]).then_inc(S("gains_loaded"), 16)
            unit(1, 1)
            unit(2, 2)
            sp.dma_start(sm[:, GAINS:N_SMALL], small[:, GAINS:N_SMALL]).then_inc(S("sm_loaded"), 16)
            sp.dma_start(cn[:, P:N_CONST], consts[:, P:N_CONST]).then_inc(S("cn_loaded"), 16)
            full = N_UNITS // RING
            with sp.Fori(1, full) as i:
                for s in range(RING):
                    sp.wait_ge(*W("lo_ready", i * RING + (s + 1 - RING)))
                    sp.dma_start(raw[s][:, :], stream[i * RING + s, :, :]).then_inc(S(f"raw_loaded{s}"), 16)
            for u in range(full * RING, N_UNITS):
                sp.wait_ge(*W("lo_ready", u + 1 - RING))
                unit(u, u % RING)
            for t in range(NT):
                sp.wait_ge(*W("final_ready", t + 1))
                sp.dma_start(out[t * P:(t + 1) * P, :], hn_f[:, t, :]).then_inc(S("out_written"), 16)
            sp.wait_ge(*W("out_written", 16 * NT))

        @block.gpsimd
        def _(pool):
            count = [0]

            def link(ins):
                count[0] += 1
                ins.then_inc(S("pool_chain"), 1)
                pool.wait_ge(*W("pool_chain", count[0]))

            link(pool.memset(half[:, :], -0.5))

            def load_post(n):
                pool.dma_start(post[:, :], posts[n:n + 1, :].to_broadcast([P, D])).then_inc(S("post_loaded"), 16)

            def root(name, a, b, width, scale=1.0):
                f = scale ** -2
                link(pool.tensor_scalar(st[:, a:b], st[:, a:b], f / width, f * EPS, ALU.mult, ALU.add))
                pool.tensor_tensor(st[:, a:b], st[:, a:b], half[:, 0:b - a], ALU.pow).then_inc(S(name), 1)

            def rstd(n, a, scale=1.0):
                for t in range(NT):
                    pool.wait_ge(*W(f"ss_{n}", t + 1))
                    root(f"rstd_{n}", a + t, a + t + 1, D, scale)

            rstd("n0", 0)
            load_post(0)
            pool.dma_start(bg[:, :], bgate).then_inc(S("bg_loaded"), 16)
            rstd("p0", 2, 0.5)
            rstd("n1", 0)
            load_post(1)
            pool.wait_ge(*W("ss_kv", 4))
            link(pool.tensor_scalar(st[:, 8:10], st[:, 8:10], 1.0 / LATENT, EPS, ALU.mult, ALU.add))
            link(pool.tensor_scalar(st[:, 10:12], st[:, 10:12], 1.0 / HEAD_DIM, EPS, ALU.mult, ALU.add))
            pool.tensor_tensor(st[:, 8:12], st[:, 8:12], half[:, 0:4], ALU.pow).then_inc(S("rstd_kv"), 1)
            pool.wait_ge(*W("rel_ready", 1))
            pool.dma_start(rscr, rel8[:, :]).then_inc(S("rel_written"), 16)
            pool.wait_ge(*W("rel_written", 16))
            pool.wait_ge(*W("hg_o", 2))
            src = rscr[:, 0:T]
            src = bass.AP(tensor=src.tensor, offset=src.offset, ap=[[1, P], [NREL, HEADS], [1, T]])
            pool.dma_start(bias[:, :, :], src).then_inc(S("bias_loaded"), 16)
            for t in range(NT):
                pool.wait_ge(*W("ss_hg", t + 1))
                root("rstd_hg", 16 + 4 * t, 20 + 4 * t, HGD)
            rstd("p1", 2)
            rstd("n2", 0)
            load_post(2)
            pool.dma_start(praw[:, :, :], pin.rearrange("(k p) t -> p k t", p=P)).then_inc(S("p_loaded"), 16)
            rstd("p2", 2, 0.5)
            rstd("n3", 0)
            load_post(3)
            rstd("p3", 2)
            rstd("n4", 0)
            load_post(4)
            for n, (a, b) in enumerate(((24, 30), (30, 32))):
                pool.wait_ge(*W("ss_ssd", n + 1))
                root("rstd_ssd", a, b, GT * P)
            rstd("n5", 0)
            rstd("n6", 0)

        @block.tensor
        def _(pe):
            drained = {}

            def take(banks, by):
                for b in banks:
                    for name, n in drained.get(b, []):
                        pe.wait_ge(*W(name, n))
                    drained[b] = by
                return banks

            def begin(u):
                pe.wait_ge(*W("lo_ready", u + 1))

            def three(o, a, b, start, stop, swap=False):
                (ah, al), (bh, bl) = a, b
                pe.matmul(o, ah, bh, start=start, stop=False)
                pe.matmul(o, ah, bl, start=False, stop=False)
                return pe.matmul(o, al, bh, start=False, stop=stop)

            def w(slot, a, b):
                return whi[slot][:, a:b], wlo[slot][:, a:b]

            def acts(hl, k, t=None):
                hi, lo = hl
                if t is None:
                    return hi[:, k, :], lo[:, k, :]
                return hi[:, k, t * P:(t + 1) * P], lo[:, k, t * P:(t + 1) * P]

            yT = (yTh, yTl)

            def row_unit(u0, n, nk, hl, banks, bias_row=None, early=None, between=None, ready=None):
                begin(u0 + n)
                s = (u0 + n) % RING
                for t in range(NT):
                    if t and early:
                        ins.then_inc(S(early), 1)
                    if t and between:
                        between()
                    o = ps[:, banks[t], :]
                    for k in range(4):
                        if ready and t == 0:
                            pe.wait_ge(*W(ready, 4 * n + k + 1))
                        last = n == nk - 1 and k == 3
                        ins = three(o, acts(hl, 4 * n + k, t), w(s, k * 512, (k + 1) * 512),
                                    n == 0 and k == 0, last and bias_row is None)
                    if n == nk - 1 and bias_row is not None:
                        one = identr[0:4, bias_row:bias_row + 1].to_broadcast([4, P])
                        pe.matmul(o, one, bgh[:, :], start=False, stop=False)
                        ins = pe.matmul(o, one, bgl[:, :], start=False, stop=True)
                ins.then_inc(S("unit_used"), 1)

            def rows(u0, nk, hl, banks):
                for n in range(nk):
                    row_unit(u0, n, nk, hl, banks)

            def features(u, bank, ready=None):
                begin(u)
                s = u % RING
                for j in range(2):
                    for k in range(KD):
                        if ready and j == 0:
                            pe.wait_ge(*W(ready, k + 1))
                        c = k * 256 + j * P
                        ins = three(ps[:, bank, j * T:(j + 1) * T], w(s, c, c + P), acts(yT, k), k == 0, k == KD - 1)
                ins.then_inc(S("unit_used"), 1)

            def turn_pair(j, bank, ready, src, name):
                take([bank], [(f"ylo_{name}", 2 * (j + 1))])
                if ready:
                    pe.wait_ge(*W(*ready))
                for f in range(2):
                    for t in range(NT):
                        c = (2 * j + f) * P
                        ins = pe.transpose(ps[:, bank, (f * NT + t) * P:(f * NT + t + 1) * P], src[:, t, c:c + P], ident)
                ins.then_inc(S(f"nT_{name}"), 1)

            def turn_full(src, name):
                for t in range(NT):
                    for j in range(4):
                        if t == 0:
                            take([j], [(f"ylo_{name}", 2 * (j + 1))])
                        if j == 0:
                            pe.wait_ge(*W(f"hn_{name}", t + 1))
                        for f in range(2):
                            c = (2 * j + f) * P
                            ins = pe.transpose(ps[:, j, (f * NT + t) * P:(f * NT + t + 1) * P], src[:, t, c:c + P],
                                               ident)
                        if t == NT - 1:
                            ins.then_inc(S(f"nT_{name}"), 1)

            def turn_half(half_, banks, ready, src, name):
                turn_pair(2 * half_, banks[0], ready, src, name)
                turn_pair(2 * half_ + 1, banks[1], None, src, name)

            def ffn(f):
                u0 = BASE[f"ffn{f}"]
                name = NET_NORM[f]
                acc, gu, tr = [4, 5, 6, 7], [0, 1], 2
                TRN = S(f"tr_done{f}")

                def up(s, half_, banks, between=None):
                    for t in range(NT):
                        if t and between:
                            between()
                        for k in range(4):
                            if t == 0 and between:
                                pe.wait_ge(*W(f"ylo_{name}", k + 1))
                            ins = three(ps[:, banks[t], :], acts(yT, 4 * half_ + k, t), w(s, k * 512, (k + 1) * 512),
                                        half_ == 0 and k == 0, half_ == 1 and k == 3)
                    ins.then_inc(S("unit_used"), 1)
                    return ins

                def turn_hidden():
                    for k in range(2):
                        for t in range(NT):
                            ins = pe.transpose(ps[:, tr, (k * NT + t) * P:(k * NT + t + 1) * P],
                                               prod[:, t, k * P:(k + 1) * P], ident)
                    ins.then_inc(TRN, 1)

                def down(s, first, between=None):
                    for k in range(2):
                        if k and between:
                            between()
                        for t in range(NT):
                            for j in range(2):
                                c = k * D + j * 512
                                ins = three(ps[:, acc[2 * t + j], :], acts((hTh, hTl), k, t), w(s, c, c + 512),
                                            first and k == 0, False)
                    ins.then_inc(S("unit_used"), 1)

                def last_down(s):
                    for t in range(NT):
                        if t:
                            ins.then_inc(S(f"t0_ffn{f}"), 1)
                        for k in range(2):
                            for j in range(2):
                                c = k * D + j * 512
                                ins = three(ps[:, acc[2 * t + j], :], acts((hTh_last, hTl_last), k, t),
                                            w(s, c, c + 512), False, k == 1)
                    ins.then_inc(S("unit_used"), 1)

                def turn_last():
                    pe.wait_ge(*W(f"prod_ready{f}", 2 * NCH))
                    turn_hidden()

                def step(c, s0, first, between=None):
                    u = 3 * c - 1 + u0
                    pe.wait_ge(*W("lo_ready", u + 1))
                    if first:
                        up(s0, 0, gu)
                        pe.wait_ge(*W(f"prod_ready{f}", 2))
                    else:
                        pe.wait_ge(*W(f"prod_ready{f}", 2 * c))
                        up(s0, 0, gu)
                    turn_hidden()
                    pe.wait_ge(*W("lo_ready", u + 2))
                    up((s0 + 1) % RING, 1, gu)
                    pe.wait_ge(*W("lo_ready", u + 3))
                    pe.wait_ge(*W(f"hT_ready{f}", c))
                    down((s0 + 2) % RING, first, between)

                halves = {1: [("x_loaded0", 16), ("x_loaded1", 16)], 2: [("h_n2", 2), ("h_n2", 4)],
                          3: [("h_n5", 2), ("h_n5", 4)]}[f]
                if f < 3:
                    turn_half(0, [2, 3], halves[0], h, name)
                take([4, 6], [])
                begin(u0)
                if f == 1:
                    pe.wait_ge(*W("lo_first", 1))
                up(u0 % RING, 0, [4, 6], lambda: turn_half(1, [2, 3], halves[1], h, name))
                pe.wait_ge(*W(f"ylo_{name}", KD))
                begin(u0 + 1)
                up((u0 + 1) % RING, 1, [4, 6])
                take(gu, [])
                take([tr], [])
                take(acc, [({1: "h_n1", 2: "h_n3", 3: "h_n6"}[f], {1: 2, 2: 4, 3: 2}[f])])
                s0 = (u0 + 2) % RING
                step(1, s0, True)
                with pe.Fori(2, NCH - 1) as c:
                    step(c, s0, False)
                step(NCH - 1, s0, False, turn_last)
                pe.wait_ge(*W("lo_ready", u0 + FFN_UNITS))
                pe.wait_ge(*W(f"hT_ready{f}", NCH))
                last_down((u0 + FFN_UNITS - 1) % RING)
                drained[0] = drained[1] = [(f"prod_ready{f}", 2 * NCH)]
                drained[2] = [(f"hT_ready{f}", NCH)]

            pe.wait_ge(*W("ident_loaded", 16))
            ffn(1)

            turn_full(hn_m, "n1")
            for part, name, b in (("f_h", "fh", 4), ("q_h", "qh", 6)):
                for n in range(2):
                    take([b + n], [(f"{name}_out", n + 1)])
                    features(BASE[part] + n, b + n, "ylo_n1" if (part, n) == ("f_h", 0) else None)
            pe.wait_ge(*W("cn_loaded", 16))
            pe.wait_ge(*W("sm_loaded", 16))
            take([3], [("rel_ready", 1)])
            pe.matmul(ps[0:HEADS, 3, 0:NREL], M("rel")[0:BUCKETS, :], C("onehot")[0:BUCKETS, :],
                      start=True, stop=True).then_inc(S("rel_done"), 1)
            u = BASE["kv"]
            begin(u)
            take([0, 1], [("kvn", 8)])
            for t in range(NT):
                for k in range(KD):
                    ins = three(ps[:, t, 0:KV_COLS], acts(yT, k, t), w(u % RING, k * 256, k * 256 + KV_COLS),
                                k == 0, k == KD - 1)
            ins.then_inc(S("unit_used"), 1)
            for part, name, b in (("q_idx", "qi", 4), ("q_a", "qa", 6)):
                for n in range(2):
                    take([b + n], [(f"{name}_out", n + 1)])
                    features(BASE[part] + n, b + n)
            take([2], [("kvT_out", 1)])
            pe.wait_ge(*W("kvn", 8))
            for m, src in enumerate((ckvn, kk2)):
                for t in range(NT):
                    ins = pe.transpose(ps[:, 2, (m * NT + t) * P:(m * NT + t + 1) * P], src[:, t, :], ident)
            ins.then_inc(S("kvT_done"), 1)

            def level(n):
                e = E[n % 2]
                if n > len(LEVELS):
                    b = take([4], [("cross_out", 1)])[0]
                    pe.wait_ge(*W("E_ready", 2 * n))
                    for hd in range(HG):
                        ins = pe.matmul(ps[:, b, hd * P:(hd + 1) * P], e[:, hd, 0:P], e[:, hd, P:T],
                                        start=True, stop=True)
                    ins.then_inc(S("cross_done"), 1)
                    return
                bs = take([4, 5], [("level_out", n + 1)])
                a, q = (e, e) if n else (kf, qh)
                if n:
                    pe.wait_ge(*W("E_ready", 2 * n))
                else:
                    pe.wait_ge(*W("qh_out", 2))
                    pe.wait_ge(*W("kf_ready", 1))
                for hd in range(HG):
                    for t in range(NT):
                        m = hd * NT + t
                        ins = pe.matmul(ps[:, bs[m // 4], (m % 4) * P:(m % 4 + 1) * P],
                                        a[:, hd, t * P:(t + 1) * P], q[:, hd, t * P:(t + 1) * P],
                                        start=True, stop=True)
                ins.then_inc(S("level_done"), 1)

            level(0)
            take([0, 1], [("ih_out", 2)])
            pe.wait_ge(*W("kvT_out", 1))
            pe.wait_ge(*W("qi_out", 2))
            for n in range(2):
                for hd in range(4 * n, 4 * n + 4):
                    b = take([6 + hd % 2], [("relu_out", hd + 1)])[0]
                    a = HEAD_DIM * (hd % 2)
                    pe.matmul(ps[:, b, 0:P], qiT[a:a + 64, hd // 2, 0:P], kvT[a:a + 64, 1, 0:P],
                              start=True, stop=True)
                    pe.matmul(ps[:, b, P:3 * P], qiT[a:a + 64, hd // 2, P:T], kvT[a:a + 64, 1, :],
                              start=True, stop=True).then_inc(S("dots_done"), 1)
                row_unit(BASE["i_h"], n, 2, yT, [0, 1])
            banks = {("g_h", 0): ([2, 3], [("gh_out", 2)]), ("gate_b", 0): ([0, 1], [("gate_b_out", 2)]),
                     ("gate_b", 2): ([2, 3], [("gate_b_out", 4)]), ("gate_a", 0): ([6, 7], [("gate_a_out", 2)])}
            for n, (part, m) in enumerate(BETWEEN):
                level(n + 1)
                if m % 2 == 0:
                    bs = take(*banks[part, m])
                row = {"g_h": None, "gate_b": 2 + m // 2, "gate_a": m // 2}[part]
                if (part, m) == ("gate_b", 0):
                    pe.wait_ge(*W("identr_ready", 1))
                    pe.wait_ge(*W("bg_split", 1))
                row_unit(BASE[part] + m // 2 * 2, m % 2, 2, yT, bs, row)
            pe.wait_ge(*W("level_out", len(LEVELS) + 1))
            pe.wait_ge(*W("cross_out", 1))
            pe.wait_ge(*W("ih_out", 2))
            for t in range(NT):
                b = take([t], [("on_ready", 2 * (t + 1))])[0]
                for hd in range(HG):
                    c = slice(hd * P, (hd + 1) * P)
                    ins = pe.matmul(ps[:, b, c], AT[:, hd, t, :], vv[:, t, c], start=True, stop=(t == 0))
                    if t:
                        ins = pe.matmul(ps[:, b, c], ATx[:, hd, :], vv[:, 0, c], start=False, stop=True)
                ins.then_inc(S("hg_o"), 1)

            def latent_queries(n):
                bs = take([4, 5], [("ql_out", 2 * (n + 1))])
                for m in range(2):
                    for r in range(2):
                        a, pair = HEAD_DIM * r, 2 * n + m
                        ins = pe.matmul(ps[:, bs[r], m * T:(m + 1) * T],
                                        M("w_uk")[a:a + 64, pair * LATENT:(pair + 1) * LATENT],
                                        qaT[a:a + 64, pair, :], start=True, stop=True)
                ins.then_inc(S("ql_done"), 1)

            pe.wait_ge(*W("qa_out", 2))
            latent_queries(0)
            bs = take([2, 3], [("gate_a_out", 4)])
            row_unit(BASE["gate_a"] + 2, 0, 2, yT, bs, 1)
            latent_queries(1)
            row_unit(BASE["gate_a"] + 2, 1, 2, yT, bs, 1)
            for t in range(NT):
                b = take([6 + t], [("yb_ready", t + 1)])[0]
                pe.wait_ge(*W("on_ready", 2 * (t + 1)))
                for hd in range(HG):
                    ins = pe.transpose(ps[:, b, hd * P:(hd + 1) * P], on[:, t, hd * P:(hd + 1) * P], ident)
                ins.then_inc(S("ybT_done"), 1)

            def logits(qt):
                nk = (qt + 1) * P
                for n in range(4):
                    b = take([4 + n], [("lg_out", 4 * qt + n + 1)])[0]
                    for r in range(2):
                        o, hd = ps[:, b, r * T:r * T + nk], 2 * n + r
                        pe.matmul(o, qlat[:, hd, qt * P:(qt + 1) * P], kvT[:, 0, 0:nk], start=True, stop=False)
                        ins = pe.matmul(o, C("flip"), bias[:, hd, T - nk:T], start=False, stop=True)
                    ins.then_inc(S("lg_done"), 1)

            pe.wait_ge(*W("ql_out", 4))
            pe.wait_ge(*W("bias_loaded", 16))

            def probabilities_turned(m, b):
                qt = 0 if m < 2 else 1
                kt, g = (m - 2 * qt) // 2, m % 2
                take([b], [("pT_out", m + 1)])
                for r in range(4):
                    ins = pe.transpose(ps[:, b, r * P:(r + 1) * P], lg[qt][:, 4 * g + r, kt * P:(kt + 1) * P], ident)
                ins.then_inc(S("pT_done"), 1)

            def latents(qt):
                pe.wait_ge(*W("pT_out", 2 + 4 * qt))
                for g in range(2):
                    b = take([6 + g], [("ol_out", 2 * qt + g + 1)])[0]
                    for kt in range(qt + 1):
                        ins = pe.matmul(ps[:, b, :], ckvn[:, kt, :],
                                        pT[:, kt, 4 * g:4 * g + 4, :].rearrange("p a b -> p (a b)"),
                                        start=(kt == 0), stop=(kt == qt))
                    ins.then_inc(S("ol_done"), 1)

            def attended(qt):
                b = take([4], [("ya_ready", qt + 1)])[0]
                pe.wait_ge(*W("ol_out", 2 * (qt + 1)))
                for hd in range(HEADS):
                    a = HEAD_DIM * (hd % 2)
                    ins = pe.matmul(ps[a:a + 64, b, (hd // 2) * P:(hd // 2 + 1) * P],
                                    M("w_uv")[:, hd * 64:(hd + 1) * 64], olat[:, hd, :], start=True, stop=True)
                ins.then_inc(S("oT_done"), 1)

            def branch_a(j, t):
                u = BASE["br_a"] + j
                if t == 0:
                    begin(u)
                for k in range(4):
                    ins = three(ps[:, 2 * j + t, :], acts((yah, yal), k, t), w(u % RING, k * 512, (k + 1) * 512),
                                k == 0, k == 3)
                ins.then_inc(S("unit_used") if t else S("br_a_t0"), 1)

            logits(0)
            pe.wait_ge(*W("yb_ready", 2))
            rows(BASE["br_b"], 1, (ybh, ybl), take([0, 1], [("mb_out", 2)]))
            logits(1)
            pe.wait_ge(*W("probs_ready", 1))
            probabilities_turned(0, 4)
            probabilities_turned(1, 5)
            row_unit(BASE["br_b"] + 1, 0, 1, (ybh, ybl), take([2, 3], [("mb_out", 4)]), between=lambda: latents(0))
            attended(0)
            take([0], [("ma_out", 6)])
            take([2], [("ma_out", 8)])
            pe.wait_ge(*W("ya_ready", 1))
            for j in range(2):
                branch_a(j, 0)
            pe.wait_ge(*W("probs_ready", 2))
            for m, b in zip(range(2, 6), (4, 5, 1, 3)):
                probabilities_turned(m, b)
            latents(1)
            attended(1)
            take([1], [("ma_out", 6)])
            take([3], [("ma_out", 8)])
            pe.wait_ge(*W("ya_ready", 2))
            for j in range(2):
                branch_a(j, 1)
            turn_half(0, [0, 1], ("ma_out", 6), hn_m, "m1")

            def out_proj(part, nk, hl, by, ready, early=None, turns={}):
                for j in range(2):
                    for n in range(nk):
                        turn = turns.get(nk * j + n)
                        if n == 0:
                            bs = take([4 + j, 6 + j], [by[j]])
                        row_unit(BASE[part] + nk * j, n, nk, hl, bs,
                                 ready=ready if j == 0 else None,
                                 early=early if j == 1 and n == nk - 1 else None,
                                 between=(lambda: turn_half(*turn)) if turn else None)

            out_proj("w_out", 2, yT, [("h_n2", 4)] * 2, "ylo_m1", "t0_w_out",
                     {0: (1, [2, 3], ("ma_out", 8), hn_m, "m1")})

            ffn(2)

            u = BASE["ple_proj"]
            begin(u)
            take([0, 1, 2, 3], [("pm_out", 4)])
            pe.wait_ge(*W("pT_split", 1))
            for t in range(NT):
                for j in range(2):
                    if t and j:
                        turn_half(0, [4, 6], ("h_n3", 2), h, "n3")
                    for k in range(2):
                        c = k * D + j * 512
                        ins = three(ps[:, 2 * t + j, :], acts((pTh, pTl), k, t), w(u % RING, c, c + 512),
                                    k == 0, k == 1)
            ins.then_inc(S("unit_used"), 1)
            out_proj("ple_gate", 2, yT, [("pg_out", 2), ("pg_out", 4)], "ylo_n3", "t0_ple_gate",
                     {0: (1, [5, 7], ("h_n3", 4), h, "n3")})

            turn_full(hn_s, "n4")
            for part in ("s_c", "s_x", "s_b"):
                for n in range(4):
                    b = take([4 + n], [(f"{part}_out", n + 1)])[0]
                    features(BASE[part] + n, b, "ylo_n4" if (part, n) == ("s_c", 0) else None)
            u = BASE["dt"]
            begin(u)
            take([4], [("dtT_out", 1)])
            for k in range(KD):
                ins = three(ps[0:SSD_HEADS, 4, 0:T], w(u % RING, k * SSD_HEADS, (k + 1) * SSD_HEADS), acts(yT, k),
                            k == 0, k == KD - 1)
            ins.then_inc(S("unit_used"), 1)
            for j in range(2):
                bs = take([2 * j, 2 * j + 1], [("gb_out", 2 * (j + 1))])
                rows(BASE["g_b"] + 2 * j, 2, yT, bs)
                if j == 0:
                    take([5], [("dt_out", 1)])
                    pe.wait_ge(*W("dtT_out", 1))
                    for t in range(NT):
                        ins = pe.transpose(ps[:, 5, t * SSD_HEADS:(t + 1) * SSD_HEADS],
                                           dtT[:, t * P:(t + 1) * P], ident[0:SSD_HEADS, 0:SSD_HEADS])
                    ins.then_inc(S("dt_turned"), 1)
            out_proj("sconv_proj", 2, (svh, svl), [("mgb_out", 2), ("mgb_out", 4)], "sv_ready")
            for n in range(12):
                b = take([4 + n % 4], [("conv_out", 2 * (n + 1))])[0]
                features(BASE["xbc"] + n, b)
                if n == 3:
                    pe.wait_ge(*W("dtA_ready", 1))
                    take([1], [("kd_sub", 1)])
                    for t in range(NT):
                        pe.matmul(ps[0:SSD_HEADS, 1, (t + 1) * P:(t + 2) * P], dts[:, 1, t, :], C("tri"),
                                  start=True, stop=True)
                    for t in range(NT):
                        pe.matmul(ps[:, 1, t * 32:(t + 1) * 32], C("tri"), dts[:, 1, t, :], start=True, stop=True)
                    pe.matmul(ps[:, 1, 64:96], C("ones"), dts[:, 1, 0, :], start=True, stop=True)\
                      .then_inc(S("ac_done"), 1)
                elif n >= 4:
                    q, t = (n - 4) // 2, (n - 4) % 2
                    b = take([2 + n % 2], [("xdt_out", n - 3)])[0]
                    pe.wait_ge(*W("xs_ready", 4 * q + 4))
                    for r in range(4):
                        ins = pe.transpose(ps[:, b, r * P:(r + 1) * P], xs[:, 4 * q + r, t * P:(t + 1) * P], ident)
                    ins.then_inc(S("xT_done"), 1)

            def sums_ahead(q):
                bs = take([4, 5], [("seg_sub", 8 * (q + 1)), ("cross_exp", 2 * (q + 1))])
                if q == 0:
                    pe.wait_ge(*W("acT_split", 1))
                for r in range(4):
                    one = identr[0:SSD_HEADS, 4 * q + r:4 * q + r + 1].to_broadcast([SSD_HEADS, P])
                    o = ps[:, bs[r // 2], (r % 2) * T:(r % 2 + 1) * T]
                    pe.matmul(o, one, acTh[:, :], start=True, stop=False)
                    ins = pe.matmul(o, one, acTl[:, :], start=False, stop=True)
                ins.then_inc(S("bc_done"), 1)

            def group_sums(g):
                pe.wait_ge(*W("sq_ready", g + 1))
                for t in range(NT):
                    c = g * NT + t
                    for k in range(GT):
                        ins = pe.matmul(ps[:, 3, c:c + 1], sq[:, k, t * P:(t + 1) * P], C("ones")[:, 0:1],
                                        start=(k == 0), stop=(k == GT - 1))
                ins.then_inc(S("ssg_done"), 1)


            def roots_ahead(groups, banks):
                for g, b in zip(groups, banks):
                    take([b], [("yn_out", g + 1)])
                    for t in range(NT):
                        c = 24 + g * NT + t
                        ins = pe.matmul(ps[:, b, t * P:(t + 1) * P], st[:, c:c + 1].to_broadcast([P, P]), ident, start=True, stop=True)
                ins.then_inc(S("rb_done"), 1)

            sums_ahead(0)

            def keys_by_queries(g, b):
                take([b], [("cb_out", 3 * (g + 1))])
                pe.matmul(ps[:, b, 0:T], bc[:, g, 0:P], bc[:, GROUPS + g, :], start=True, stop=True)
                pe.matmul(ps[:, b, T:T + P], bc[:, g, P:T], bc[:, GROUPS + g, P:T],
                          start=True, stop=True).then_inc(S("cb_done"), 1)

            for q in range(8):
                take([Z_BANKS[q]], [("zs_ready", q + 1)])
                features(Z_UNITS[q], Z_BANKS[q])
                if q == 0:
                    pe.wait_ge(*W("xs_ready", 24))
                    keys_by_queries(0, 6)
                if q + 1 < GROUPS:
                    keys_by_queries(q + 1, 3)
                if q == 0:
                    bs = take([1, 2], [("ga_out", 2)])
                    row_unit(BASE["g_a0"], 0, 2, yT, bs)
                if q < 7:
                    sums_ahead(q + 1)
                if q == 3:
                    take([3], [("ss_ssd", 1)])
                if q >= 3 and q % 2:
                    group_sums((q - 3) // 2)
                if q == 7:
                    bs = take([1, 2], [("ga_out", 4)])
                    row_unit(BASE["g_a1"], 0, 2, yT, bs)
                    pe.wait_ge(*W("rstd_ssd", 1))
                    roots_ahead((0, 1, 2), (4, 5, 0))
                    take([3], [("ss_ssd", 2)])
                pe.wait_ge(*W("sc_ready", q + 1))
                if q == 0:
                    pe.wait_ge(*W("xw_ready", 1))
                b = take([6 + q % 2], [("y_out", 2 * (q + 1))])[0]
                for r in range(4):
                    hd = 4 * q + r
                    a, c = 64 * (r % 2), (r // 2) * T
                    pe.matmul(ps[a:a + 64, b, c:c + P], xdt[:, 0, hd, :], seg[:, r, 0, :], start=True, stop=True)
                    pe.matmul(ps[a:a + 64, b, c + P:c + T], xw[:, hd, :], seg[:, r, 1, :], start=True, stop=False)
                    ins = pe.matmul(ps[a:a + 64, b, c + P:c + T], xdt[:, 1, hd, :], seg[:, r, 2, :],
                                    start=False, stop=True)
                ins.then_inc(S("y_done"), 1)
                if q == 0:
                    row_unit(BASE["g_a0"], 1, 2, yT, bs)
            row_unit(BASE["g_a1"], 1, 2, yT, bs, between=lambda: group_sums(GROUPS - 1))
            pe.wait_ge(*W("rstd_ssd", 2))
            roots_ahead((3,), (3,))
            out_proj("ssd_proj", 4, (yhi, ylo), [("mga_out", 4), ("mga_out", 8)], "ylo_ssd", None,
                     {7: (0, [0, 1], ("mga_out", 4), merged, "m2")})
            out_proj("w_o", 2, yT, [("h_n5", 2), ("h_n5", 4)], "ylo_m2", None,
                     {0: (1, [2, 3], ("mga_out", 8), merged, "m2"), 3: (0, [2, 3], ("h_n5", 2), h, "n5")})

            ffn(3)

        @block.scalar
        def _(act):
            done = [0]
            count = [0]

            def link(ins):
                count[0] += 1
                ins.then_inc(S("act_chain"), 1)
                act.wait_ge(*W("act_chain", count[0]))

            def hi(slot, n=UNIT):
                act.activation(whi[slot][:, 0:n], raw[slot][:, 0:n], ACT.Copy).then_inc(S("hi_ready"), 1)

            def through(part, n):
                act.wait_ge(*W("unit_used", BASE[part] + n))

            def ahead(n):
                while done[0] < min(n, N_UNITS):
                    u = done[0]
                    act.wait_ge(*W(f"raw_loaded{u % RING}", 16 * (u // RING + 1)))
                    if u >= RING:
                        act.wait_ge(*W("unit_used", u - RING + 1))
                    hi(u % RING, DT_UNIT if u == BASE["dt"] else UNIT)
                    done[0] += 1

            cur = [hn_f]

            def junk(t):
                return cur[0][:, t, :]

            def turned(n, g, banks, halves=(0, 1)):
                for f in range(4 * halves[0], 4 * halves[-1] + 4):
                    if f % 2 == 0:
                        act.wait_ge(*W(f"nT_{n}", f // 2 + 1))
                    src = ps[:, banks[f // 2], (f % 2) * T:(f % 2 + 1) * T]
                    sc = 1.0 if g is None else M(g)[:, f:f + 1]
                    act.activation(yTh[:, f, :], src, ACT.Copy, scale=sc).then_inc(S(f"yhi_{n}"), 1)

            def ffn(f, beside=None):
                u0 = BASE[f"ffn{f}"]
                s0 = (u0 + 2) % RING
                SIL, HHI = S(f"sil_ready{f}"), S(f"hTh_ready{f}")

                def silu(used, banks=(0, 1)):
                    act.wait_ge(*W("unit_used", used))
                    for t in range(NT):
                        act.activation(sil[:, t, :], ps[:, banks[t], 0:FCH], ACT.Silu, scale=st[:, t:t + 1]).then_inc(SIL, 1)

                def hidden(c, dst=hTh):
                    act.wait_ge(*W(f"tr_done{f}", c))
                    act.activation(dst[:, :, :].rearrange("p a b -> p (a b)"), ps[:, 2, :], ACT.Copy).then_inc(HHI, 1)

                def split(u, slot, landed):
                    act.wait_ge(*W(f"raw_loaded{slot}", landed))
                    act.wait_ge(*W("unit_used", u - RING + 1))
                    hi(slot)

                ahead(u0 + 2)
                ahead(u0 + 3)
                act.wait_ge(*W(f"rstd_{NET_NORM[f]}", NT))
                ahead(u0 + 4)
                silu(u0 + 2, (4, 6))
                ahead(u0 + 5)
                if beside:
                    beside()

                def step(c, splits):
                    u = 3 * c + (u0 + 2)
                    hidden(c)
                    for n in range(RING):
                        if n == 1:
                            silu(3 * c + (u0 + 1))
                        if n < splits:
                            split(u + n, (s0 + n) % RING, 16 * c + 16 * ((u0 + 2 + n) // RING + 1))

                with act.Fori(1, NCH - 1) as c:
                    step(c, RING)
                step(NCH - 1, min(2, N_UNITS - (u0 + FFN_UNITS - 1)))
                done[0] = u0 + FFN_UNITS + 1
                hidden(NCH, hTh_last)

            def norm_sums(n, ready=None):
                for t in range(NT):
                    if ready:
                        act.wait_ge(*W(f"h_{n}", ready[t]))
                    act.activation(junk(t), h[:, t, :], ACT.Square, accum_out=st[:, t:t + 1])\
                       .then_inc(S(f"ss_{n}"), 1)

            def post_sums(part, units, n):
                for t in range(NT):
                    if t == 0:
                        act.wait_ge(*W(f"t0_{part}", 1))
                    else:
                        through(part, units)
                    act.activation(junk(t), ps[:, 4 + 2 * t:6 + 2 * t, :].rearrange("p a b -> p (a b)"), ACT.Square,
                                   accum_out=st[:, 2 + t:3 + t]).then_inc(S(f"ss_{n}"), 1)

            IN_NET = (2, 3, 2, 3)
            act.wait_ge(*W("raw_first", 16))
            act.activation(whi[0][:, 0:UNIT // 2], raw[0][:, 0:UNIT // 2], ACT.Copy).then_inc(S("hi_first"), 1)
            act.wait_ge(*W("raw_loaded0", 16))
            act.activation(whi[0][:, UNIT // 2:UNIT], raw[0][:, UNIT // 2:UNIT], ACT.Copy).then_inc(S("hi_ready"), 1)
            done[0] = 1
            act.wait_ge(*W("gains_loaded", 16))
            turned("n0", "g_ffn1", IN_NET, (0,))
            ahead(2)
            turned("n0", "g_ffn1", IN_NET, (1,))
            for j in range(2):
                act.wait_ge(*W(f"x_loaded{j}", 16))
            norm_sums("n0")
            ffn(1)

            ahead(BASE["f_h"] + 2)
            post_sums("ffn1", FFN_UNITS, "p0")
            cur[0] = hn_m
            norm_sums("n1", (1, 2))
            turned("n1", "g_mix", (0, 1, 2, 3))
            ahead(BASE["f_h"] + 3)
            act.wait_ge(*W("lb_sub", 2))
            act.activation(st[:, 40:48], st[:, 40:48], ACT.Exp).then_inc(S("lb_exp"), 1)
            act.activation(M("a_log"), M("a_log"), ACT.Exp).then_inc(S("alog_exp"), 1)

            def both(t):
                return t.rearrange("p a b -> p (a b)")

            def project(part, name, dst, fn, b):
                for m in range(2):
                    through(part, m + 1)
                    act.activation(both(dst[:, 2 * m:2 * m + 2, :]), ps[:, b + m, :], fn).then_inc(S(f"{name}_out"), 1)
                    ahead(BASE[part] + m + 1 + RING)

            act.wait_ge(*W("ident_loaded", 16))
            act.activation(identr[:, :], ident, ACT.Copy).then_inc(S("identr_ready"), 1)
            act.wait_ge(*W("bg_loaded", 16))
            act.activation(bgh[:, :], bg[:, :], ACT.Copy).then_inc(S("bgh_ready"), 1)
            project("f_h", "fh", sg, ACT.Sigmoid, 4)
            project("q_h", "qh", qh, ACT.Silu, 6)
            act.wait_ge(*W("f_ready", 1))
            act.activation(sg[:, :, :], sg[:, :, :], ACT.Ln).then_inc(S("lnf_ready"), 1)
            for t in range(NT):
                through("kv", 1)
                act.activation(hn_m[:, t, 0:LATENT], ps[:, t, 0:LATENT], ACT.Square,
                               accum_out=st[:, 8 + t:9 + t]).then_inc(S("ss_kv"), 1)
                act.activation(hn_m[:, t, LATENT:LATENT + 64], ps[:, t, LATENT:LATENT + 64], ACT.Square,
                               accum_out=st[:, 10 + t:11 + t]).then_inc(S("ss_kv"), 1)
            act.wait_ge(*W("rel_done", 1))
            act.activation(rel8[:, :], ps[0:HEADS, 3, 0:NREL], ACT.Copy).then_inc(S("rel_ready"), 1)
            ahead(BASE["kv"] + 1 + RING)
            project("q_idx", "qi", qiT, ACT.Copy, 4)
            project("q_a", "qa", qaT, ACT.Copy, 6)
            act.wait_ge(*W("kvT_done", 1))
            act.activation(both(kvT[:, :, :]), ps[:, 2, :], ACT.Copy).then_inc(S("kvT_out"), 1)

            def exponential(n):
                act.wait_ge(*W("X_sub", 2 * n))
                act.activation(X[:, :, :], X[:, :, :], ACT.Exp).then_inc(S("X_exp"), 1)

            def gate(j, part, dst, b):
                through(part, 2 * (j + 1))
                for t in range(NT):
                    act.activation(dst[:, t, :], ps[:, b + t, :], ACT.Sigmoid).then_inc(S(f"{part}_out"), 1)

            exponential(1)
            for n in range(2):
                for hd in range(4 * n, 4 * n + 4):
                    act.wait_ge(*W("dots_done", hd + 1))
                    if hd >= 2:
                        act.wait_ge(*W("score_acc", 2 * (hd - 1)))
                    act.activation(both(relu[hd % 2]), ps[:, 6 + hd % 2, 0:3 * P], ACT.Relu)\
                       .then_inc(S("relu_out"), 1)
                if n == 0:
                    exponential(2)
            ahead(BASE["i_h"] + 1 + RING)
            for n, (part, m) in enumerate(BETWEEN):
                ahead(BASE[part] + m + RING)
                if n + 3 <= len(LEVELS) + 1:
                    exponential(n + 3)
                if n == 0:
                    through("i_h", 2)
                    for t in range(NT):
                        act.activation(vv[:, t, :], ps[:, t, :], ACT.Copy).then_inc(S("ih_out"), 1)
                elif (part, m) == ("gate_b", 0):
                    through("g_h", 2)
                    for t in range(NT):
                        act.activation(sgh[:, t, :], ps[:, 2 + t, :], ACT.Silu).then_inc(S("gh_out"), 1)
                elif (part, m) == ("gate_b", 2):
                    gate(0, "gate_b", gates[:, :, 0:512], 0)
                elif (part, m) == ("gate_a", 0):
                    gate(1, "gate_b", gates[:, :, 512:1024], 2)
            for t in range(NT):
                act.wait_ge(*W("hg_o", t + 1))
                act.activation(on[:, t, 512:1024], ps[:, t, :], ACT.Square).then_inc(S("osq_ready"), 1)

            def latent_queries(n):
                act.wait_ge(*W("ql_done", n + 1))
                for r in range(2):
                    q = qlat[:, 4 * n:4 * n + 4, :].rearrange("p (m r) t -> p r m t", r=2)
                    act.activation(q[:, r, :, :], ps[:, 4 + r, :].rearrange("p (m t) -> p m t", m=2), ACT.Copy,
                                   scale=ATT_SCALE)\
                       .then_inc(S("ql_out"), 1)

            latent_queries(0)
            ahead(BASE["gate_a"] + 2 + RING)
            gate(0, "gate_a", gates_a[0], 6)
            latent_queries(1)
            ahead(BASE["gate_a"] + 3 + RING)
            for t in range(NT):
                act.wait_ge(*W("ybT_done", t + 1))
                act.activation(ybh[:, :, t * P:(t + 1) * P], ps[:, 6 + t, :].rearrange("p (a b) -> p a b", a=4),
                               ACT.Copy, scale=M("hg_norm")).then_inc(S("ybh_ready"), 1)
            act.wait_ge(*W("on_ready", 4))
            gate(1, "gate_a", gates_a[1], 2)
            ahead(BASE["gate_a"] + 4 + RING)

            def exponentials(qt, heads=range(HEADS)):
                nk = (qt + 1) * P
                act.wait_ge(*W("max_ready", qt + 1))
                for hd in heads:
                    act.activation(lg[qt][:, hd, 0:nk], lg[qt][:, hd, 0:nk], ACT.Exp,
                                   bias=st[:, MAXIMA[qt] + hd:MAXIMA[qt] + hd + 1],
                                   accum_out=st[:, TOTALS[qt] + hd:TOTALS[qt] + hd + 1]).then_inc(S("exp_ready"), 1)

            def probabilities_out(m, b):
                kt, g = (m - (0 if m < 2 else 2)) // 2, m % 2
                act.wait_ge(*W("pT_done", m + 1))
                if m == 2:
                    act.wait_ge(*W("ol_done", 2))
                act.activation(both(pT[:, kt, 4 * g:4 * g + 4, :]), ps[:, b, :], ACT.Copy).then_inc(S("pT_out"), 1)

            def latents_out(qt):
                for g in range(2):
                    act.wait_ge(*W("ol_done", 2 * qt + g + 1))
                    if qt:
                        act.wait_ge(*W("oT_done", qt))
                    act.activation(both(olat[:, 4 * g:4 * g + 4, :]), ps[:, 6 + g, :], ACT.Copy)\
                       .then_inc(S("ol_out"), 1)

            def attended_out(qt):
                act.wait_ge(*W("oT_done", qt + 1))
                act.activation(yah[:, :, qt * P:(qt + 1) * P], ps[:, 4, :].rearrange("p (a b) -> p a b", a=4),
                               ACT.Copy).then_inc(S("yah_ready"), 1)

            exponentials(0)
            ahead(BASE["br_b"] + 1 + RING)
            probabilities_out(0, 4)
            probabilities_out(1, 5)
            latents_out(0)
            exponentials(1, range(6))
            attended_out(0)
            exponentials(1, range(6, HEADS))
            ahead(BASE["br_b"] + 2 + RING)
            for m, b in zip(range(2, 6), (4, 5, 1, 3)):
                probabilities_out(m, b)
            latents_out(1)
            attended_out(1)
            ahead(BASE["br_a"] + 1 + RING)
            turned("m1", None, (0, 1, 2, 3), (0,))
            ahead(BASE["br_a"] + 2 + RING)
            turned("m1", None, (0, 1, 2, 3), (1,))
            ahead(BASE["w_out"] + 3 + RING)
            cur[0] = squares
            act.wait_ge(*W("gained", 2))
            post_sums("w_out", 4, "p1")
            turned("n2", "g_ffn2", IN_NET)
            norm_sums("n2", (4, 4))
            ahead(BASE["w_out"] + 4 + RING)

            def per_layer():
                act.wait_ge(*W("p_loaded", 16))
                act.activation(pTh[:, :, :], praw[:, :, :], ACT.Copy).then_inc(S("pTh_ready"), 1)

            ffn(2, per_layer)
            ahead(BASE["ple_proj"] + 2)
            post_sums("ffn2", FFN_UNITS, "p2")
            ahead(BASE["ple_proj"] + 3)
            turned("n3", "g_ple", (4, 6, 5, 7))
            ahead(BASE["ple_gate"] + RING)
            norm_sums("n3", (4, 4))
            ahead(BASE["ple_gate"] + 2 + RING)
            for j in range(2):
                for t in range(NT):
                    act.wait_ge(*W("rstd_n3", t + 1))
                    if j and t == 0:
                        act.wait_ge(*W("t0_ple_gate", 1))
                    else:
                        through("ple_gate", 2 * (j + 1))
                    act.activation(pgate[:, t, j * 512:(j + 1) * 512], ps[:, 4 + 2 * t + j, :], ACT.Sigmoid,
                                   scale=st[:, t:t + 1]).then_inc(S("pg_out"), 1)
                if j == 0:
                    ahead(BASE["ple_gate"] + 3 + RING)
            for t in range(NT):
                act.wait_ge(*W("pm_out", 3 + t))
                act.activation(squares[:, t, :], pgate[:, t, :], ACT.Square, accum_out=st[:, 2 + t:3 + t])\
                   .then_inc(S("ss_p3"), 1)

            cur[0] = hn_s
            norm_sums("n4", (1, 2))
            turned("n4", "g_mix2", (0, 1, 2, 3))
            ahead(BASE["ple_gate"] + 4 + RING)
            w3 = M("sconv_w")
            for n in range(4):
                through("s_c", n + 1)
                act.activation(both(cx[:, 2 * n:2 * n + 2, :]), ps[:, 4 + n, :], ACT.Copy).then_inc(S("s_c_out"), 1)
                ahead(BASE["s_c"] + n + 1 + RING)
            for n in range(4):
                act.wait_ge(*W("s_x_out", n + 1))
                for f in (2 * n, 2 * n + 1):
                    act.activation(cv[:, f, :], cx[:, f, :], ACT.Copy, scale=w3[:, 3 * f + 2:3 * f + 3])\
                       .then_inc(S("cv_first"), 1)
                ahead(BASE["s_x"] + n + 1 + RING)
            for n in range(4):
                act.wait_ge(*W("s_b_out", n + 1))
                act.activation(both(svh[:, 2 * n:2 * n + 2, :]), both(cx[:, 2 * n:2 * n + 2, :]), ACT.Copy)\
                   .then_inc(S("svh_ready"), 1)
                ahead(BASE["s_b"] + n + 1 + RING)
            through("dt", 1)
            act.activation(dtT[:, :], ps[0:SSD_HEADS, 4, 0:T], ACT.Copy).then_inc(S("dtT_out"), 1)
            ahead(BASE["dt"] + 1 + RING)
            for j in range(2):
                through("g_b", 2 * (j + 1))
                for t in range(NT):
                    act.activation(sga[:, t, j * 512:(j + 1) * 512], ps[:, 2 * j + t, :], ACT.Sigmoid)\
                       .then_inc(S("gb_out"), 1)
                ahead(BASE["g_b"] + 2 * j + 2 + RING)
                if j == 0:
                    act.wait_ge(*W("sp_abs", 1))
                    act.activation(dts[:, 3, :, :], dts[:, 3, :, :], ACT.Exp, scale=-1.0).then_inc(S("sp_exp"), 1)
            ahead(BASE["sconv_proj"] + 4 + RING)
            cw, cb = M("conv_w"), M("conv_b")

            def conv_silu(n):
                act.wait_ge(*W("conv_out", 2 * (n + 1)))
                dst = xs[:, 2 * n:2 * n + 2, :] if n < 8 else bc[:, 2 * n - 16:2 * n - 14, :]
                act.activation(both(dst), both(cvt[:, n % 2, :, :]), ACT.Silu).then_inc(S("xs_ready"), 2)

            for n in range(12):
                through("xbc", n + 1)
                if n >= 2:
                    act.wait_ge(*W("xs_ready", 2 * (n - 1)))
                for r in range(2):
                    f = 2 * n + r
                    act.activation(cvt[:, n % 2, r, :], ps[:, 4 + n % 4, r * T:(r + 1) * T], ACT.Identity,
                                   bias=cb[:, f:f + 1], scale=cw[:, 4 * f + 3:4 * f + 4]).then_inc(S("cvt_first"), 1)
                if n:
                    conv_silu(n - 1)
                if n == 4:
                    act.wait_ge(*W("ac_done", 1))
                    act.activation(acTh[:, :], ps[0:SSD_HEADS, 1, P:P + T], ACT.Copy).then_inc(S("acTh_ready"), 1)
                ahead(BASE["xbc"] + n + 1 + RING)
            conv_silu(11)
            act.wait_ge(*W("kd_sub", 1))
            act.activation(dts[:, 8, 0, :], dts[:, 8, 0, :], ACT.Exp).then_inc(S("kd_exp"), 1)

            def gates_out(j, banks):
                through(f"g_a{j}", 2)
                for t in range(NT):
                    act.activation(sga[:, t, j * 512:(j + 1) * 512], ps[:, banks[t], :], ACT.Sigmoid)\
                       .then_inc(S("ga_out"), 1)

            def group_squares(g):
                act.wait_ge(*W("z_out", 2 * g + 2))
                if g:
                    act.wait_ge(*W("ssg_done", g))
                act.activation(both(sq[:, :, :]), both(xs[:, GT * g:GT * g + GT, :]), ACT.Square)\
                   .then_inc(S("sq_ready"), 1)

            for q in range(8):
                act.wait_ge(*W("bc_done", q + 1))
                if q:
                    act.wait_ge(*W("y_done", q))
                for n in range(2):
                    act.activation(seg[:, 2 * n:2 * n + 2, 1, :],
                                   ps[:, 4 + n, :].rearrange("p (r t c) -> p r t c", r=2, t=NT)[:, :, 1, :], ACT.Exp)\
                       .then_inc(S("cross_exp"), 1)
                if q >= 2:
                    ahead(Z_UNITS[q - 1] + 1 + RING)
                act.wait_ge(*W("seg_sub", 8 * (q + 1)))
                for n in (0, 2):
                    act.activation(seg[:, :, n, :], seg[:, :, n, :], ACT.Exp).then_inc(S("seg_exp"), 1)
                if q == 1:
                    ahead(BASE["g_a0"] + 2 + RING)
                    gates_out(0, (1, 2))
                if q >= 2 and q % 2 == 0:
                    group_squares(q // 2 - 1)
                act.wait_ge(*W("unit_used", Z_UNITS[q] + 1))
                if q:
                    act.wait_ge(*W("z_out", q))
                act.activation(both(zs[:, :, :]), ps[:, Z_BANKS[q], :], ACT.Silu).then_inc(S("zs_ready"), 1)
                if q < 7:
                    act.activation(st[:, 63:64], half[:, 0:1], ACT.Exp)
                if q == 0:
                    ahead(Z_UNITS[0] + 1 + RING)
                    ahead(BASE["g_a0"] + 1 + RING)
            ahead(BASE["g_a1"] + 1 + RING)
            group_squares(GROUPS - 1)
            nw = M("ssd_norm")
            for f in range(XT):
                if f == 0:
                    act.wait_ge(*W("y_done", 8))
                act.wait_ge(*W("yn_out", f // GT + 1))
                act.activation(yhi[:, f, :], xs[:, f, :], ACT.Copy, scale=nw[:, f:f + 1]).then_inc(S("yhi_ssd"), 1)
            gates_out(1, (1, 2))
            ahead(BASE["g_a1"] + 2 + RING)
            ahead(BASE["ssd_proj"] + 7 + RING)
            turned("m2", None, (0, 1, 2, 3), (0,))
            ahead(BASE["ssd_proj"] + 8 + RING)
            turned("m2", None, (0, 1, 2, 3), (1,))
            ahead(BASE["w_o"] + 3 + RING)
            cur[0] = hn_f
            turned("n5", "g_ffn3", IN_NET)
            norm_sums("n5", (4, 4))
            ahead(BASE["w_o"] + 4 + RING)
            ffn(3)
            norm_sums("n6", (1, 2))

        @block.vector
        def _(dve):
            done = [0]
            count = [0]

            def link(ins):
                count[0] += 1
                ins.then_inc(S("dve_chain"), 1)
                dve.wait_ge(*W("dve_chain", count[0]))

            def lo(slot, n=UNIT):
                dve.tensor_tensor(wlo[slot][:, 0:n], raw[slot][:, 0:n], f32(whi[slot][:, 0:n]), ALU.subtract)\
                   .then_inc(S("lo_ready"), 1)

            def through(part, n):
                dve.wait_ge(*W("unit_used", BASE[part] + n))

            def ahead(n):
                while done[0] < min(n, N_UNITS):
                    u = done[0]
                    dve.wait_ge(*W("hi_ready", u + 1))
                    lo(u % RING, DT_UNIT if u == BASE["dt"] else UNIT)
                    done[0] += 1

            def normed(n, dst):
                for t in range(NT):
                    dve.wait_ge(*W(f"rstd_{n}", t + 1))
                    dve.tensor_scalar(dst[:, t, :], h[:, t, :], st[:, t:t + 1], None, ALU.mult)\
                       .then_inc(S(f"hn_{n}"), 1)

            def turned(n, g, banks, halves=(0, 1)):
                for f in range(4 * halves[0], 4 * halves[-1] + 4):
                    src = ps[:, banks[f // 2], (f % 2) * T:(f % 2 + 1) * T]
                    if f % 2 == 0:
                        dve.wait_ge(*W(f"yhi_{n}", f + 2))
                    if g is None:
                        ins = dve.tensor_tensor(yTl[:, f, :], src, f32(yTh[:, f, :]), ALU.subtract)
                    else:
                        ins = dve.scalar_tensor_tensor(yTl[:, f, :], src, M(g)[:, f:f + 1], f32(yTh[:, f, :]),
                                                       ALU.mult, ALU.subtract)
                    ins.then_inc(S(f"ylo_{n}"), 1)

            def ffn(f, beside=None):
                u0 = BASE[f"ffn{f}"]
                s0 = (u0 + 2) % RING
                def gated(c2, banks=(0, 1)):
                    for t in range(NT):
                        dve.wait_ge(*W(f"sil_ready{f}", c2 + t + 1))
                        dve.scalar_tensor_tensor(prod[:, t, :], ps[:, banks[t], FCH:2 * FCH], st[:, t:t + 1], sil[:, t, :],
                                                 ALU.mult, ALU.mult).then_inc(S(f"prod_ready{f}"), 1)

                def hidden(c, hi=hTh, low=hTl):
                    dve.wait_ge(*W(f"hTh_ready{f}", c))
                    dve.tensor_tensor(low[:, :, :].rearrange("p a b -> p (a b)"), ps[:, 2, :],
                                      f32(hi[:, :, :].rearrange("p a b -> p (a b)")), ALU.subtract)\
                       .then_inc(S(f"hT_ready{f}"), 1)

                ahead(u0 + 2)
                ahead(u0 + 3)
                ahead(u0 + 4)
                gated(0, (4, 6))
                ahead(u0 + 5)
                if beside:
                    beside()

                def step(c, splits):
                    hidden(c)
                    for n in range(RING):
                        if n == 1:
                            gated(2 * c)
                        if n < splits:
                            dve.wait_ge(*W("hi_ready", 3 * c + (u0 + 2 + n + 1)))
                            lo((s0 + n) % RING)

                with dve.Fori(1, NCH - 1) as c:
                    step(c, RING)
                step(NCH - 1, min(2, N_UNITS - (u0 + FFN_UNITS - 1)))
                done[0] = u0 + FFN_UNITS + 1
                hidden(NCH, hTh_last, hTl_last)

            def post_norm(n, new, src, by_halves, first=0):

                def renew(t, c):
                    dve.wait_ge(*W(f"rstd_{n}", t + 1))
                    dve.scalar_tensor_tensor(h[:, t, c], scr[0][:, t, c], st[:, 2 + t:3 + t], h[:, t, c],
                                             ALU.mult, ALU.add).then_inc(S(f"h_{new}"), 1)

                for t in range(NT):
                    dve.wait_ge(*W(f"ss_{n}", t + 1))
                    if first < D:
                        link(dve.tensor_tensor(scr[0][:, t, first:], src(t)[:, first:], post[:, first:], ALU.mult))
                    else:
                        dve.wait_ge(*W("dve_chain", count[0]))
                    if by_halves:
                        renew(t, slice(0, 512))
                    else:
                        renew(t, slice(0, D))
                if by_halves:
                    for t in range(NT):
                        renew(t, slice(512, D))

            def acc(t):
                return ps[:, 4 + 2 * t:6 + 2 * t, :].rearrange("p a b -> p (a b)")

            scr = [hn_f]
            IN_NET = (2, 3, 2, 3)
            for c, made in ((slice(0, UNIT // 2), ("hi_first", "lo_first")),
                            (slice(UNIT // 2, UNIT), ("hi_ready", "lo_ready"))):
                dve.wait_ge(*W(made[0], 1))
                dve.tensor_tensor(wlo[0][:, c], raw[0][:, c], f32(whi[0][:, c]), ALU.subtract).then_inc(S(made[1]), 1)
            done[0] = 1
            dve.wait_ge(*W("gains_loaded", 16))
            turned("n0", "g_ffn1", IN_NET, (0,))
            ahead(2)
            turned("n0", "g_ffn1", IN_NET, (1,))
            dve.wait_ge(*W("rstd_n0", NT))
            ffn(1)
            dve.wait_ge(*W("sm_loaded", 16))
            lbr = M("hg_lb").rearrange("p (a b) -> p a b", a=2)
            link(dve.tensor_tensor(st[:, 36:40], lbr[:, 0, :], lbr[:, 1, :], ALU.max))
            for r in range(2):
                dve.tensor_tensor(st[:, 40 + 4 * r:44 + 4 * r], lbr[:, r, :], st[:, 36:40], ALU.subtract)\
                   .then_inc(S("lb_sub"), 1)
            ahead(BASE["f_h"] + 2)
            dve.wait_ge(*W("post_loaded", 16))
            post_norm("p0", "n1", acc, False)
            scr[0] = hn_m
            normed("n1", hn_m)
            turned("n1", "g_mix", (0, 1, 2, 3))
            ahead(BASE["f_h"] + 3)
            dve.wait_ge(*W("bgh_ready", 1))
            dve.tensor_tensor(bgl[:, :], bg[:, :], f32(bgh[:, :]), ALU.subtract).then_inc(S("bg_split"), 1)
            dve.wait_ge(*W("lb_exp", 1))
            link(dve.tensor_tensor(st[:, 44:48], st[:, 40:44], st[:, 44:48], ALU.add))
            link(dve.reciprocal(st[:, 44:48], st[:, 44:48]))
            link(dve.tensor_tensor(st[:, 40:44], st[:, 40:44], st[:, 44:48], ALU.mult))
            link(dve.tensor_scalar(st[:, 44:48], st[:, 40:44], -1.0, 1.0, ALU.mult, ALU.add))
            ahead(BASE["f_h"] + 1 + RING)
            dve.wait_ge(*W("fh_out", 2))
            for hd in range(HG):
                link(dve.tensor_scalar(sg[:, hd, :], sg[:, hd, :], st[:, 44 + hd:45 + hd], st[:, 40 + hd:41 + hd],
                                       ALU.mult, ALU.add))
            dve.tensor_scalar(kf[:, :, :], sg[:, :, :], -1.0, 1.0, ALU.mult, ALU.add).then_inc(S("kf_ready"), 1)
            dve.wait_ge(*W("kf_ready", 1))
            dve.tensor_scalar(sg[:, :, :], sg[:, :, :], 2.0 ** -64, None, ALU.max).then_inc(S("f_ready"), 1)
            for n in range(1, 4):
                ahead(BASE["f_h"] + n + 1 + RING)
            dve.memset(AT[:, :, :, :], 0.0).then_inc(S("AT_zero"), 1)
            dve.wait_ge(*W("lnf_ready", 1))
            for hd in range(HG):
                link(dve.tensor_tensor_scan(G[:, hd, :], C("reset"), sg[:, hd, :], 0.0, ALU.mult, ALU.add))
            dve.wait_ge(*W("rstd_kv", 1))
            for t in range(NT):
                dve.scalar_tensor_tensor(ckvn[:, t, :], ps[:, t, 0:LATENT], st[:, 8 + t:9 + t], M("kv_g"),
                                         ALU.mult, ALU.mult).then_inc(S("kvn"), 1)
                for r in range(2):
                    dve.scalar_tensor_tensor(kk2[:, t, r * 64:(r + 1) * 64], ps[:, t, LATENT:LATENT + 64],
                                             st[:, 10 + t:11 + t], M("ki_g"), ALU.mult, ALU.mult)\
                       .then_inc(S("kvn"), 1)
                dve.tensor_scalar(wi[:, t, :], ps[:, t, LATENT + 64:KV_COLS], IDX_W_SCALE, None, ALU.mult)\
                   .then_inc(S("kvn"), 1)
            ahead(BASE["kv"] + 1 + RING)

            def blocks(x, b):
                return x.rearrange("p h (n r b) -> p (h n) r b", r=2, b=b)

            def exponents(n):
                if n > 1:
                    dve.wait_ge(*W("E_ready", 2 * (n - 1)))
                if n <= len(LEVELS):
                    b = LEVELS[n - 1]
                    g, x = blocks(G[:, :, :], b), blocks(X[:, :, :], b)
                    nb = HG * T // (2 * b)
                    ref = g[:, :, 0, b - 1:b].to_broadcast([P, nb, b])
                    if b < CHUNK:
                        dve.tensor_tensor(x[:, :, 1, :], g[:, :, 1, :], ref, ALU.subtract).then_inc(S("X_sub"), 1)
                    else:
                        dve.tensor_copy(x[:, :, 1, :], g[:, :, 1, :]).then_inc(S("X_sub"), 1)
                    dve.tensor_tensor(x[:, :, 0, :], ref, g[:, :, 0, :], ALU.subtract).then_inc(S("X_sub"), 1)
                else:
                    g = G[:, :, :].rearrange("p h (n c) -> p h n c", c=CHUNK)
                    x = X[:, :, :].rearrange("p h (n c) -> p h n c", c=CHUNK)

                    def last(c):
                        return g[:, :, c, CHUNK - 1:CHUNK].to_broadcast([P, HG, CHUNK])

                    link(dve.tensor_copy(x[:, :, 2, :], g[:, :, 2, :]))
                    link(dve.tensor_tensor(x[:, :, 3, :], g[:, :, 3, :], last(2), ALU.add))
                    link(dve.tensor_tensor(x[:, :, 1, :], last(1), g[:, :, 1, :], ALU.subtract))
                    link(dve.tensor_tensor(x[:, :, 0, :], last(0), g[:, :, 0, :], ALU.subtract))
                    dve.tensor_tensor(x[:, :, 0, :], x[:, :, 0, :], last(1), ALU.add).then_inc(S("X_sub"), 2)

            def decayed(n):
                dve.wait_ge(*W("X_exp", n))
                if n == 1:
                    dve.wait_ge(*W("qh_out", 2))
                e = E[n % 2]
                b = LEVELS[n - 1] if n <= len(LEVELS) else P
                x, eb = blocks(X[:, :, :], b), blocks(e[:, :, :], b)
                dve.tensor_tensor(eb[:, :, 1, :], x[:, :, 1, :], blocks(qh[:, :, :], b)[:, :, 1, :], ALU.mult)\
                   .then_inc(S("E_ready"), 1)
                dve.tensor_tensor(eb[:, :, 0, :], x[:, :, 0, :], blocks(kf[:, :, :], b)[:, :, 0, :], ALU.mult)\
                   .then_inc(S("E_ready"), 1)

            def level_out(n):
                if n > len(LEVELS):
                    dve.wait_ge(*W("cross_done", 1))
                    dve.tensor_copy(ATx[:, :, :].rearrange("p a b -> p (a b)"), ps[:, 4, :])\
                       .then_inc(S("cross_out"), 1)
                    return
                mask = C("levels")[:, n * P:(n + 1) * P].bitcast(U32)
                dve.wait_ge(*W("level_done", n + 1))
                if n == 0:
                    dve.wait_ge(*W("AT_zero", 1))
                else:
                    dve.wait_ge(*W("level_out", n))
                a = AT[:, :, :, :].rearrange("p h t c -> p (h t) c")
                dve.copy_predicated(a, mask.rearrange("p (a b) -> p a b", a=1).to_broadcast([P, HG * NT, P]),
                                    ps[:, 4:6, :].rearrange("p n (m c) -> p (n m) c", c=P)).then_inc(S("level_out"), 1)

            def scores(hd):
                dve.wait_ge(*W("relu_out", hd + 1))
                for qt in range(NT):
                    v = score[:, 0:1, :] if qt == 0 else score[:, 1:3, :]
                    r = relu[hd % 2][:, 0:1, :] if qt == 0 else relu[hd % 2][:, 1:3, :]
                    if hd:
                        dve.wait_ge(*W("score_acc", 2 * (hd - 1) + qt + 1))
                    dve.scalar_tensor_tensor(v, r, wi[:, qt, hd:hd + 1], v, ALU.mult, ALU.add)\
                       .then_inc(S("score_acc"), 1)

            def rivals(qt):
                return (score[:, 0:1, :] if qt == 0 else score[:, 1:3, :]).rearrange("p a b -> p (a b)")

            def best(qt, n=1):
                v = rivals(qt)
                for _ in range(n):
                    link(dve.max(top8[:, :], v))
                    link(dve.match_replace(v, top8[:, :], v, -3.0e38))

            def chosen(qt):
                v = rivals(qt)
                link(dve.tensor_scalar(v, v, -2.0e38, -1.0e30, ALU.is_gt, ALU.mult))
                d = score[:, 2 * qt, :]
                link(dve.tensor_tensor(d, d, C("causal"), ALU.add))

            exponents(1)
            for n in range(2):
                ahead(BASE["q_idx"] + n + 1 + RING)
            score_init(dve, S, score, C)
            for n in range(2):
                ahead(BASE["q_a"] + n + 1 + RING)
            decayed(1)
            exponents(2)
            level_out(0)
            dve.wait_ge(*W("score_init", 3))
            for n in range(2):
                for hd in range(4 * n, 4 * n + 4):
                    scores(hd)
            ahead(BASE["i_h"] + 1 + RING)
            dve.wait_ge(*W("score_acc", 2 * HEADS))
            for n, (part, m) in enumerate(BETWEEN):
                if n + 2 <= len(LEVELS) + 1:
                    decayed(n + 2)
                if n + 3 <= len(LEVELS) + 1:
                    exponents(n + 3)
                level_out(n + 1)
                if n < 5:
                    best(0)
                ahead(BASE[part] + m + RING)

            def wide(t):
                return on[:, t, 0:512].rearrange("p (a b) -> p a b", a=HG)

            for t in range(NT):
                dve.wait_ge(*W("osq_ready", t + 1))
                dve.tensor_reduce(st[:, 16 + 4 * t:20 + 4 * t], on[:, t, 512:1024].rearrange("p (a b) -> p a b", a=HG),
                                  AX.X, ALU.add).then_inc(S("ss_hg"), 1)
            best(0, 3)
            chosen(0)
            for t in range(NT):
                dve.wait_ge(*W("rstd_hg", t + 1))
                dve.wait_ge(*W("gh_out", t + 1))
                r = st[:, 16 + 4 * t:20 + 4 * t].rearrange("p (a b) -> p a b", b=1).to_broadcast([P, HG, P])
                dve.tensor_tensor(wide(t), ps[:, t, :].rearrange("p (a b) -> p a b", a=HG), r, ALU.mult)\
                   .then_inc(S("on_ready"), 1)
                dve.wait_ge(*W("on_ready", 2 * t + 1))
                dve.tensor_tensor(on[:, t, 0:512], on[:, t, 0:512], sgh[:, t, :], ALU.mult)\
                   .then_inc(S("on_ready"), 1)
            ahead(BASE["gate_a"] + 2 + RING)
            best(1, 4)
            ahead(BASE["gate_a"] + 3 + RING)
            for t in range(NT):
                dve.wait_ge(*W("ybh_ready", t + 1))
                v = slice(t * P, (t + 1) * P)
                dve.scalar_tensor_tensor(ybl[:, :, v], ps[:, 6 + t, :].rearrange("p (a b) -> p a b", a=4),
                                         M("hg_norm"), f32(ybh[:, :, v]), ALU.mult, ALU.subtract)\
                   .then_inc(S("yb_ready"), 1)
            best(1, 4)
            chosen(1)

            def selected(qt):
                nk = (qt + 1) * P
                sel = rivals(qt).rearrange("p (a b) -> p a b", a=1).to_broadcast([P, 2, nk])
                for n in range(HEADS // 2):
                    dve.wait_ge(*W("lg_done", 4 * qt + n + 1))
                    src = ps[:, 4 + n, :].rearrange("p (a b) -> p a b", a=2)[:, :, 0:nk]
                    dve.tensor_tensor(lg[qt][:, 2 * n:2 * n + 2, 0:nk], src, sel, ALU.add).then_inc(S("lg_out"), 1)
                dve.wait_ge(*W("lg_out", 4 * (qt + 1)))
                dve.tensor_reduce(st[:, MAXIMA[qt]:MAXIMA[qt] + 8], lg[qt][:, :, 0:nk], AX.X, ALU.max, negate=True)\
                   .then_inc(S("max_ready"), 1)

            def probabilities(qt):
                nk = (qt + 1) * P
                dve.wait_ge(*W("exp_ready", 8 * (qt + 1)))
                total = st[:, TOTALS[qt]:TOTALS[qt] + 8]
                link(dve.reciprocal(total, total))
                r = total.rearrange("p (a b) -> p a b", b=1).to_broadcast([P, HEADS, nk])
                dve.tensor_tensor(lg[qt][:, :, 0:nk], lg[qt][:, :, 0:nk], r, ALU.mult).then_inc(S("probs_ready"), 1)

            def branch_b_out(j):
                through("br_b", j + 1)
                for t in range(NT):
                    c = slice(j * 512, (j + 1) * 512)
                    if j == 0 and t == 0:
                        dve.wait_ge(*W("gate_b_out", 4))
                        dve.wait_ge(*W("ybT_done", 2))
                    dve.tensor_tensor(hn_m[:, t, c], ps[:, 2 * j + t, :], gates[:, t, c], ALU.mult)\
                       .then_inc(S("mb_out"), 1)

            def attended_low(qt):
                dve.wait_ge(*W("yah_ready", qt + 1))
                q = slice(qt * P, (qt + 1) * P)
                dve.tensor_tensor(yal[:, :, q], ps[:, 4, :].rearrange("p (a b) -> p a b", a=4), f32(yah[:, :, q]),
                                  ALU.subtract).then_inc(S("ya_ready"), 1)

            def branch_a_out(j, t, n):
                if t == 0:
                    dve.wait_ge(*W("br_a_t0", j + 1))
                else:
                    through("br_a", j + 1)
                dve.wait_ge(*W("gate_a_out", 4))
                c = slice(j * 512, (j + 1) * 512)
                dve.tensor_tensor(gates_a[j][:, t, :], ps[:, 2 * j + t, :], gates_a[j][:, t, :], ALU.mult)\
                   .then_inc(S("ma_out"), 1)
                dve.wait_ge(*W("ma_out", 2 * n + 1))
                dve.tensor_tensor(hn_m[:, t, c], hn_m[:, t, c], gates_a[j][:, t, :], ALU.add)\
                   .then_inc(S("ma_out"), 1)

            selected(0)
            ahead(BASE["gate_a"] + 4 + RING)
            probabilities(0)
            branch_b_out(0)
            selected(1)
            ahead(BASE["br_b"] + 1 + RING)
            branch_b_out(1)
            attended_low(0)
            probabilities(1)
            ahead(BASE["br_b"] + 2 + RING)
            branch_a_out(0, 0, 0)
            branch_a_out(1, 0, 1)
            attended_low(1)
            branch_a_out(0, 1, 2)
            turned("m1", None, (0, 1, 2, 3), (0,))
            branch_a_out(1, 1, 3)
            ahead(BASE["br_a"] + 1 + RING)
            turned("m1", None, (0, 1, 2, 3), (1,))
            ahead(BASE["br_a"] + 2 + RING)
            ahead(BASE["w_out"] + 2 + RING)
            scr[0] = hn_f
            dve.wait_ge(*W("post_loaded", 32))
            dve.wait_ge(*W("nT_m1", 4))
            through("w_out", 2)
            for t in range(NT):
                dve.tensor_tensor(scr[0][:, t, 0:512], ps[:, 4 + 2 * t, :], post[:, 0:512], ALU.mult)\
                   .then_inc(S("gained"), 1)
            dve.wait_ge(*W("gained", 2))
            ahead(BASE["w_out"] + 3 + RING)
            post_norm("p1", "n2", acc, True, 512)
            turned("n2", "g_ffn2", IN_NET)
            ahead(BASE["w_out"] + 4 + RING)

            def per_layer():
                dve.wait_ge(*W("pTh_ready", 1))
                dve.tensor_tensor(pTl[:, :, :], praw[:, :, :], f32(pTh[:, :, :]), ALU.subtract)\
                   .then_inc(S("pT_split"), 1)

            dve.wait_ge(*W("rstd_n2", NT))
            ffn(2, per_layer)
            ahead(BASE["ple_proj"] + 2)
            dve.wait_ge(*W("post_loaded", 48))
            post_norm("p2", "n3", acc, True)
            turned("n3", "g_ple", (4, 6, 5, 7), (0,))
            ahead(BASE["ple_proj"] + 3)
            turned("n3", "g_ple", (4, 6, 5, 7), (1,))
            ahead(BASE["ple_gate"] + 2 + RING)
            through("ple_proj", 1)
            for j in range(2):
                for t in range(NT):
                    dve.wait_ge(*W("pg_out", 2 * j + t + 1))
                    c = slice(j * 512, (j + 1) * 512)
                    dve.tensor_tensor(pgate[:, t, c], pgate[:, t, c], ps[:, 2 * t + j, :], ALU.mult)\
                       .then_inc(S("pm_out"), 1)
                    dve.wait_ge(*W("post_loaded", 64))
                    dve.wait_ge(*W("ss_n3", NT))
                    dve.wait_ge(*W("pm_out", 2 * j + t + 1))
                    link(dve.tensor_tensor(hn_s[:, t, c], pgate[:, t, c], post[:, c], ALU.mult))
                if j == 0:
                    ahead(BASE["ple_gate"] + 3 + RING)
            scr[0] = hn_s
            post_norm("p3", "n4", None, False, D)
            normed("n4", hn_s)
            turned("n4", "g_mix2", (0, 1, 2, 3))
            ahead(BASE["ple_gate"] + 4 + RING)

            w3 = M("sconv_w")
            for n in range(4):
                ahead(BASE["s_c"] + n + 1 + RING)
            def short_conv(n):
                for f in (2 * n, 2 * n + 1):
                    dve.wait_ge(*W("cv_first", f + 1))
                    for s in (1, 2):
                        link(dve.scalar_tensor_tensor(cv[:, f, s:T], cx[:, f, 0:T - s],
                                                      w3[:, 3 * f + 2 - s:3 * f + 3 - s], cv[:, f, s:T],
                                                      ALU.mult, ALU.add))

            for n in range(4):
                f = slice(2 * n, 2 * n + 2)
                through("s_x", n + 1)
                dve.wait_ge(*W("s_c_out", n + 1))
                dve.tensor_tensor(cx[:, f, :], cx[:, f, :], ps[:, 4 + n, :].rearrange("p (a b) -> p a b", a=2),
                                  ALU.mult).then_inc(S("s_x_out"), 1)
                if n:
                    short_conv(n - 1)
                ahead(BASE["s_x"] + n + 1 + RING)
            short_conv(3)
            for n in range(4):
                f = slice(2 * n, 2 * n + 2)
                through("s_b", n + 1)
                dve.tensor_tensor(cx[:, f, :], cv[:, f, :], ps[:, 4 + n, :].rearrange("p (a b) -> p a b", a=2),
                                  ALU.mult).then_inc(S("s_b_out"), 1)
                dve.wait_ge(*W("svh_ready", n + 1))
                dve.tensor_tensor(svl[:, f, :], cx[:, f, :], f32(svh[:, f, :]), ALU.subtract)\
                   .then_inc(S("sv_ready"), 2)
                ahead(BASE["s_b"] + n + 1 + RING)
            ahead(BASE["g_b"] + 2 + RING)
            dve.wait_ge(*W("dt_turned", 1))
            x, dt_, dtA, e, z, z2, p_ = (dts[:, i, :, :] for i in (2, 0, 1, 3, 4, 5, 6))
            bb = M("dt_bias").rearrange("p (a b) -> p a b", a=1).to_broadcast([P, NT, SSD_HEADS])
            dve.tensor_tensor(x, ps[:, 5, 0:NT * SSD_HEADS].rearrange("p (a b) -> p a b", a=NT), bb, ALU.add)\
               .then_inc(S("dt_out"), 1)
            dve.wait_ge(*W("dt_out", 1))
            dve.scalar_tensor_tensor(e, x, -1.0, x, ALU.mult, ALU.max).then_inc(S("sp_abs"), 1)
            dve.wait_ge(*W("sp_exp", 1))
            link(dve.tensor_scalar(z, e, 2.0, None, ALU.add))
            link(dve.reciprocal(z, z))
            link(dve.tensor_tensor(z, z, e, ALU.mult))
            link(dve.tensor_tensor(z2, z, z, ALU.mult))
            link(dve.tensor_scalar(p_, z2, 1.0 / 15, None, ALU.mult))
            for d in (13, 11, 9, 7, 5, 3):
                link(dve.scalar_tensor_tensor(p_, p_, 1.0 / d, z2, ALU.add, ALU.mult))
            link(dve.scalar_tensor_tensor(p_, p_, 1.0, z, ALU.add, ALU.mult))
            link(dve.tensor_scalar(x, x, 0.0, None, ALU.max))
            link(dve.scalar_tensor_tensor(dt_, p_, 2.0, x, ALU.mult, ALU.add))
            dve.wait_ge(*W("alog_exp", 1))
            al = M("a_log").rearrange("p (a b) -> p a b", a=1).to_broadcast([P, NT, SSD_HEADS])
            dve.scalar_tensor_tensor(dtA, dt_, -1.0, al, ALU.mult, ALU.mult).then_inc(S("dtA_ready"), 1)
            ahead(BASE["g_b"] + 4 + RING)
            for j in range(2):
                for t in range(NT):
                    c = slice(j * 512, (j + 1) * 512)
                    dve.wait_ge(*W("gb_out", 2 * j + t + 1))
                    through("sconv_proj", 2 * (j + 1))
                    if j == 0 and t == 0:
                        dve.wait_ge(*W("nT_n4", 4))
                    dve.tensor_tensor(merged[:, t, c], ps[:, 4 + 2 * t + j, :], sga[:, t, c], ALU.mult)\
                       .then_inc(S("mgb_out"), 1)
                ahead(BASE["sconv_proj"] + 2 * j + 2 + RING)
            cw = M("conv_w")

            def times_dt(n):
                q, t = n // 2, n % 2
                dve.wait_ge(*W("xT_done", n + 1))
                d = dts[:, 0, t, 8 * q:8 * q + 8].rearrange("p (a b) -> p a b", b=1).to_broadcast([P, 8, SSD_HD])
                dve.tensor_tensor(xdt[:, t, 8 * q:8 * q + 8, :],
                                  ps[:, 2 + n % 2, :].rearrange("p (a b) -> p a b", a=8), d, ALU.mult)\
                   .then_inc(S("xdt_out"), 1)

            for n in range(12):
                for r in range(2):
                    f = 2 * n + r
                    if r == 0:
                        dve.wait_ge(*W("cvt_first", f + 2))
                    v = cvt[:, n % 2, r, :]
                    for s in (1, 2, 3):
                        ins = dve.scalar_tensor_tensor(v[:, s:T], ps[:, 4 + n % 4, r * T:(r + 1) * T - s],
                                                       cw[:, 4 * f + 3 - s:4 * f + 4 - s], v[:, s:T],
                                                       ALU.mult, ALU.add)
                        if s < 3:
                            link(ins)
                        else:
                            ins.then_inc(S("conv_out"), 1)
                if n == 4:
                    dve.wait_ge(*W("acTh_ready", 1))
                    dve.tensor_tensor(acTl[:, :], ps[0:SSD_HEADS, 1, P:P + T], f32(acTh[:, :]), ALU.subtract)\
                       .then_inc(S("acT_split"), 1)
                    ac = dts[:, 7, :, :]
                    link(dve.tensor_copy(ac, ps[:, 1, 0:64].rearrange("p (a b) -> p a b", a=NT)))
                    dve.tensor_tensor(dts[:, 8, 0, :], ps[:, 1, 64:96], ac[:, 0, :], ALU.subtract)\
                       .then_inc(S("kd_sub"), 1)
                if n >= 5:
                    times_dt(n - 5)
                if n == 11:
                    times_dt(7)
                else:
                    ahead(BASE["xbc"] + n + 1 + RING)
            tri = C("tri")

            def keys_out(g):
                dve.wait_ge(*W("cb_done", g + 1))
                b = 3 if g else 6
                dve.tensor_tensor(cbm[:, g, 0, :], ps[:, b, 0:P], tri, ALU.mult).then_inc(S("cb_out"), 1)
                dve.tensor_copy(cbm[:, g, 1, :], ps[:, b, P:2 * P]).then_inc(S("cb_out"), 1)
                dve.tensor_tensor(cbm[:, g, 2, :], ps[:, b, 2 * P:3 * P], tri, ALU.mult).then_inc(S("cb_out"), 1)

            ds = M("d_skip")

            def gated(n):
                dve.wait_ge(*W("zs_ready", n + 1))
                dve.wait_ge(*W("y_out", 2 * n + 2))
                v = xs[:, 2 * n:2 * n + 2, :]
                dve.tensor_tensor(v, v, zs[:, :, :], ALU.mult).then_inc(S("z_out"), 1)

            for q in range(8):
                dve.wait_ge(*W("bc_done", q + 1))
                if q:
                    dve.wait_ge(*W("y_done", q))
                dve.wait_ge(*W("cross_exp", 2 * (q + 1)))
                for r in range(4):
                    for t in range(NT):
                        c = ((r % 2) * NT + t) * P
                        hd = 4 * q + r
                        dve.tensor_scalar(seg[:, r, 2 * t, :], ps[:, 4 + r // 2, c:c + P], ac[:, t, hd:hd + 1], 0.0,
                                          ALU.subtract, ALU.min).then_inc(S("seg_sub"), 1)
                if q:
                    y_out(dve, S, xs, ps, ds, q - 1)
                    gated(q - 1)
                    if q == 7:
                        dve.wait_ge(*W("ssg_done", GROUPS - 1))
                        dve.tensor_copy(st[:, 24:30], ps[:, 3, 0:6]).then_inc(S("ss_ssd"), 1)
                else:
                    dve.wait_ge(*W("xdt_out", 8))
                    dve.wait_ge(*W("kd_exp", 1))
                    d = dts[:, 8, 0, :].rearrange("p (a b) -> p a b", b=1).to_broadcast([P, SSD_HEADS, SSD_HD])
                    dve.tensor_tensor(xw[:, :, :], xdt[:, 0, :, :], d, ALU.mult).then_inc(S("xw_ready"), 1)
                    keys_out(0)
                dve.wait_ge(*W("cb_out", 3 * (q // 2 + 1)))
                dve.wait_ge(*W("seg_exp", 2 * (q + 1)))
                m = cbm[:, q // 2:q // 2 + 1, :, :].rearrange("p a b c -> p a (b c)").to_broadcast([P, 4, 3 * P])
                sv = seg[:, :, :, :].rearrange("p a b c -> p a (b c)")
                dve.tensor_tensor(sv, sv, m, ALU.mult).then_inc(S("sc_ready"), 1)
                if q + 1 < GROUPS:
                    keys_out(q + 1)
                ahead(Z_UNITS[q] + RING)
                if q == 0:
                    ahead(Z_UNITS[0] + 1 + RING)
                    ahead(BASE["g_a0"] + 1 + RING)
            nw = M("ssd_norm")

            def low_halves(g):
                for f in range(GT * g, GT * g + GT):
                    dve.wait_ge(*W("yhi_ssd", f + 1))
                    dve.scalar_tensor_tensor(ylo[:, f, :], xs[:, f, :], nw[:, f:f + 1], f32(yhi[:, f, :]),
                                             ALU.mult, ALU.subtract).then_inc(S("ylo_ssd"), 1)

            def group_normed(g, done):
                dve.wait_ge(*W("rb_done", done))
                b = (4, 5, 0, 3)[g]
                v = xs[:, GT * g:GT * g + GT, :]
                r = ps[:, b:b + 1, 0:T].to_broadcast([P, GT, T])
                dve.tensor_tensor(v, v, r, ALU.mult).then_inc(S("yn_out"), 1)

            ahead(Z_UNITS[7] + 1 + RING)
            group_normed(0, 1)
            dve.wait_ge(*W("y_done", 8))
            y_out(dve, S, xs, ps, ds, 7)
            gated(7)
            group_normed(1, 1)
            low_halves(0)
            ahead(BASE["g_a1"] + 1 + RING)
            dve.wait_ge(*W("ssg_done", GROUPS))
            dve.tensor_copy(st[:, 30:32], ps[:, 3, 6:8]).then_inc(S("ss_ssd"), 1)
            group_normed(2, 1)
            low_halves(1)
            group_normed(3, 2)
            low_halves(2)
            low_halves(3)
            ahead(BASE["g_a1"] + 2 + RING)
            ahead(BASE["ssd_proj"] + 4 + RING)
            for j in range(2):
                if j:
                    ahead(BASE["ssd_proj"] + 7 + RING)
                    turned("m2", None, (0, 1, 2, 3), (0,))
                for t in range(NT):
                    c = slice(j * 512, (j + 1) * 512)
                    n = 2 * (2 * j + t)
                    dve.wait_ge(*W("ga_out", 4))
                    through("ssd_proj", 4 * (j + 1))
                    dve.tensor_tensor(sga[:, t, c], ps[:, 4 + 2 * t + j, :], sga[:, t, c], ALU.mult)\
                       .then_inc(S("mga_out"), 1)
                    dve.wait_ge(*W("mga_out", n + 1))
                    dve.tensor_tensor(merged[:, t, c], merged[:, t, c], sga[:, t, c], ALU.add)\
                       .then_inc(S("mga_out"), 1)
            ahead(BASE["ssd_proj"] + 8 + RING)
            turned("m2", None, (0, 1, 2, 3), (1,))
            ahead(BASE["w_o"] + 2 + RING)
            for j in range(2):
                through("w_o", 2 * (j + 1))
                for t in range(NT):
                    c = slice(j * 512, (j + 1) * 512)
                    dve.tensor_tensor(h[:, t, c], h[:, t, c], ps[:, 4 + 2 * t + j, :], ALU.add)\
                       .then_inc(S("h_n5"), 1)
                if j == 0:
                    ahead(BASE["w_o"] + 3 + RING)
                turned("n5", "g_ffn3", IN_NET, (j,))
            ahead(BASE["w_o"] + 4 + RING)
            dve.wait_ge(*W("rstd_n5", NT))
            ffn(3)
            for t in range(NT):
                if t == 0:
                    dve.wait_ge(*W("t0_ffn3", 1))
                else:
                    through("ffn3", FFN_UNITS)
                dve.tensor_tensor(h[:, t, :], h[:, t, :], acc(t), ALU.add).then_inc(S("h_n6"), 1)
            dve.wait_ge(*W("post_loaded", 80))
            for t in range(NT):
                dve.wait_ge(*W("rstd_n6", t + 1))
                dve.scalar_tensor_tensor(hn_f[:, t, :], h[:, t, :], st[:, t:t + 1], post[:, :], ALU.mult, ALU.mult)\
                   .then_inc(S("final_ready"), 1)


def score_init(dve, S, score, C):
    for n in (0, 2):
        dve.tensor_copy(score[:, n, :], C("causal")).then_inc(S("score_init"), 1)
    dve.memset(score[:, 1, :], 0.0).then_inc(S("score_init"), 1)


def y_out(dve, S, xs, ps, ds, q):
    for r in range(2):
        f = 2 * q + r
        dve.scalar_tensor_tensor(xs[:, f, :], xs[:, f, :], ds[:, f:f + 1], ps[:, 6 + q % 2, r * T:(r + 1) * T],
                                 ALU.mult, ALU.add).then_inc(S("y_out"), 1)


def by_rows(w, n):
    k = w.shape[0] // 512
    a = w.reshape(k, 4, P, n, 512).transpose(3, 0, 2, 1, 4)
    return a.reshape(n * k, P, UNIT)


def by_features(w):
    n = w.shape[1] // 256
    return w.reshape(KD, P, n, 256).transpose(2, 1, 0, 3).reshape(n, P, UNIT)


def feed_forward(gate, up, down):
    g = gate.reshape(2, 4, P, NCH, FCH).transpose(3, 0, 2, 1, 4)
    u = up.reshape(2, 4, P, NCH, FCH).transpose(3, 0, 2, 1, 4)
    gu = np.concatenate([g, u], axis=-1).reshape(NCH, 2, P, UNIT)
    dn = down.reshape(NCH, 2, P, D).transpose(0, 2, 1, 3).reshape(NCH, P, UNIT)
    out = [gu[0, 0], gu[0, 1]]
    for c in range(1, NCH):
        out += [gu[c, 0], gu[c, 1], dn[c - 1]]
    return np.stack(out + [dn[NCH - 1]])


def padded(w, cols):
    a = w.reshape(KD, P, w.shape[1]).transpose(1, 0, 2)
    a = np.concatenate([a, np.zeros((P, KD, cols - a.shape[2]), np.float32)], axis=2).reshape(P, KD * cols)
    return np.concatenate([a, np.zeros((P, UNIT - KD * cols), np.float32)], axis=1)[None]


def weight_stream(i):
    w, w2 = i["w_in"][0], i["w_in_2"][0]
    cuts = np.cumsum([0, 512, 128, 512, 64, 8, 512, 512, 512, 512, 1024, 1024])
    c = dict(zip(("q_a", "kv", "q_idx", "ki", "wi", "q_h", "f_h", "i_h", "g_h", "gate_a", "gate_b"),
                 (w[:, a:b] for a, b in zip(cuts[:-1], cuts[1:]))))
    cuts = np.cumsum([0, 2048, 3072, 32, 1024, 1024, 1024, 1024, 1024])
    d = dict(zip(("z", "xbc", "dt", "s_b", "s_c", "s_x", "g_a", "g_b"),
                 (w2[:, a:b] for a, b in zip(cuts[:-1], cuts[1:]))))
    pp = i["w_ple_proj"][0].reshape(2, P, D).transpose(1, 0, 2).reshape(1, P, UNIT)
    parts = {
        "ffn1": feed_forward(i["ffn1_w_gate"][0], i["ffn1_w_up"][0], i["ffn1_w_down"][0]),
        "kv": padded(np.concatenate([c["kv"], c["ki"], c["wi"]], axis=1), 256),
        "q_idx": by_features(c["q_idx"]), "q_a": by_features(c["q_a"]),
        "f_h": by_features(c["f_h"]), "q_h": by_features(c["q_h"]),
        "i_h": by_rows(c["i_h"], 1), "g_h": by_rows(c["g_h"], 1),
        "gate_b": by_rows(c["gate_b"], 2), "br_b": by_rows(i["w_br_b"][0], 2),
        "gate_a": by_rows(c["gate_a"], 2), "br_a": by_rows(i["w_br_a"][0], 2),
        "w_out": by_rows(i["w_out"][0], 2),
        "ffn2": feed_forward(i["ffn2_w_gate"][0], i["ffn2_w_up"][0], i["ffn2_w_down"][0]),
        "ple_gate": by_rows(i["w_ple_gate"][0], 2), "ple_proj": pp,
        "s_c": by_features(d["s_c"]), "s_x": by_features(d["s_x"]), "s_b": by_features(d["s_b"]),
        "sconv_proj": by_rows(i["w_sconv_proj_2"][0], 2), "g_b": by_rows(d["g_b"], 2),
        "xbc": by_features(d["xbc"]), "dt": padded(d["dt"], 32), "z_first": by_features(d["z"])[0:1],
        "z": by_features(d["z"])[1:8], "g_a0": by_rows(d["g_a"], 2)[0:2], "g_a1": by_rows(d["g_a"], 2)[2:4], "ssd_proj": by_rows(i["w_ssd_proj_2"][0], 2),
        "w_o": by_rows(i["w_o_2"][0], 2),
        "ffn3": feed_forward(i["w_gate_2"][0], i["w_up_2"][0], i["w_down_2"][0]),
    }
    for name, n in PARTS:
        assert parts[name].shape[0] == n, name
    return np.concatenate([parts[name] for name, _ in PARTS])


def small_parameters(i):
    def tiles(v):
        return v.reshape(-1, P).T

    def all_rows(v):
        return np.broadcast_to(v.reshape(1, -1), (P, v.size))

    conv = i["ssd_conv_w_2"][0].T.reshape(24, P, CONV_K).transpose(1, 0, 2).reshape(P, -1)
    sconv = i["sconv_w_2"][0].T.reshape(KD, P, SCONV_K).transpose(1, 0, 2).reshape(P, -1)
    uk = i["w_uk"][0].transpose(0, 2, 1).reshape(PAIRS, 2 * HEAD_DIM, LATENT).transpose(1, 0, 2).reshape(P, -1)
    uv = i["w_uv"][0].transpose(1, 0, 2).reshape(P, -1)
    rel = np.concatenate([i["rel_bias"], np.zeros((P - BUCKETS, HEADS), np.float32)])
    parts = {
        "g_ffn1": tiles(i["ffn1_pre_g"][0]), "g_mix": tiles(i["mix_pre_g"][0]), "g_ffn2": tiles(i["ffn2_pre_g"][0]),
        "g_ple": tiles(i["ple_pre_g"][0]), "g_mix2": tiles(i["norm_mix_w_2"][0]), "g_ffn3": tiles(i["norm_ffn_w_2"][0]),
        "ssd_norm": tiles(i["ssd_norm_w_2"][0]), "conv_w": conv, "conv_b": tiles(i["ssd_conv_b_2"][0]),
        "sconv_w": sconv, "d_skip": tiles(np.repeat(i["d_skip_2"][0], SSD_HD)),
        "hg_lb": i["hgrn_lb"].reshape(2, HG, P).transpose(2, 0, 1).reshape(P, 2 * HG),
        "hg_norm": i["hgrn_norm_g"][0].reshape(P, 1), "dt_bias": all_rows(i["dt_bias_2"][0]),
        "a_log": all_rows(i["a_log_2"][0]), "kv_g": all_rows(i["kv_norm_g"][0]), "ki_g": all_rows(i["kidx_norm_g"][0]),
        "w_uk": uk, "w_uv": uv, "rel": rel,
    }
    return np.ascontiguousarray(np.concatenate([parts[name] for name, _ in SMALL], axis=1), dtype=np.float32)


def shape_constants():
    s, t = np.arange(P)[:, None], np.arange(P)[None, :]
    levels = [s == t]
    for b in LEVELS:
        levels.append((s // (2 * b) == t // (2 * b)) & ((s // b) % 2 == 0) & ((t // b) % 2 == 1))
    dist = np.maximum(T - 1 - np.arange(NREL), 0)
    exact = BUCKETS // 2
    log_b = exact + (np.log(np.maximum(dist, 1).astype(np.float32) / exact) / math.log(MAX_DIST / exact)
                     * (BUCKETS - exact)).astype(np.int32)
    bucket = np.where(dist < exact, dist, np.minimum(log_b, BUCKETS - 1))
    parts = {
        "ident": s == t, "tri": s <= t, "ones": np.ones((P, P)),
        "causal": np.where(t <= s, 0.0, -1.0e38),
        "reset": np.broadcast_to((np.arange(T) % CHUNK != 0)[None, :], (P, T)),
        "flip": s + t == P - 1,
        "levels": np.concatenate(levels, axis=1),
        "onehot": np.arange(P)[:, None] == bucket[None, :],
    }
    return np.ascontiguousarray(np.concatenate([parts[name] for name, _ in CONSTS], axis=1), dtype=np.float32)


def kernel(**inputs):
    import concourse.bacc as bacc
    from concourse.bass_utils import run_bass_kernel_spmd

    i = {k: np.asarray(v) for k, v in inputs.items()}
    posts = np.stack([i["ffn1_post_g"][0], i["mix_post_g"][0], i["ffn2_post_g"][0], i["ple_post_g"][0],
                      i["final_norm_w_2"]])
    arrays = {
        "stream": weight_stream(i), "small": small_parameters(i), "consts": shape_constants(),
        "bgate": np.ascontiguousarray(i["b_gate"][0].reshape(4, 512)), "posts": posts,
        "x": np.ascontiguousarray(i["x"][0]), "p_turned": np.ascontiguousarray(i["p"][0, 0].T),
    }
    nc = bacc.Bacc("TRN2", target_bir_lowering=False, num_devices=1)
    aps = [nc.dram_tensor(n, a.shape, F32, kind="ExternalInput").ap() for n, a in arrays.items()]
    out = nc.dram_tensor("out", (T, D), F32, kind="ExternalOutput").ap()
    build(nc, *aps, out)
    r = run_bass_kernel_spmd(nc, [arrays], core_ids=[0])
    return r.results[0]["out"].reshape(1, T, D)
```
